# Optimizing a Trainium2 kernel written in Bass

```python
import math
import jax, jax.numpy as jnp
from jax import lax
import numpy as np

D_MODEL = 1024
BATCH = 1
SEQ = 256
DEPTH = 2

N_A_LAYERS = DEPTH // 2
N_B_LAYERS = DEPTH - N_A_LAYERS
QB = 128
DA_HEAD_DIM = 64
DA_HEADS = D_MODEL // (2 * DA_HEAD_DIM)
DA_QK = DA_HEADS * 2 * DA_HEAD_DIM
DA_V = DA_HEADS * 2 * DA_HEAD_DIM
DA_IN = 2 * DA_QK + DA_V + DA_V
LAMBDA_INIT = tuple(0.8 - 0.6 * math.exp(-0.3 * l) for l in range(N_A_LAYERS))
SB_HEAD_DIM = 64
SB_HEADS = D_MODEL // SB_HEAD_DIM
SB_W = SB_HEADS * SB_HEAD_DIM
SB_IN = SB_W + SB_W
ROPE_THETA = 500000.0
ROT_DIM = DA_HEAD_DIM // 4
RMS_EPS = 1e-6


def _rms(x, g):
    xf = x.astype(jnp.float32)
    y = xf * lax.rsqrt(jnp.mean(xf * xf, axis=-1, keepdims=True) + RMS_EPS)
    return (y * g.astype(jnp.float32)).astype(x.dtype)

def _rope_partial(t, pos):
    half = ROT_DIM // 2
    inv = jnp.power(jnp.float32(ROPE_THETA), -jnp.arange(half, dtype=jnp.float32) / half)
    ang = pos.astype(jnp.float32)[:, None] * inv[None, :]
    cos = jnp.cos(ang)[None, :, None, :]
    sin = jnp.sin(ang)[None, :, None, :]
    t1 = t[..., :half].astype(jnp.float32)
    t2 = t[..., half:ROT_DIM].astype(jnp.float32)
    rot = jnp.concatenate([t1 * cos - t2 * sin, t1 * sin + t2 * cos], axis=-1)
    return jnp.concatenate([rot.astype(t.dtype), t[..., ROT_DIM:]], axis=-1)

def _to_blocks(t):
    b, s, h, d = t.shape
    return t.reshape(b, s // QB, QB, h, d).transpose(1, 0, 3, 2, 4)

def _from_blocks(o):
    nb, b, h, qb, e = o.shape
    return o.transpose(1, 0, 3, 2, 4).reshape(b, nb * qb, h, e)

def _diff_attention(q1, q2, k1, k2, v, lam):
    s_len = q1.shape[1]
    kpos = jnp.arange(s_len)
    scale = DA_HEAD_DIM ** -0.5

    def block(args):
        i, qb1, qb2 = args
        qpos = i * QB + jnp.arange(QB)
        mask = kpos[None, :] <= qpos[:, None]

        def probs(qb, k):
            s = jnp.einsum('bhqd,bshd->bhqs', qb, k).astype(jnp.float32) * scale
            return jax.nn.softmax(jnp.where(mask, s, -jnp.inf), axis=-1)

        a = probs(qb1, k1) - lam * probs(qb2, k2)
        return jnp.einsum('bhqs,bshe->bhqe', a.astype(v.dtype), v)

    nb = s_len // QB
    o = lax.map(block, (jnp.arange(nb), _to_blocks(q1), _to_blocks(q2)))
    return _from_blocks(o)

def _stick_breaking(q, k, v):
    s_len = q.shape[1]
    kpos = jnp.arange(s_len)
    scale = SB_HEAD_DIM ** -0.5

    def block(args):
        i, qb = args
        qpos = i * QB + jnp.arange(QB)
        mask = kpos[None, :] < qpos[:, None]
        z = jnp.einsum('bhqd,bshd->bhqs', qb, k).astype(jnp.float32) * scale
        log_beta = jax.nn.log_sigmoid(z)
        log_1mb = jnp.where(mask, jax.nn.log_sigmoid(-z), 0.0)
        suffix = lax.cumsum(log_1mb, axis=3, reverse=True) - log_1mb
        a = jnp.where(mask, jnp.exp(log_beta + suffix), 0.0)
        return jnp.einsum('bhqs,bshe->bhqe', a.astype(v.dtype), v)

    nb = s_len // QB
    o = lax.map(block, (jnp.arange(nb), _to_blocks(q)))
    return _from_blocks(o)

def _diff_layer(x, pos, norm_g, w_in, w_out, q_norm, k_norm, lq1, lk1, lq2, lk2,
                subln, lambda_init):
    b, s, _ = x.shape
    h = _rms(x, norm_g)
    proj = h @ w_in
    q, k, v, g = jnp.split(proj, [DA_QK, 2 * DA_QK, 2 * DA_QK + DA_V], axis=-1)
    q = q.reshape(b, s, DA_HEADS, 2, DA_HEAD_DIM)
    k = k.reshape(b, s, DA_HEADS, 2, DA_HEAD_DIM)
    v = v.reshape(b, s, DA_HEADS, 2 * DA_HEAD_DIM)
    qs = [_rope_partial(_rms(q[:, :, :, c], q_norm), pos) for c in range(2)]
    ks = [_rope_partial(_rms(k[:, :, :, c], k_norm), pos) for c in range(2)]
    lam = (jnp.exp(jnp.sum(lq1.astype(jnp.float32) * lk1.astype(jnp.float32)))
           - jnp.exp(jnp.sum(lq2.astype(jnp.float32) * lk2.astype(jnp.float32)))
           + lambda_init)
    o = _diff_attention(qs[0], qs[1], ks[0], ks[1], v, lam)
    o = _rms(o, subln) * (1.0 - lambda_init)
    o = o.reshape(b, s, DA_V) * jax.nn.silu(g)
    return x + o @ w_out

def _shared_kv(x, kv_norm, w_kv):
    b, s, _ = x.shape
    kv = _rms(x, kv_norm) @ w_kv
    k, v = jnp.split(kv, [SB_W], axis=-1)
    return (k.reshape(b, s, SB_HEADS, SB_HEAD_DIM), v.reshape(b, s, SB_HEADS, SB_HEAD_DIM))

def _sb_layer(x, k, v, norm_g, w_in, w_out):
    b, s, _ = x.shape
    proj = _rms(x, norm_g) @ w_in
    q, g = jnp.split(proj, [SB_W], axis=-1)
    o = _stick_breaking(q.reshape(b, s, SB_HEADS, SB_HEAD_DIM), k, v)
    o = o.reshape(b, s, SB_W) * jax.nn.silu(g)
    return x + o @ w_out

def first_inputs(seed: int = 0) -> dict:
    key = jax.random.key(seed)
    ks = jax.random.split(key, 20)
    f32 = jnp.float32
    nrm = lambda k, shape, scale: jax.random.normal(k, shape, f32) * scale
    gain = lambda k, shape: 1.0 + 0.02 * jax.random.normal(k, shape, f32)
    return {
        "x": jax.random.normal(ks[0], (BATCH, SEQ, D_MODEL), f32),
        "a_norm": gain(ks[1], (N_A_LAYERS, D_MODEL)),
        "a_w_in": nrm(ks[2], (N_A_LAYERS, D_MODEL, DA_IN), D_MODEL ** -0.5),
        "a_w_out": nrm(ks[3], (N_A_LAYERS, DA_V, D_MODEL), DA_V ** -0.5),
        "a_q_norm": gain(ks[4], (N_A_LAYERS, DA_HEAD_DIM)),
        "a_k_norm": gain(ks[5], (N_A_LAYERS, DA_HEAD_DIM)),
        "a_lq1": nrm(ks[6], (N_A_LAYERS, DA_HEAD_DIM), 0.1),
        "a_lk1": nrm(ks[7], (N_A_LAYERS, DA_HEAD_DIM), 0.1),
        "a_lq2": nrm(ks[8], (N_A_LAYERS, DA_HEAD_DIM), 0.1),
        "a_lk2": nrm(ks[9], (N_A_LAYERS, DA_HEAD_DIM), 0.1),
        "a_subln": gain(ks[10], (N_A_LAYERS, 2 * DA_HEAD_DIM)),
        "kv_norm": gain(ks[11], (D_MODEL,)),
        "w_kv": nrm(ks[12], (D_MODEL, 2 * SB_W), D_MODEL ** -0.5),
        "b_norm": gain(ks[13], (N_B_LAYERS, D_MODEL)),
        "b_w_in": nrm(ks[14], (N_B_LAYERS, D_MODEL, SB_IN), D_MODEL ** -0.5),
        "b_w_out": nrm(ks[15], (N_B_LAYERS, SB_W, D_MODEL), SB_W ** -0.5),
    }

def first_block(x, a_norm, a_w_in, a_w_out, a_q_norm, a_k_norm, a_lq1, a_lk1, a_lq2,
              a_lk2, a_subln, kv_norm, w_kv, b_norm, b_w_in, b_w_out):
    pos = jnp.arange(x.shape[1])
    shared_k = None
    shared_v = None
    for layer in range(DEPTH):
        if layer < N_A_LAYERS:
            x = _diff_layer(x, pos, a_norm[layer], a_w_in[layer], a_w_out[layer],
                            a_q_norm[layer], a_k_norm[layer], a_lq1[layer], a_lk1[layer],
                            a_lq2[layer], a_lk2[layer], a_subln[layer], LAMBDA_INIT[layer])
        else:
            if layer == N_A_LAYERS:
                shared_k, shared_v = _shared_kv(x, kv_norm, w_kv)
            j = layer - N_A_LAYERS
            x = _sb_layer(x, shared_k, shared_v, b_norm[j], b_w_in[j], b_w_out[j])
    return x


N_AB_LAYERS = (DEPTH + 1) // 2
N_C_LAYERS = DEPTH // 2

M_HEADS = 4
M_QK_DIM = 64
M_V_DIM = 128
M_CHUNK = 64
GATE_SOFTCAP = 15.0
G_HEADS = 4
G_K_DIM = 128
G_V_DIM = 128
G_CHUNK = 64
SHORT_CONV = 4
C_HEADS = 8
C_K_DIM = D_MODEL // C_HEADS
C_V_DIM = D_MODEL // C_HEADS
C_CHUNK = 32
D_FF = 2816
FFN_CONV = 3
EPS = 1e-6

M_QK = M_HEADS * M_QK_DIM
M_V = M_HEADS * M_V_DIM
G_QK = G_HEADS * G_K_DIM
G_V = G_HEADS * G_V_DIM
AB_SPLITS = (M_QK, M_QK, M_V, M_V, M_HEADS, M_HEADS, G_QK, G_QK, G_V, G_V, G_HEADS, G_HEADS)
AB_SPLIT_IDX = tuple(int(s) for s in np.cumsum(AB_SPLITS)[:-1])
AB_IN = sum(AB_SPLITS)
AB_MIX = M_V + G_V
C_K_TOTAL = C_HEADS * C_K_DIM
C_MIX = C_HEADS * C_V_DIM
C_IN = 2 * C_K_TOTAL + 2 * C_MIX


def rms_norm(x, gain):
    xf = x.astype(jnp.float32)
    y = xf * lax.rsqrt(jnp.mean(jnp.square(xf), -1, keepdims=True) + EPS)
    return (y * gain.astype(jnp.float32)).astype(x.dtype)

def head_rms_norm(x, gain):
    B, S, H, d = x.shape
    y = x * lax.rsqrt(jnp.mean(jnp.square(x), -1, keepdims=True) + EPS)
    return y.reshape(B, S, H * d) * gain.astype(jnp.float32)

def l2_norm(x):
    return x * lax.rsqrt(jnp.sum(jnp.square(x), -1, keepdims=True) + EPS)

def softcap(x, cap):
    return cap * jnp.tanh(x / cap)

def causal_dwconv(x, w):
    K, C = w.shape
    return lax.conv_general_dilated(
        x, w[:, None, :].astype(x.dtype), window_strides=(1,), padding=[(K - 1, 0)],
        dimension_numbers=("NWC", "WIO", "NWC"), feature_group_count=C)

def to_heads(t, n_heads):
    B, S, C = t.shape
    return t.reshape(B, S, n_heads, C // n_heads)

def to_chunks(t, L):
    B, S, H = t.shape[:3]
    t = t.reshape((B, S // L, L, H) + t.shape[3:])
    return jnp.moveaxis(t, (1, 3), (0, 2))

def from_chunks(t):
    N, B, H, L = t.shape[:4]
    t = jnp.moveaxis(t, (0, 2), (1, 3))
    return t.reshape((B, N * L, H) + t.shape[4:])

def mlstm_chunkwise(q, k, v, i_pre, f_pre):
    B, S, H, DK = q.shape
    DV = v.shape[-1]
    L = M_CHUNK
    q = q * DK ** -0.5
    qc, kc, vc = to_chunks(q, L), to_chunks(k, L), to_chunks(v, L)
    lfc = to_chunks(jax.nn.log_sigmoid(f_pre), L)
    igc = to_chunks(i_pre, L)
    causal = jnp.tril(jnp.ones((L, L), bool))

    def step(carry, inp):
        C, n, m = carry
        q_, k_, v_, lf_, ig_ = inp
        b = jnp.cumsum(lf_, -1)
        log_d = jnp.where(causal, b[..., :, None] - b[..., None, :] + ig_[..., None, :], -jnp.inf)
        log_inter = b + m[..., None]
        m_t = jnp.maximum(jnp.max(log_d, -1), log_inter)
        d = jnp.exp(log_d - m_t[..., None])
        w_inter = jnp.exp(log_inter - m_t)
        s = jnp.einsum("bhld,bhsd->bhls", q_, k_) * d
        num = jnp.einsum("bhls,bhsv->bhlv", s, v_) + w_inter[..., None] * jnp.einsum("bhld,bhdv->bhlv", q_, C)
        den = jnp.sum(s, -1) + w_inter * jnp.einsum("bhld,bhd->bhl", q_, n)
        h = num / jnp.maximum(jnp.abs(den), jnp.exp(-m_t))[..., None]
        b_last = b[..., -1]
        log_w = b_last[..., None] - b + ig_
        m_new = jnp.maximum(b_last + m, jnp.max(log_w, -1))
        wk = jnp.exp(log_w - m_new[..., None])
        carry_decay = jnp.exp(b_last + m - m_new)
        C = carry_decay[..., None, None] * C + jnp.einsum("bhl,bhld,bhlv->bhdv", wk, k_, v_)
        n = carry_decay[..., None] * n + jnp.einsum("bhl,bhld->bhd", wk, k_)
        return (C, n, m_new), h

    init = (jnp.zeros((B, H, DK, DV), jnp.float32), jnp.zeros((B, H, DK), jnp.float32),
            jnp.zeros((B, H), jnp.float32))
    _, h = lax.scan(step, init, (qc, kc, vc, lfc, igc))
    return from_chunks(h)

def gated_delta_chunkwise(q, k, v, g, beta):
    B, S, H, DK = q.shape
    DV = v.shape[-1]
    L = G_CHUNK
    q = q * DK ** -0.5
    qc, kc, vc = to_chunks(q, L), to_chunks(k, L), to_chunks(v, L)
    bc = to_chunks(beta, L)
    G = jnp.cumsum(to_chunks(g, L), -1)
    incl = jnp.tril(jnp.ones((L, L), bool))
    strict = jnp.tril(jnp.ones((L, L), bool), -1)
    diff = G[..., :, None] - G[..., None, :]
    decay = jnp.where(incl, jnp.exp(jnp.where(incl, diff, 0.0)), 0.0)
    kk = jnp.einsum("nbhld,nbhsd->nbhls", kc, kc)
    a_mat = jnp.where(strict, bc[..., :, None] * kk * decay, 0.0) + jnp.eye(L, dtype=jnp.float32)
    rhs = jnp.concatenate([vc * bc[..., None], kc * (bc * jnp.exp(G))[..., None]], -1)
    sol = lax.linalg.triangular_solve(a_mat, rhs, left_side=True, lower=True, unit_diagonal=True)
    u, w = sol[..., :DV], sol[..., DV:]
    attn = jnp.einsum("nbhld,nbhsd->nbhls", qc, kc) * decay
    q_dec = qc * jnp.exp(G)[..., None]
    k_dec = kc * jnp.exp(G[..., -1:] - G)[..., None]
    g_last = jnp.exp(G[..., -1])

    def step(state, inp):
        u_, w_, attn_, qd_, kd_, gl_ = inp
        v_new = u_ - jnp.einsum("bhld,bhdv->bhlv", w_, state)
        o = jnp.einsum("bhld,bhdv->bhlv", qd_, state) + jnp.einsum("bhls,bhsv->bhlv", attn_, v_new)
        state = gl_[..., None, None] * state + jnp.einsum("bhld,bhlv->bhdv", kd_, v_new)
        return state, o

    _, o = lax.scan(step, jnp.zeros((B, H, DK, DV), jnp.float32), (u, w, attn, q_dec, k_dec, g_last))
    return from_chunks(o)

def hgrn2_chunkwise(q, k, v, log_f):
    B, S, H, DK = q.shape
    DV = v.shape[-1]
    L = C_CHUNK
    q = q * DK ** -0.5
    qc, kc, vc = to_chunks(q, L), to_chunks(k, L), to_chunks(v, L)
    G = jnp.cumsum(to_chunks(log_f, L), -2)
    q_dec = qc * jnp.exp(G)
    k_dec = kc * jnp.exp(G[..., -1:, :] - G)
    g_last = jnp.exp(G[..., -1, :])
    incl = jnp.tril(jnp.ones((L, L), bool))[:, :, None]

    def step(state, inp):
        q_, k_, v_, G_, qd_, kd_, gl_ = inp
        diff = G_[..., :, None, :] - G_[..., None, :, :]
        pair_decay = jnp.exp(jnp.where(incl, diff, -jnp.inf))
        attn = jnp.einsum("bhld,bhlsd,bhsd->bhls", q_, pair_decay, k_)
        o = jnp.einsum("bhld,bhdv->bhlv", qd_, state) + jnp.einsum("bhls,bhsv->bhlv", attn, v_)
        state = gl_[..., :, None] * state + jnp.einsum("bhld,bhlv->bhdv", kd_, v_)
        return state, o

    _, o = lax.scan(step, jnp.zeros((B, H, DK, DV), jnp.float32), (qc, kc, vc, G, q_dec, k_dec, g_last))
    return from_chunks(o)

def hgrn_lower_bounds(lb_logits):
    p = jax.nn.softmax(lb_logits.astype(jnp.float32), axis=0)
    return jnp.cumsum(p, axis=0) - p[0]

def ab_mixer(u, w_in, conv_m, m_gate_bias, m_norm, conv_g, g_a_log, g_dt_bias, g_norm, w_out):
    f32 = jnp.float32
    proj = u @ w_in
    m_q, m_k, m_v, m_o, m_i, m_f, g_q, g_k, g_v, g_gate, g_a, g_b = jnp.split(proj, AB_SPLIT_IDX, axis=-1)
    m_qk = jax.nn.silu(causal_dwconv(jnp.concatenate([m_q, m_k], -1), conv_m))
    m_q, m_k = jnp.split(m_qk, 2, axis=-1)
    gb = m_gate_bias.astype(f32)
    i_pre = softcap(m_i.astype(f32) + gb[0], GATE_SOFTCAP)
    f_pre = softcap(m_f.astype(f32) + gb[1], GATE_SOFTCAP)
    h_m = mlstm_chunkwise(to_heads(m_q, M_HEADS).astype(f32), to_heads(m_k, M_HEADS).astype(f32),
                          to_heads(m_v, M_HEADS).astype(f32), i_pre, f_pre)
    y_m = jax.nn.sigmoid(m_o.astype(f32)) * head_rms_norm(h_m, m_norm)
    g_qkv = jax.nn.silu(causal_dwconv(jnp.concatenate([g_q, g_k, g_v], -1), conv_g))
    g_q, g_k, g_v = jnp.split(g_qkv, 3, axis=-1)
    log_decay = -jnp.exp(g_a_log.astype(f32)) * jax.nn.softplus(g_a.astype(f32) + g_dt_bias.astype(f32))
    beta = jax.nn.sigmoid(g_b.astype(f32))
    h_g = gated_delta_chunkwise(l2_norm(to_heads(g_q, G_HEADS).astype(f32)),
                                l2_norm(to_heads(g_k, G_HEADS).astype(f32)),
                                to_heads(g_v, G_HEADS).astype(f32), log_decay, beta)
    y_g = head_rms_norm(h_g, g_norm) * jax.nn.silu(g_gate.astype(f32))
    y = jnp.concatenate([y_m, y_g], -1).astype(u.dtype)
    return y @ w_out

def hgrn2_mixer(u, w_in, lower_bound, norm_gain, w_out):
    f32 = jnp.float32
    q, f, i, gate = jnp.split(u @ w_in, [C_K_TOTAL, 2 * C_K_TOTAL, 2 * C_K_TOTAL + C_MIX], axis=-1)
    lb = lower_bound.astype(f32)
    ff = f.astype(f32)
    log_f = jnp.logaddexp(jnp.log(lb), jnp.log1p(-lb) + jax.nn.log_sigmoid(ff))
    k = (1.0 - lb) * jax.nn.sigmoid(-ff)
    o = hgrn2_chunkwise(to_heads(jax.nn.silu(q.astype(f32)), C_HEADS), to_heads(k, C_HEADS),
                        to_heads(i.astype(f32), C_HEADS), to_heads(log_f, C_HEADS))
    y = head_rms_norm(o, norm_gain) * jax.nn.silu(gate.astype(f32))
    return y.astype(u.dtype) @ w_out

def conv_ffn(u, w_up, conv_w, conv_b, w_down):
    hdn = causal_dwconv(u @ w_up, conv_w) + conv_b
    gate, val = jnp.split(hdn, 2, axis=-1)
    return (jax.nn.silu(gate) * val) @ w_down

def second_inputs(seed: int = 0) -> dict:
    key = jax.random.key(seed)
    ks = jax.random.split(key, 24)
    f32 = jnp.float32

    def nrm(k, shape, scale):
        return jax.random.normal(k, shape, f32) * scale

    dt = jnp.exp(jax.random.uniform(ks[9], (N_AB_LAYERS, G_HEADS), f32, np.log(1e-3), np.log(1e-1)))
    return {
        "x": nrm(ks[0], (BATCH, SEQ, D_MODEL), 1.0),
        "norm_gains": 1.0 + nrm(ks[1], (DEPTH, 4, D_MODEL), 0.05),
        "ab_w_in": nrm(ks[2], (N_AB_LAYERS, D_MODEL, AB_IN), D_MODEL ** -0.5),
        "ab_conv_m": nrm(ks[3], (N_AB_LAYERS, SHORT_CONV, 2 * M_QK), SHORT_CONV ** -0.5),
        "ab_m_gate_bias": jnp.stack([nrm(ks[4], (N_AB_LAYERS, M_HEADS), 0.1),
                                     jnp.linspace(3.0, 6.0, M_HEADS, dtype=f32) + nrm(ks[5], (N_AB_LAYERS, M_HEADS), 0.1)], axis=1),
        "ab_m_norm": 1.0 + nrm(ks[6], (N_AB_LAYERS, M_V), 0.05),
        "ab_conv_g": nrm(ks[7], (N_AB_LAYERS, SHORT_CONV, 2 * G_QK + G_V), SHORT_CONV ** -0.5),
        "ab_g_a_log": jnp.log(jax.random.uniform(ks[8], (N_AB_LAYERS, G_HEADS), f32, 1.0, 16.0)),
        "ab_g_dt_bias": dt + jnp.log(-jnp.expm1(-dt)),
        "ab_g_norm": 1.0 + nrm(ks[10], (N_AB_LAYERS, G_V), 0.05),
        "ab_w_out": nrm(ks[11], (N_AB_LAYERS, AB_MIX, D_MODEL), AB_MIX ** -0.5),
        "c_w_in": nrm(ks[12], (N_C_LAYERS, D_MODEL, C_IN), D_MODEL ** -0.5),
        "c_lb_logits": nrm(ks[13], (DEPTH, C_K_TOTAL), 0.5),
        "c_norm": 1.0 + nrm(ks[14], (N_C_LAYERS, C_MIX), 0.05),
        "c_w_out": nrm(ks[15], (N_C_LAYERS, C_MIX, D_MODEL), C_MIX ** -0.5),
        "ffn_w_up": nrm(ks[16], (DEPTH, D_MODEL, 2 * D_FF), D_MODEL ** -0.5),
        "ffn_conv_w": nrm(ks[17], (DEPTH, FFN_CONV, 2 * D_FF), FFN_CONV ** -0.5),
        "ffn_conv_b": nrm(ks[18], (DEPTH, 2 * D_FF), 0.02),
        "ffn_w_down": nrm(ks[19], (DEPTH, D_FF, D_MODEL), D_FF ** -0.5),
    }

def second_block(x, norm_gains, ab_w_in, ab_conv_m, ab_m_gate_bias, ab_m_norm, ab_conv_g, ab_g_a_log,
              ab_g_dt_bias, ab_g_norm, ab_w_out, c_w_in, c_lb_logits, c_norm, c_w_out,
              ffn_w_up, ffn_conv_w, ffn_conv_b, ffn_w_down):
    lower_bounds = hgrn_lower_bounds(c_lb_logits)
    for layer in range(DEPTH):
        j = layer // 2
        u = rms_norm(x, norm_gains[layer, 0])
        if layer % 2 == 0:
            mix = ab_mixer(u, ab_w_in[j], ab_conv_m[j], ab_m_gate_bias[j], ab_m_norm[j], ab_conv_g[j],
                           ab_g_a_log[j], ab_g_dt_bias[j], ab_g_norm[j], ab_w_out[j])
        else:
            mix = hgrn2_mixer(u, c_w_in[j], lower_bounds[layer], c_norm[j], c_w_out[j])
        x = x + rms_norm(mix, norm_gains[layer, 1])
        u = rms_norm(x, norm_gains[layer, 2])
        ff = conv_ffn(u, ffn_w_up[layer], ffn_conv_w[layer], ffn_conv_b[layer], ffn_w_down[layer])
        x = x + rms_norm(ff, norm_gains[layer, 3])
    return x


def setup_inputs(seed=0):
    out = dict(first_inputs(seed))
    for name, value in second_inputs(seed + 1).items():
        if name != "x":
            out[name + "_2"] = value
    return out


def reference(
    x, a_norm, a_w_in, a_w_out, a_q_norm, a_k_norm, a_lq1, a_lk1, a_lq2, a_lk2, a_subln,
    kv_norm, w_kv, b_norm, b_w_in, b_w_out, norm_gains_2, ab_w_in_2, ab_conv_m_2,
    ab_m_gate_bias_2, ab_m_norm_2, ab_conv_g_2, ab_g_a_log_2, ab_g_dt_bias_2, ab_g_norm_2,
    ab_w_out_2, c_w_in_2, c_lb_logits_2, c_norm_2, c_w_out_2, ffn_w_up_2, ffn_conv_w_2,
    ffn_conv_b_2, ffn_w_down_2,
):
    x = first_block(
        x, a_norm, a_w_in, a_w_out, a_q_norm, a_k_norm, a_lq1, a_lk1, a_lq2, a_lk2, a_subln,
        kv_norm, w_kv, b_norm, b_w_in, b_w_out,
    )
    return second_block(
        x, norm_gains_2, ab_w_in_2, ab_conv_m_2, ab_m_gate_bias_2, ab_m_norm_2, ab_conv_g_2,
        ab_g_a_log_2, ab_g_dt_bias_2, ab_g_norm_2, ab_w_out_2, c_w_in_2, c_lb_logits_2,
        c_norm_2, c_w_out_2, ffn_w_up_2, ffn_conv_w_2, ffn_conv_b_2, ffn_w_down_2,
    )


_drawn_inputs = setup_inputs


def setup_inputs(seed=0):
    import zlib

    import numpy as np

    out = dict(_drawn_inputs(seed))
    spreads = {}
    factors = {'a_q_norm': 3.567,
     'a_k_norm': 3.083,
     'a_lk2': 8.0,
     'a_subln': 2.781,
     'kv_norm': 4.094,
     'b_norm': 3.904,
     'norm_gains_2': 3.275,
     'ab_m_norm_2': 8.0,
     'ab_g_a_log_2': 8.0,
     'ab_g_dt_bias_2': 3.098,
     'ab_g_norm_2': 8.0,
     'c_lb_logits_2': 8.0,
     'c_norm_2': 8.0,
     'ffn_conv_b_2': 8.0}
    for name, (base, spread) in spreads.items():
        noise = np.random.default_rng([zlib.crc32(name.encode()), seed]).standard_normal(out[name].shape)
        drawn = base * np.exp(spread * noise) if base else spread * noise
        out[name] = __import__('jax').numpy.asarray(drawn.astype(out[name].dtype))
    for name, factor in factors.items():
        out[name] = (out[name] * factor).astype(out[name].dtype)
    return out
```

```python
import math
import numpy as np
import concourse.bass as bass
from concourse import mybir

F32 = mybir.dt.float32
I32 = mybir.dt.int32
ALU = mybir.AluOpType
ACT = mybir.ActivationFunctionType
AX = mybir.AxisListType

P = 128
D = 1024
S = 256
ST = S // P
KT = D // P
NC = 512
EPS = 1e-6
DA_HEADS, DA_DIM = 8, 64
SB_HEADS, SB_DIM = 16, 64
M_HEADS, G_HEADS, C_HEADS = 4, 4, 8
D_FF = 2816
FT = D_FF // P
LAMBDA_INIT = 0.8 - 0.6 * math.exp(-0.3 * 0)
ROPE_THETA, ROT = 500000.0, 16
LEVELS = [1, 2, 4, 8, 16, 32, 64]
NEG = -1.0e30

AB_MQK, AB_MV, AB_MO, AB_MG, AB_GQKV, AB_GG, AB_GAB = 0, 512, 1024, 1536, 1544, 3080, 3592

ROW = {}


def _rows():
    at = 0
    for name, n in [("a_norm", 8), ("kv_norm", 8), ("b_norm", 8), ("subln", 1), ("n00", 8), ("n02", 8),
                    ("n10", 8), ("n12", 8), ("m_norm", 4), ("g_norm", 4), ("c_norm", 8), ("lb", 16),
                    ("conv_m", 16)]:
        ROW[name] = at
        at += n
    assert at <= P
    ROW["conv_g"] = P
    for l in range(2):
        for i, name in enumerate(("tap0", "tap1", "tap2", "bias")):
            ROW[f"{name}_{l}"] = (2 + 2 * l + i // 2) * P + (i % 2) * 2 * FT


_rows()
ROW_COUNTS = [105, 48, 88, 88, 88, 88]

CONST = {}


def _const():
    at = 0
    for name, n in [("ident", P), ("upper", P), ("after", P), ("sb_neg", P), ("neg_ones", P), ("ones", P),
                    ("causal_neg", P), ("sb_mask", 3 * P), ("sb_bias", 3 * P), ("levels", P * len(LEVELS)),
                    ("cos", ST * ROT // 2), ("sin", ST * ROT // 2), ("select", 4 * P)]:
        CONST[name] = (at, n)
        at += n
    return at


N_CONST = _const()


def constant_table():
    t = np.zeros((P, N_CONST), np.float32)
    r, c = np.arange(P)[:, None], np.arange(P)[None, :]

    def put(name, value):
        at, n = CONST[name]
        t[:, at:at + n] = value

    put("ident", r == c)
    put("upper", r <= c)
    put("after", r > c)
    put("sb_neg", -(r >= c).astype(np.float32))
    put("neg_ones", -1.0)
    put("ones", 1.0)
    put("causal_neg", np.where(c <= r, 0.0, NEG))
    strict = (r < c).astype(np.float32)
    full = np.ones((P, P), np.float32)
    put("sb_mask", np.concatenate([strict, full, strict], 1))
    put("sb_bias", np.where(np.concatenate([strict, full, strict], 1) > 0, 0.0, NEG))
    put("levels", np.concatenate([(r // (2 * n) == c // (2 * n)) & (r // n % 2 == 0) & (c // n % 2 == 1)
                                  for n in LEVELS], 1))
    half = ROT // 2
    inv = np.power(np.float32(ROPE_THETA), -np.arange(half, dtype=np.float32) / np.float32(half))
    ang = np.arange(S, dtype=np.float32)[:, None] * inv.astype(np.float32)[None, :]
    for name, f in (("cos", np.cos), ("sin", np.sin)):
        put(name, f(ang).astype(np.float32).reshape(ST, P, half).transpose(1, 0, 2).reshape(P, -1))
    sel = np.zeros((P, 4, P), np.float32)
    for h in range(4):
        sel[h, h] = 1.0
    put("select", sel.reshape(P, -1))
    return t


class Count:

    def __init__(self, nc, name, all_counts):
        self.sem, self.name, self.a, self.b = nc.alloc_semaphore(name), name, 0, 0
        all_counts.append(self)

    def now(self):
        return (self, self.a, self.b)


def before(token):
    return (token[0], token[1] - token[2], token[2])


class Queue:

    def __init__(self, prog, eng, name):
        self.prog, self.eng, self.count, self.seen = prog, eng, Count(prog.nc, name, prog.counts), {}

    def wait(self, *tokens):
        for t in tokens:
            if t is None:
                continue
            if isinstance(t, list):
                self.wait(*t)
                continue
            c, a, b = t
            if b == 0 and a <= 0:
                continue
            if any(bb == b and aa >= a for aa, bb in self.seen.get(c, ())):
                continue
            self.seen.setdefault(c, []).append((a, b))
            if self.prog.dry:
                continue
            assert a >= 1, (c.name, a, b)
            self.eng.wait_ge(c.sem, a + self.prog.i * b if b else a)

    def __call__(self, make, *tokens, inc=None, by=1):
        self.wait(*tokens)
        c = inc or self.count
        if not self.prog.dry:
            make().then_inc(c.sem, by)
        c.a += by
        return c.now()

    def many(self, makes, *tokens, inc=None):
        self.wait(*tokens)
        c = inc or self.count
        if not self.prog.dry:
            for m in makes[:-1]:
                m()
            makes[-1]().then_inc(c.sem, 1)
        c.a += 1
        return c.now()


class Program:
    def __init__(self, nc):
        self.nc, self.counts, self.dry, self.i = nc, [], False, 0
        self.pe = Queue(self, nc.tensor, "pe_done")
        self.act = Queue(self, nc.scalar, "act_done")
        self.dve = Queue(self, nc.vector, "dve_done")
        self.pool = Queue(self, nc.gpsimd, "pool_done")
        self.sp = Queue(self, nc.sync, "sp_dma")
        self.queues = [self.pe, self.act, self.dve, self.pool, self.sp]

    def counter(self, name):
        return Count(self.nc, name, self.counts)

    def loop(self, n, body, state):
        start = [(c, c.a) for c in self.counts]
        seen = [{k: list(v) for k, v in q.seen.items()} for q in self.queues]
        self.dry = True
        end = body(0, state)
        self.dry = False
        step = {c: c.a - a for c, a in start}
        for c, a in start:
            c.a, c.b = a, step[c]
        for q, s in zip(self.queues, seen):
            q.seen = {k: list(v) for k, v in s.items()}
        state = {k: (t[0], t[1] - step[t[0]], step[t[0]]) for k, t in end.items()}
        with self.nc.Fori(0, n) as i:
            self.i = i
            body(i, state)
        self.i = 0
        for c, a in start:
            assert c.a == a + step[c]
            c.a, c.b = a + n * step[c], 0
        for q, s in zip(self.queues, seen):
            q.seen = s
        return {k: (t[0], t[0].a - (step[t[0]] - (t[1] - dict(start)[t[0]])), 0) for k, t in end.items()}


def build(nc, a, out, table):
    g = Program(nc)
    pe, act, dve, pool, sp = g.pe, g.act, g.dve, g.pool, g.sp

    def sb(name, *shape, dt=F32):
        return nc.alloc_sbuf_tensor(name, [P, *shape], dt)

    ring = [sb(f"weights{i}", 8, NC) for i in range(2)]
    x_res = sb("x_res", ST, D)
    normed = sb("normed", ST, D)
    u_t = sb("u_t", KT, S)
    u2_t = sb("u2_t", KT, S)
    big = sb("big", 4 * ST * D)
    feat = sb("feat", 16, S)
    scr = sb("scr", 14 * 1024)
    const = sb("const", N_CONST)
    cols = sb("cols", 6 * P)
    post_gain = sb("post_gain", 4, D)
    qk_gain = sb("qk_gain", 2, DA_DIM)
    lam_in = sb("lam_in", 4, DA_DIM)
    small = sb("small", 640)
    psum = nc.alloc_psum_tensor("psum", [P, 8, NC], F32)

    def c_(name, lo=0, hi=None):
        at, n = CONST[name]
        return const[:, at + lo:at + (n if hi is None else hi)]

    def col(name, j=0, tile=None):
        k = ROW[name]
        return cols[:, bass.ds(k + j, 1)] if not isinstance(j, int) else cols[:, k + j:k + j + 1]

    def view(buf, at, *dims):
        n = 1
        for d in dims:
            n *= d
        v = buf[:, at:at + n]
        if len(dims) == 1:
            return v
        names = "abcd"[:len(dims)]
        return v.rearrange(f"p ({' '.join(names)}) -> p {' '.join(names)}",
                           **{m: d for m, d in zip(names[1:], dims[1:])})

    small_at = [0]

    def tiny(*dims):
        n = int(np.prod(dims))
        v = view(small, small_at[0], *dims)
        small_at[0] += n
        assert small_at[0] <= 640
        return v

    ident = c_("ident")

    loaded = [g.counter(f"loaded{i}") for i in range(2)]
    used = [g.counter(f"used{i}") for i in range(2)]
    loads = [0]
    slot_free = [[], []]
    bank_free = {b: [] for b in range(8)}

    def mm(o, lhs, rhs, start=True, stop=True, loose=False):
        kw = {"skip_group_check": True} if loose else {}
        return lambda: nc.tensor.matmul(o, lhs, rhs, start=start, stop=stop, **kw)

    def tr(o, src, n=P):
        return lambda: nc.tensor.transpose(o, src, ident[0:n, 0:n])

    in_x, in_const, in_rows, in_gain, in_first = (g.counter(n) for n in
                                                  ("in_x", "in_const", "in_rows", "in_gain", "in_first"))

    def fetch(dst, src, inc):
        return act(lambda: nc.scalar.dma_start(dst, src), inc=inc, by=16)

    x_here = fetch(x_res[:, :, :], a["x"].rearrange("b (t p) n -> p (b t) n", p=P), in_x)
    const_here = fetch(const[:, :], table, in_const)
    rows = [view(scr, i * P, P) for i in range(6)]

    def as_rows(src):
        return src.rearrange("(r c) -> r c", c=P)

    def put_rows(name, src, n):
        k = ROW[name]
        fetch(rows[k // P][k % P:k % P + n, :], as_rows(src), in_rows)

    put_rows("a_norm", a["a_norm"][0, :], 8)
    put_rows("kv_norm", a["kv_norm"], 8)
    put_rows("b_norm", a["b_norm"][0, :], 8)
    put_rows("subln", a["a_subln"][0, :], 1)
    for l in range(2):
        put_rows(f"n{l}0", a["norm_gains_2"][l, 0, :], 8)
        put_rows(f"n{l}2", a["norm_gains_2"][l, 2, :], 8)
    put_rows("m_norm", a["ab_m_norm_2"][0, :], 4)
    put_rows("g_norm", a["ab_g_norm_2"][0, :], 4)
    put_rows("c_norm", a["c_norm_2"][0, :], 8)
    put_rows("lb", a["c_lb_logits_2"].rearrange("l c -> (l c)"), 16)
    put_rows("conv_m", a["ab_conv_m_2"][0, :, :].rearrange("t c -> (t c)"), 16)
    put_rows("conv_g", a["ab_conv_g_2"][0, :, :].rearrange("t c -> (t c)"), 48)
    for l in range(2):
        for tap in range(3):
            put_rows(f"tap{tap}_{l}", a["ffn_conv_w_2"][l, tap, :], 2 * FT)
        put_rows(f"bias_{l}", a["ffn_conv_b_2"][l, :], 2 * FT)
    rows_here = in_rows.now()

    def across(src):
        return src.rearrange("(a n) -> a n", a=1).broadcast_to([P, src.shape[0]])

    for i, n in enumerate(("a_q_norm", "a_k_norm")):
        fetch(qk_gain[:, i, :], across(a[n][0, :]), in_gain)
    for i, n in enumerate(("a_lq1", "a_lk1", "a_lq2", "a_lk2")):
        fetch(lam_in[:, i, :], across(a[n][0, :]), in_gain)
    for l in range(2):
        for i, k in enumerate((1, 3)):
            fetch(post_gain[:, 2 * l + i, :], across(a["norm_gains_2"][l, k, :]), in_gain)
    gate_col = tiny(4)
    for i, src in enumerate((a["ab_m_gate_bias_2"][0, 0, :], a["ab_m_gate_bias_2"][0, 1, :],
                             a["ab_g_dt_bias_2"][0, :], a["ab_g_a_log_2"][0, :])):
        fetch(gate_col[0:4, i:i + 1], src.rearrange("(n a) -> n a", a=1), in_gain)
    gains_here = in_gain.now()

    def load(cut, slot):
        def go(dst, src):
            return sp(lambda: nc.sync.dma_start(dst, src), used[slot].now(), slot_free[slot],
                      inc=loaded[slot], by=16)
        t = None
        for dst, src in cut(ring[slot]):
            t = go(dst, src)
        slot_free[slot] = []
        return t

    def w_cols(w, c0, n=NC):
        w3 = w.rearrange("(k p) n -> p k n", p=P)
        cc = slice(c0, c0 + n) if isinstance(c0, int) else bass.ds(c0, n)
        return lambda r: [(r[:, 0:4, 0:n], w3[:, 0:4, cc]), (r[:, 4:8, 0:n], w3[:, 4:8, cc])]

    def chunk_tokens(w, c0, src_t, ready, slot=None, free=None):
        if slot is None:
            slot = loads[0] % 2
            loads[0] += 1
        here = load(w_cols(w, c0), slot)
        toks = []
        for t in range(ST):
            b = 2 * slot + t
            pe.wait(here, ready, bank_free[b] if free is None else free[t])
            toks.append(pe.many([mm(psum[:, b, :], src_t[:, k, t * P:(t + 1) * P], ring[slot][:, k, :],
                                    k == 0, k == KT - 1) for k in range(KT)],
                                inc=used[slot] if t == ST - 1 else None))
        return slot, toks

    def chunk_features(w, c0, src_t, ready):
        slot = loads[0] % 2
        loads[0] += 1
        here = load(w_cols(w, c0), slot)
        toks = []
        for pair in range(2):
            b = 2 * slot + pair
            pe.wait(here, ready, bank_free[b])
            toks.append(pe.many([mm(psum[:, b, (f % 2) * S:(f % 2 + 1) * S], ring[slot][:, k, f * P:(f + 1) * P],
                                    src_t[:, k, :], k == 0, k == KT - 1)
                                 for f in (2 * pair, 2 * pair + 1) for k in range(KT)],
                                inc=used[slot] if pair == 1 else None))
        return slot, toks

    def rstd_of(sums, n, ready, dst):
        t = dve(lambda: nc.vector.tensor_scalar(dst, sums, 1.0 / n, EPS, ALU.mult, ALU.add), ready)
        t = act(lambda: nc.scalar.activation(dst, dst, ACT.Sqrt), t)
        return dve(lambda: nc.vector.reciprocal(dst, dst), t)

    def to_features(src, ready, write, banks=(4, 5, 6, 7)):
        done = []
        for kk in range(KT // 2):
            b = banks[kk % len(banks)]
            t = pe.many([tr(psum[:, b, (j * ST + s) * P:(j * ST + s + 1) * P],
                            src[:, s, (2 * kk + j) * P:(2 * kk + j + 1) * P]) for j in range(2) for s in range(ST)],
                        ready, bank_free[b])
            here = []
            for j in range(2):
                here += write(2 * kk + j, psum[:, b, j * S:(j + 1) * S], t)
            bank_free[b] = here
            done += here
        return last_of(done)

    def last_of(tokens):
        best = {}
        for c, v, b in tokens:
            if c not in best or best[c][1] < v:
                best[c] = (c, v, b)
        return list(best.values())

    def scaled(dst, src, column, k, *tokens):
        if k // 2 % 2 == 0:
            return act(lambda: nc.scalar.activation(dst, src, ACT.Copy, scale=column), *tokens)
        return dve(lambda: nc.vector.tensor_scalar(dst, src, column, None, ALU.mult), *tokens)

    def norm_features(ready, dsts, free):
        sums, rstd = tiny(ST), tiny(ST)
        sq = [act(lambda: nc.scalar.activation(normed[:, 0, :], x_res[:, 0, :], ACT.Square,
                                               accum_out=sums[:, 0:1]), ready, free),
              act(lambda: nc.scalar.activation(normed[:, 1, :], x_res[:, 1, :], ACT.Square,
                                               accum_out=sums[:, 1:2]))]
        r = rstd_of(sums, D, sq, rstd)
        n = [act(lambda: nc.scalar.activation(normed[:, 0, :], x_res[:, 0, :], ACT.Copy, scale=rstd[:, 0:1]), r),
             dve(lambda: nc.vector.tensor_scalar(normed[:, 1, :], x_res[:, 1, :], rstd[:, 1:2], None, ALU.mult), r)]

        def write(k, src, t):
            return [scaled(dst[:, k, :], src, col(gain, k), k, t, cols_here, free)
                    for m, (dst, gain) in enumerate(dsts)]

        return to_features(normed, n, write)

    cols_toks = []
    for i, n in enumerate(ROW_COUNTS):
        t = pe(tr(psum[:, 4 + i % 4, 0:n], rows[i][0:n, :], n), const_here, rows_here, bank_free[4 + i % 4])
        v = dve(lambda i=i, n=n: nc.vector.tensor_copy(cols[:, i * P:i * P + n], psum[:, 4 + i % 4, 0:n]), t)
        bank_free[4 + i % 4] = [v]
        cols_toks.append(v)
    cols_here = cols_toks[-1]

    lam_p, lam_s, lam_e, neg_lam, sub_gain = tiny(2, DA_DIM), tiny(2), tiny(2), tiny(1), tiny(1)
    t = dve(lambda: nc.vector.tensor_tensor(lam_p, lam_in[:, 0:4:2, :], lam_in[:, 1:4:2, :], ALU.mult), gains_here)
    t = dve(lambda: nc.vector.tensor_reduce(lam_s, lam_p, AX.X, ALU.add), t)
    t = act(lambda: nc.scalar.activation(lam_e, lam_s, ACT.Exp), t)
    t = dve(lambda: nc.vector.tensor_tensor(neg_lam, lam_e[:, 1:2], lam_e[:, 0:1], ALU.subtract), t)
    t = dve(lambda: nc.vector.tensor_scalar(neg_lam, neg_lam, LAMBDA_INIT, None, ALU.subtract), t)
    lam_here = dve(lambda: nc.vector.tensor_scalar(sub_gain, col("subln"), 1.0 - LAMBDA_INIT, None, ALU.mult),
                   cols_here)

    w_in, w_out = a["a_w_in"][0, :, :], a["a_w_out"][0, :, :]
    u_here = norm_features(x_here, [(u_t, "a_norm")], None)
    proj = view(big, 0, ST, 4 * D)

    def take_chunk(c, slot, toks, w=NC):
        dst = proj[:, :, bass.ds(c * NC, NC)] if not isinstance(c, int) else proj[:, :, c * NC:(c + 1) * NC]
        e0 = act(lambda: nc.scalar.activation(dst[:, 0, :], psum[:, 2 * slot, :], ACT.Copy), toks[0])
        e1 = dve(lambda: nc.vector.tensor_copy(dst[:, 1, :], psum[:, 2 * slot + 1, :]), toks[1])
        return e0, e1

    for c in range(2):
        slot, toks = chunk_tokens(w_in, c * NC, u_t, u_here)
        e = take_chunk(c, slot, toks)
        bank_free[2 * slot], bank_free[2 * slot + 1] = [e[0]], [e[1]]

    for b in range(4):
        pe.wait(bank_free[b])

    def qk_chunks(i, st):
        new = {}
        for s in range(2):
            c = i * 2 + (2 + s)
            slot, toks = chunk_tokens(w_in, c * NC, u_t, u_here, slot=s, free=(st.get((s, 0)), st.get((s, 1))))
            new[s, 0], new[s, 1] = take_chunk(c, slot, toks)
        return new

    end = g.loop(7 // 2, qk_chunks, {})
    for s in range(2):
        bank_free[2 * s], bank_free[2 * s + 1] = [end[s, 0]], [end[s, 1]]
    got_qkvg = [end[k] for k in end]

    groups = 2 * D // DA_DIM
    qk_sq = [view(scr, 6 * P + t * 2 * D, groups, DA_DIM) for t in range(ST)]
    qk_sum, qk_rstd = tiny(ST, groups), tiny(ST, groups)
    rope = view(scr, 6 * P + 4 * D, 4, groups, ROT // 2)
    qt, kt = feat[:, 0:8, :], feat[:, 8:16, :]
    qk_written = []
    for t in range(ST):
        qk = proj[:, t, 0:2 * D].rearrange("p (g d) -> p g d", d=DA_DIM)
        s = act(lambda t=t, qk=qk: nc.scalar.activation(qk_sq[t], qk, ACT.Square), got_qkvg)
        s = dve(lambda t=t: nc.vector.tensor_reduce(qk_sum[:, t, :], qk_sq[t], AX.X, ALU.add), s)
        r = rstd_of(qk_sum[:, t, :], DA_DIM, s, qk_rstd[:, t, :])
        n = dve(lambda t=t, qk=qk: nc.vector.tensor_tensor(
            qk, qk, qk_rstd[:, t, :].unsqueeze(2).broadcast_to([P, groups, DA_DIM]), ALU.mult), r)
        for half in range(2):
            part = qk[:, half * 16:(half + 1) * 16, :]
            n2 = pool(lambda part=part, half=half: nc.gpsimd.tensor_tensor(
                part, part, qk_gain[:, half:half + 1, :].broadcast_to([P, 16, DA_DIM]), ALU.mult), n, gains_here)
        t1, t2 = qk[:, :, 0:8], qk[:, :, 8:16]
        cs = c_("cos", t * 8, t * 8 + 8).unsqueeze(1).broadcast_to([P, groups, 8])
        sn = c_("sin", t * 8, t * 8 + 8).unsqueeze(1).broadcast_to([P, groups, 8])
        for i, (x, w) in enumerate(((t1, cs), (t2, sn), (t1, sn), (t2, cs))):
            m = dve(lambda i=i, x=x, w=w: nc.vector.tensor_tensor(rope[:, i], x, w, ALU.mult), n2, const_here)
        r1 = dve(lambda: nc.vector.tensor_tensor(t1, rope[:, 0], rope[:, 1], ALU.subtract), m)
        r2 = dve(lambda: nc.vector.tensor_tensor(t2, rope[:, 2], rope[:, 3], ALU.add), m)
        for q in range(4):
            b = 4 + q
            tt = pe.many([tr(psum[:, b, j * P:(j + 1) * P], proj[:, t, (4 * q + j) * P:(4 * q + j + 1) * P])
                          for j in range(4)], r2, n2, bank_free[b])
            dst = feat[:, 4 * q:4 * q + 4, t * P:(t + 1) * P]
            src = psum[:, b, :].rearrange("p (j t) -> p j t", j=4)
            if q % 2:
                w = act(lambda dst=dst, src=src: nc.scalar.activation(dst, src, ACT.Copy), tt)
            else:
                w = dve(lambda dst=dst, src=src: nc.vector.tensor_copy(dst, src), tt)
            bank_free[b] = [w]
            qk_written.append(w)
    qk_written = last_of(qk_written)

    o_tok = view(big, 0, ST, 4 * D)[:, :, 0:D]
    v_tok = proj[:, :, 2 * D:3 * D]
    probs = [view(scr, 6 * P + i * 768, 2, 384) for i in range(2)]
    mixed = [view(scr, 6 * P + 1536 + i * 384, 384) for i in range(2)]
    mixed_t = [view(scr, 6 * P + 2304 + i * 384, 384) for i in range(2)]
    peak, denom, inv = [[tiny(2, 2) for _ in range(2)] for _ in range(3)]
    scale = DA_DIM ** -0.5
    sc_free, bt_free, mixed_free, probs_free = [[], []], [[], []], [[], []], [[], []]
    o_written = []
    for b in range(8):
        pe.wait(bank_free[b])
    for h in range(DA_HEADS):
        z = h % 2
        sc = psum[:, 4 * z:4 * z + 2, :]
        bt, bo = psum[:, 4 * z + 2, :], psum[:, 4 * z + 3, :]
        for c in range(2):
            r = slice(64 * c, 64 * c + 64)
            s = pe.many([mm(sc[:, c, 0:P], qt[r, h, 0:P], kt[r, h, 0:P]),
                         mm(sc[:, c, P:3 * P], qt[r, h, P:S], kt[r, h, 0:S])],
                        qk_written, sc_free[z])
        diag = sc.rearrange("p c (j n) -> p c j n", n=P)[:, :, 0:3:2, :]
        m = dve(lambda diag=diag: nc.vector.tensor_tensor(
            diag, diag, c_("causal_neg").unsqueeze(1).unsqueeze(1).broadcast_to([P, 2, 2, P]), ALU.add), s)
        m0 = dve(lambda sc=sc, z=z: nc.vector.tensor_reduce(peak[z][:, 0, :], sc[:, :, 0:P], AX.X, ALU.max), m)
        m1 = dve(lambda sc=sc, z=z: nc.vector.tensor_reduce(peak[z][:, 1, :], sc[:, :, P:3 * P], AX.X, ALU.max), m)
        m = dve(lambda z=z: nc.vector.tensor_scalar(peak[z], peak[z], -scale, None, ALU.mult), m1)
        for t in range(ST):
            cs = slice(0, P) if t == 0 else slice(P, 3 * P)
            for c in range(2):
                e = act(lambda t=t, c=c, cs=cs, z=z, sc=sc: nc.scalar.activation(
                    probs[z][:, c, cs], sc[:, c, cs], ACT.Exp, bias=peak[z][:, t, c:c + 1], scale=scale,
                    accum_out=denom[z][:, t, c:c + 1]), m, probs_free[z])
        sc_free[z] = [e]
        i_ = dve(lambda z=z: nc.vector.reciprocal(inv[z], denom[z]), e)
        i_ = dve(lambda z=z: nc.vector.tensor_scalar(inv[z][:, :, 1], inv[z][:, :, 1], neg_lam, None, ALU.mult),
                 i_, lam_here)
        for t in range(ST):
            cs = slice(0, P) if t == 0 else slice(P, 3 * P)
            x1 = dve(lambda cs=cs, z=z, t=t: nc.vector.tensor_scalar(
                mixed[z][:, cs], probs[z][:, 0, cs], inv[z][:, t, 0:1], None, ALU.mult), i_, mixed_free[z])
            x1 = dve(lambda cs=cs, z=z, t=t: nc.vector.scalar_tensor_tensor(
                mixed[z][:, cs], probs[z][:, 1, cs], inv[z][:, t, 1:2], mixed[z][:, cs], ALU.mult, ALU.add), x1)
        probs_free[z] = [x1]
        tt = pe.many([tr(bt[:, j * P:(j + 1) * P], mixed[z][:, j * P:(j + 1) * P]) for j in range(3)],
                     x1, bt_free[z])
        mixed_free[z] = [tt]
        w = act(lambda z=z, bt=bt: nc.scalar.activation(mixed_t[z], bt[:, 0:3 * P], ACT.Copy), tt)
        vh = slice(h * P, (h + 1) * P)
        o = pe.many([mm(bo[:, 0:P], mixed_t[z][:, 0:P], v_tok[:, 0, vh]),
                     mm(bo[:, P:S], mixed_t[z][:, P:2 * P], v_tok[:, 0, vh], True, False),
                     mm(bo[:, P:S], mixed_t[z][:, 2 * P:3 * P], v_tok[:, 1, vh], False, True)], w)
        w = dve(lambda vh=vh, bo=bo: nc.vector.tensor_copy(o_tok[:, :, vh], bo[:, 0:S].rearrange(
            "p (t n) -> p t n", t=ST)), o)
        bt_free[z] = [w]
        o_written.append(w)
    for b in range(8):
        bank_free[b] = [o_written[-1]]

    def silu_of(dst, src, *ready):
        return act(lambda: nc.scalar.activation(dst, src, ACT.Silu), *ready)

    def head_norm(o, heads, ready, sq):
        sums, rstd = tiny(ST, heads), tiny(ST, heads)
        s = pool(lambda: nc.gpsimd.tensor_tensor(sq, o, o, ALU.mult), ready)
        s = dve(lambda: nc.vector.tensor_reduce(sums, sq, AX.X, ALU.add), s)
        r = rstd_of(sums, P, s, rstd)
        return dve(lambda: nc.vector.tensor_tensor(
            o, o, rstd.unsqueeze(3).broadcast_to([P, ST, heads, P]), ALU.mult), r)

    gate = proj[:, :, 3 * D:4 * D]
    g_here = silu_of(gate, gate, got_qkvg)
    sq = view(scr, 6 * P + 4 * D, ST, 8, P)
    n = head_norm(o_tok.rearrange("p t (h n) -> p t h n", n=P), 8, o_written[-1], sq)
    y = normed
    y_here = dve(lambda: nc.vector.tensor_tensor(y[:, :, :], o_tok, gate, ALU.mult), n, g_here)
    y_here = to_features(y, y_here, lambda k, src, t: [scaled(u2_t[:, k, :], src, sub_gain, k, t, lam_here)])

    def add_projection(w, src_t, ready):
        done = []
        for c in range(2):
            slot, toks = chunk_tokens(w, c * NC, src_t, ready)
            for t in range(ST):
                dst = x_res[:, t, c * NC:(c + 1) * NC]
                e = dve(lambda dst=dst, b=2 * slot + t: nc.vector.tensor_tensor(dst, psum[:, b, :], dst, ALU.add),
                        toks[t])
                bank_free[2 * slot + t] = [e]
            done.append(e)
        return done[-1]

    x_here = add_projection(w_out, u2_t, y_here)

    w_kv, w_in, w_out = a["w_kv"], a["b_w_in"][0, :, :], a["b_w_out"][0, :, :]
    u_here = norm_features(x_here, [(u_t, "kv_norm"), (u2_t, "b_norm")], None)

    def take_features(dst, slot, toks, scale=None):
        src = [psum[:, 2 * slot + i, :].rearrange("p (f t) -> p f t", f=2) for i in range(2)]
        e0 = act(lambda: nc.scalar.activation(dst[:, 0:2, :], src[0], ACT.Copy, scale=scale or 1.0), toks[0])
        e1 = dve(lambda: nc.vector.tensor_scalar(dst[:, 2:4, :], src[1], scale or 1.0, None, ALU.mult), toks[1])
        bank_free[2 * slot], bank_free[2 * slot + 1] = [e0], [e1]
        return [e0, e1]

    def take_tokens(dst, slot, toks):
        e0 = act(lambda: nc.scalar.activation(dst[:, 0], psum[:, 2 * slot, :], ACT.Copy), toks[0])
        e1 = dve(lambda: nc.vector.tensor_copy(dst[:, 1], psum[:, 2 * slot + 1, :]), toks[1])
        bank_free[2 * slot], bank_free[2 * slot + 1] = [e0], [e1]
        return [e0, e1]

    v_tok, gate = view(big, 0, ST, D), view(big, ST * D, ST, D)
    for c in range(2):
        slot, toks = chunk_features(w_kv, c * NC, u_t, u_here)
        qk_here = take_features(kt[:, 4 * c:4 * c + 4, :], slot, toks)
    for c in range(2):
        slot, toks = chunk_features(w_in, c * NC, u2_t, u_here)
        qk_here = take_features(qt[:, 4 * c:4 * c + 4, :], slot, toks, scale=SB_DIM ** -0.5)
    for c in range(2):
        slot, toks = chunk_tokens(w_kv, D + c * NC, u_t, u_here)
        v_here = take_tokens(v_tok[:, :, c * NC:(c + 1) * NC], slot, toks)
    for c in range(2):
        slot, toks = chunk_tokens(w_in, D + c * NC, u2_t, u_here)
        g_here = take_tokens(gate[:, :, c * NC:(c + 1) * NC], slot, toks)
    g_here = silu_of(gate, gate, g_here)

    soft = [view(scr, i * 768, 2, 384) for i in range(2)]
    work = [view(scr, 1536 + i * 768, 2, 384) for i in range(2)]
    stick = [view(scr, 3072 + i * 768, 2, 384) for i in range(2)]
    z_free, soft_free, stick_free = [[], []], [[], []], [[], []]
    for b in range(4):
        pe.wait(bank_free[b])

    def pair_bcast(name):
        return c_(name).unsqueeze(1).broadcast_to([P, 2, 384])

    for hp in range(SB_HEADS // 2):
        i = hp % 2
        zz = psum[:, 4 + 2 * i:6 + 2 * i, 0:384]
        for c in range(2):
            r = slice(64 * c, 64 * c + 64)
            s = pe.many([mm(zz[:, c, 0:S], kt[r, hp, 0:P], qt[r, hp, :], True, False),
                         mm(zz[:, c, S:384], kt[r, hp, P:S], qt[r, hp, P:S], False, True)],
                        qk_here, z_free[i] or [bank_free[4 + 2 * i], bank_free[5 + 2 * i]])
        e = act(lambda i=i, zz=zz: nc.scalar.activation(work[i], zz, ACT.Abs), s, soft_free[i])
        e = act(lambda i=i: nc.scalar.activation(work[i], work[i], ACT.Exp, scale=-1.0), e)
        e = act(lambda i=i: nc.scalar.activation(work[i], work[i], ACT.Ln, bias=1.0), e)
        d = dve(lambda i=i, zz=zz: nc.vector.scalar_tensor_tensor(
            soft[i], zz, 0.0, work[i], ALU.max, ALU.add), e, soft_free[i])
        d = dve(lambda i=i: nc.vector.tensor_tensor(soft[i], soft[i], pair_bcast("sb_mask"), ALU.mult), d)
        for c in range(2):
            s = pe.many([mm(zz[:, c, :], c_("sb_neg"), soft[i][:, c, :], False, False, True),
                         mm(zz[:, c, P:S], c_("neg_ones"), soft[i][:, c, S:384], False, True, True)], d)
        soft_free[i] = [s]
        d = dve(lambda i=i, zz=zz: nc.vector.scalar_tensor_tensor(
            stick[i], zz, 0.0, pair_bcast("sb_bias"), ALU.min, ALU.add), s, stick_free[i])
        z_free[i] = [d]
        e = act(lambda i=i: nc.scalar.activation(stick[i], stick[i], ACT.Exp), d)
        for c in range(2):
            hd = 2 * hp + c
            vh = slice(hd * 64, hd * 64 + 64)
            o0 = psum[:, hd // 8, (hd % 8) * 64:(hd % 8 + 1) * 64]
            o1 = psum[:, 2 + hd // 8, (hd % 8) * 64:(hd % 8 + 1) * 64]
            o = pe.many([mm(o0, stick[i][:, c, 0:P], v_tok[:, 0, vh]),
                         mm(o1, stick[i][:, c, P:S], v_tok[:, 0, vh], True, False),
                         mm(o1, stick[i][:, c, S:384], v_tok[:, 1, vh], False, True)], e, v_here)
        stick_free[i] = [o]
    y_here = []
    for t in range(ST):
        y_here.append(dve(lambda t=t: nc.vector.tensor_tensor(
            normed[:, t, :], psum[:, 2 * t:2 * t + 2, :].rearrange("p b n -> p (b n)"), gate[:, t, :], ALU.mult),
            o, g_here))
    for b in range(4):
        bank_free[b] = [y_here[-1]]
        bank_free[4 + b] = [y_here[-1]]

    def plain(dst):
        def write(k, src, t):
            if k // 2 % 2 == 0:
                return [act(lambda: nc.scalar.activation(dst[:, k, :], src, ACT.Copy), t)]
            return [dve(lambda: nc.vector.tensor_copy(dst[:, k, :], src), t)]
        return write

    y_here = to_features(normed, y_here, plain(u_t))
    x_here = add_projection(w_out, u_t, y_here)

    mix = view(scr, 0, ST, D)

    def mix_out(w, src_t, ready, gain):
        sums, rstd = tiny(ST), tiny(ST)
        e = []
        for c in range(2):
            slot, toks = chunk_tokens(w, c * NC, src_t, ready)
            e += take_tokens(mix[:, :, c * NC:(c + 1) * NC], slot, toks)
        return add_normed(mix, last_of(e), gain, normed)

    def add_normed(src, ready, gain, sq):
        sums, rstd = tiny(ST), tiny(ST)
        for t in range(ST):
            s = act(lambda t=t: nc.scalar.activation(sq[:, t, :], src[:, t, :], ACT.Square,
                                                     accum_out=sums[:, t:t + 1]), ready)
        r = rstd_of(sums, D, s, rstd)
        for t in range(ST):
            d = dve(lambda t=t: nc.vector.scalar_tensor_tensor(
                sq[:, t, :], src[:, t, :], rstd[:, t:t + 1], post_gain[:, gain, :], ALU.mult, ALU.mult),
                r, gains_here)
            d = dve(lambda t=t: nc.vector.tensor_tensor(x_res[:, t, :], x_res[:, t, :], sq[:, t, :], ALU.add), d)
        return d

    up_here = [g.counter(f"up_here{i}") for i in range(2)]
    up_used = [g.counter(f"up_used{i}") for i in range(2)]
    down_here = [g.counter(f"down_here{i}") for i in range(2)]
    down_used = [g.counter(f"down_used{i}") for i in range(2)]
    hidden_here = [g.counter(f"hidden{i}") for i in range(2)]

    def ffn(l, x_here):
        w_up = a["ffn_w_up_2"][l, :, :].rearrange("(k p) n -> p k n", p=P)
        w_down = a["ffn_w_down_2"][l, :, :]
        u_here = norm_features(x_here, [(u_t, f"n{l}2")], None)
        conv = [view(scr, i * 512, 2, S) for i in range(2)]
        silu = [view(scr, 1024 + i * S, S) for i in range(2)]
        hid = [view(scr, 1536 + i * S, S) for i in range(2)]
        for b in range(8):
            pe.wait(bank_free[b])
        for s in range(2):
            sp.wait(used[s].now(), slot_free[s])

        def up(j, s):
            gate_c = j * P if isinstance(j, int) else None
            cut = (lambda off: slice(off + j * P, off + (j + 1) * P) if isinstance(j, int)
                   else bass.ds(j * P + off, P))
            r = ring[s][:, :, :].rearrange("p k n -> p (k n)")
            wg = view(r, 0, KT, P)
            wv = view(r, KT * P, KT, P)
            wd = r[:, 2 * KT * P:2 * KT * P + D]
            sp(lambda: nc.sync.dma_start(wg, w_up[:, :, cut(0)]), up_used[s].now(), inc=up_here[s], by=16)
            here = sp(lambda: nc.sync.dma_start(wv, w_up[:, :, cut(D_FF)]), inc=up_here[s], by=16)
            sp(lambda: nc.sync.dma_start(wd, w_down[cut(0), :]), down_used[s].now(), inc=down_here[s], by=16)
            p = pe.many([mm(psum[:, s, i * S:(i + 1) * S], w[:, k, :], u_t[:, k, :], k == 0, k == KT - 1)
                         for i, w in enumerate((wg, wv)) for k in range(KT)],
                        here, u_here, hidden_here[s].now(), inc=up_used[s])
            for i in range(2):
                e = act(lambda i=i: nc.scalar.activation(
                    conv[s][:, i, :], psum[:, s, i * S:(i + 1) * S], ACT.Identity,
                    scale=col(f"tap2_{l}", j + i * FT), bias=col(f"bias_{l}", j + i * FT)),
                    p, hidden_here[s].now())
            d = [e, e]
            for tap in (1, 0):
                back = 2 - tap
                for i in range(2):
                    d[i] = dve(lambda i=i, back=back, tap=tap: nc.vector.scalar_tensor_tensor(
                        conv[s][:, i, back:], psum[:, s, i * S:(i + 1) * S - back], col(f"tap{tap}_{l}", j + i * FT),
                        conv[s][:, i, back:], ALU.mult, ALU.add), d[i])
            e = act(lambda: nc.scalar.activation(silu[s], conv[s][:, 0, :], ACT.Silu), d[0], hidden_here[s].now())
            dve(lambda: nc.vector.tensor_tensor(hid[s], silu[s], conv[s][:, 1, :], ALU.mult), e, d[1],
                down_used[s].now(), inc=hidden_here[s])

        def down(s, first=False, last=False):
            wd = ring[s][:, :, :].rearrange("p k n -> p (k n)")[:, 2 * KT * P:2 * KT * P + D]
            return pe.many([mm(psum[:, 4 + 2 * t + n, :], hid[s][:, t * P:(t + 1) * P], wd[:, n * NC:(n + 1) * NC],
                               first, last, True) for t in range(ST) for n in range(2)],
                           down_here[s].now(), hidden_here[s].now(), inc=down_used[s])

        up(0, 0)
        up(1, 1)
        down(0, first=True)

        def steps(i, st):
            up(i * 2 + 2, 0)
            down(1)
            up(i * 2 + 3, 1)
            down(0)
            return {}

        g.loop(FT // 2 - 1, steps, {})
        done = down(1, last=True)
        for s in range(2):
            slot_free[s] = [up_used[s].now(), down_used[s].now()]
            bank_free[s] = [hidden_here[s].now()]
        out_ps = psum[:, 4:8, :].rearrange("p (t b) n -> p t (b n)", t=ST)
        x_here = add_normed(out_ps, done, 2 * l + 1, normed)
        for b in range(4, 8):
            bank_free[b] = [x_here]
        return x_here

    w_in, w_out = a["ab_w_in_2"][0, :, :], a["ab_w_out_2"][0, :, :]
    u_here = norm_features(x_here, [(u_t, "n00")], None)
    gate_w = view(u2_t[:, :, :].rearrange("p k s -> p (k s)"), 0, KT, 16)
    w3 = w_in.rearrange("(k p) n -> p k n", p=P)
    gw_here = g.counter("gate_weights")
    sp(lambda: nc.sync.dma_start(gate_w[:, :, 0:8], w3[:, :, AB_MG:AB_MG + 8]), x_here, inc=gw_here, by=16)
    gw = sp(lambda: nc.sync.dma_start(gate_w[:, :, 8:16], w3[:, :, AB_GAB:AB_GAB + 8]), inc=gw_here, by=16)
    cv = feat
    v1 = view(big, 0, ST, M_HEADS, P + 1)
    o_gate = view(big, 1032, ST, NC)
    g_gate = view(big, 2056, ST, NC)
    ym = view(big, 3080, ST, D)
    g_tok = view(big, 5128, ST, 16)
    row = view(big, 5160, 11, S)
    t_ones = pool(lambda: nc.gpsimd.memset(v1[:, :, :, P:P + 1], 1.0), x_here)

    for t in range(ST):
        p = pe.many([mm(psum[:, 4, t * 16:(t + 1) * 16], u_t[:, k, t * P:(t + 1) * P], gate_w[:, k, :],
                        k == 0, k == KT - 1) for k in range(KT)], u_here, gw, bank_free[4])
    e = dve(lambda: nc.vector.tensor_copy(g_tok, psum[:, 4, 0:32].rearrange("p (t n) -> p t n", t=ST)), p)
    p = pe.many([tr(psum[0:4, 5 + kd // 2, (kd % 2) * S + t * P:(kd % 2) * S + (t + 1) * P],
                    g_tok[:, t, kd * 4:kd * 4 + 4]) for kd in range(4) for t in range(ST)],
                e, bank_free[5], bank_free[6])
    bank_free[4] = [e]
    gi, gf, ga, gb = (psum[0:4, 5 + kd // 2, (kd % 2) * S:(kd % 2 + 1) * S] for kd in range(4))
    R_A, R_ENM, R_G, R_B, R_C, R_T, R_U, R_V, R_I, R_X, R_Y = range(11)
    R_W = R_T

    def rw(k):
        return row[0:4, k, :]

    b15 = tiny(4)
    t0 = dve(lambda: nc.vector.tensor_scalar(b15[0:4, 0:2], gate_col[0:4, 0:2], 1.0 / 15.0, None, ALU.mult),
             gains_here)
    e1 = act(lambda: nc.scalar.activation(rw(R_I), gi, ACT.Tanh, scale=1.0 / 15.0, bias=b15[0:4, 0:1]), p, t0)
    e2 = act(lambda: nc.scalar.activation(rw(R_T), gf, ACT.Tanh, scale=1.0 / 15.0, bias=b15[0:4, 1:2]), p, t0)
    e = act(lambda: nc.scalar.activation(rw(R_T), rw(R_T), ACT.Exp, scale=-15.0), e2)
    e = act(lambda: nc.scalar.activation(rw(R_T), rw(R_T), ACT.Ln, bias=1.0), e)
    d = dve(lambda: nc.vector.tensor_tensor_scan(rw(R_U), c_("ones")[0:4, 0:1].broadcast_to([4, S]), rw(R_T), 0.0,
                                                 ALU.mult, ALU.add), e)
    d = dve(lambda: nc.vector.scalar_tensor_tensor(rw(R_A), rw(R_I), 15.0, rw(R_U), ALU.mult, ALU.add), d, e1)
    d = dve(lambda: nc.vector.tensor_tensor_scan(rw(R_C), c_("ones")[0:4, 0:1].broadcast_to([4, S]), rw(R_A), 0.0,
                                                 ALU.mult, ALU.max), d)
    d = dve(lambda: nc.vector.tensor_tensor(rw(R_ENM), rw(R_U), rw(R_C), ALU.subtract), d)
    m_rows = act(lambda: nc.scalar.activation(rw(R_ENM), rw(R_ENM), ACT.Exp), d)
    ea = tiny(1)
    e0 = act(lambda: nc.scalar.activation(ea[0:4, :], gate_col[0:4, 3:4], ACT.Exp), gains_here)
    d = ga_read = dve(lambda: nc.vector.tensor_scalar(rw(R_V), ga, gate_col[0:4, 2:3], None, ALU.add), p,
                      gains_here)
    e = act(lambda: nc.scalar.activation(rw(R_W), rw(R_V), ACT.Abs), d)
    e = act(lambda: nc.scalar.activation(rw(R_W), rw(R_W), ACT.Exp, scale=-1.0), e)
    d = dve(lambda: nc.vector.tensor_scalar(rw(R_X), rw(R_W), 2.0, None, ALU.add), e)
    d = dve(lambda: nc.vector.reciprocal(rw(R_X), rw(R_X)), d)
    d = dve(lambda: nc.vector.tensor_tensor(rw(R_W), rw(R_W), rw(R_X), ALU.mult), d)
    sq_here = d = dve(lambda: nc.vector.tensor_tensor(rw(R_X), rw(R_W), rw(R_W), ALU.mult), d)
    d = dve(lambda: nc.vector.tensor_scalar(rw(R_Y), rw(R_X), 1.0 / 17, None, ALU.mult), d)
    for k in (15, 13, 11, 9, 7, 5, 3):
        d = dve(lambda k=k: nc.vector.scalar_tensor_tensor(rw(R_Y), rw(R_Y), 1.0 / k, rw(R_X), ALU.add, ALU.mult), d)
    d = dve(lambda: nc.vector.scalar_tensor_tensor(rw(R_Y), rw(R_Y), 1.0, rw(R_W), ALU.add, ALU.mult), d)
    d = dve(lambda: nc.vector.tensor_scalar(rw(R_Y), rw(R_Y), 2.0, None, ALU.mult), d)
    d = dve(lambda: nc.vector.scalar_tensor_tensor(rw(R_V), rw(R_V), 0.0, rw(R_Y), ALU.max, ALU.add), d)
    g_row = dve(lambda: nc.vector.tensor_scalar(rw(R_G), rw(R_V), ea[0:4, :], -1.0, ALU.mult, ALU.mult), d, e0)
    e = act(lambda: nc.scalar.activation(rw(R_B), gb, ACT.Exp, scale=-1.0), p, ga_read)
    d = dve(lambda: nc.vector.tensor_scalar(rw(R_B), rw(R_B), 1.0, None, ALU.add), e)
    g_rows = dve(lambda: nc.vector.reciprocal(rw(R_B), rw(R_B)), d)
    bank_free[5] = bank_free[6] = [g_rows, e]
    gcol = tiny(4, ST, 4)
    p = pe.many([tr(psum[:, 4, (kd * ST + t) * 4:(kd * ST + t) * 4 + 4], row[0:4, kd, t * P:(t + 1) * P], 4)
                 for kd in range(4) for t in range(ST)], m_rows, g_rows, g_row, e, bank_free[4])
    gcol_here = dve(lambda: nc.vector.tensor_copy(gcol, psum[:, 4, 0:32].rearrange(
        "p (k t h) -> p k t h", k=4, t=ST)), p)
    bank_free[4] = [gcol_here]

    def gc(kind, t, h):
        return gcol[:, kind, t, h:h + 1]

    def conv_chunk(c0, tiles, taps, stride, base):
        slot, toks = chunk_features(w_in, c0, u_t, u_here)
        out_t, last_tap = [], []
        srcs = [psum[:, 2 * slot + f // 2, (f % 2) * S:(f % 2 + 1) * S] for f in range(4)]
        for f, src in enumerate(srcs):
            dst = cv[:, tiles + f, :]
            last_tap.append(act(lambda dst=dst, src=src, f=f: nc.scalar.activation(
                dst, src, ACT.Copy, scale=col(taps, 3 * stride + base + f)), toks[f // 2]))
        for f, src in enumerate(srcs):
            dst, e = cv[:, tiles + f, :], last_tap[f // 2 * 2 + 1]
            for tap in (2, 1, 0):
                back = 3 - tap
                e = dve(lambda dst=dst, src=src, f=f, back=back, tap=tap: nc.vector.scalar_tensor_tensor(
                    dst[:, back:], src[:, 0:S - back], col(taps, tap * stride + base + f), dst[:, back:],
                    ALU.mult, ALU.add), e)
            out_t.append(e)
        bank_free[2 * slot], bank_free[2 * slot + 1] = [out_t[1]], [out_t[3]]
        return silu_of(cv[:, tiles:tiles + 4, :], cv[:, tiles:tiles + 4, :], out_t[3])

    cv_here = []
    for n in range(3):
        cv_here.append(conv_chunk(AB_GQKV + n * NC, 4 + 4 * n, "conv_g", 12, 4 * n))
    mqk_here = conv_chunk(AB_MQK, 0, "conv_m", 4, 0)
    slot, toks = chunk_tokens(w_in, AB_MV, u_t, u_here)
    vs = [act(lambda: nc.scalar.activation(v1[:, 0, :, 0:P], psum[:, 2 * slot, :].rearrange(
        "p (h n) -> p h n", n=P), ACT.Copy), toks[0]),
        dve(lambda: nc.vector.tensor_copy(v1[:, 1, :, 0:P], psum[:, 2 * slot + 1, :].rearrange(
            "p (h n) -> p h n", n=P)), toks[1])]
    bank_free[2 * slot], bank_free[2 * slot + 1] = [vs[0]], [vs[1]]
    slot, toks = chunk_tokens(w_in, AB_MO, u_t, u_here)
    og = take_tokens(o_gate, slot, toks)
    og = act(lambda: nc.scalar.activation(o_gate, o_gate, ACT.Sigmoid), og)
    slot, toks = chunk_tokens(w_in, AB_GG, u_t, u_here)
    gg = take_tokens(g_gate, slot, toks)
    gg = silu_of(g_gate, g_gate, gg)

    def row_bcast(kind, h, dst):
        return mm(dst, c_("select", h * P, (h + 1) * P)[0:4, :], rw(kind))

    dm = view(scr, 0, M_HEADS, 384)
    st_ = view(scr, 1536, M_HEADS, 384)
    for b in range(8):
        pe.wait(bank_free[b])
    p = pe.many([row_bcast(R_C, h, psum[:, h // 2, (h % 2) * S:(h % 2 + 1) * S]) for h in range(4)], m_rows)
    for h in range(M_HEADS):
        cb = psum[:, h // 2, (h % 2) * S:(h % 2 + 1) * S]
        d = dve(lambda h=h, cb=cb: nc.vector.tensor_scalar(dm[:, h, 0:S], cb, gc(R_A, 0, h), 0.0,
                                                           ALU.subtract, ALU.max), p, gcol_here)
        d = dve(lambda h=h, cb=cb: nc.vector.tensor_scalar(dm[:, h, S:384], cb[:, P:S], gc(R_A, 1, h), 0.0,
                                                           ALU.subtract, ALU.max))
    e = act(lambda: nc.scalar.activation(dm, dm, ACT.Exp, scale=-1.0), d)
    dd = dm.rearrange("p h (j n) -> p h j n", n=P)[:, :, 0:3:2, :]
    msk = c_("upper").unsqueeze(1).unsqueeze(1).broadcast_to([P, 4, 2, P])
    dd_here = dve(lambda: nc.vector.tensor_tensor(dd, dd, msk, ALU.mult), e)
    outs = []
    for h in range(M_HEADS):
        r = slice(64 * (h % 2), 64 * (h % 2) + 64)
        sc = psum[:, 4 + h, 0:384]
        p = pe.many([mm(sc[:, 0:S], cv[r, 2 + h // 2, 0:P], cv[r, h // 2, :]),
                     mm(sc[:, S:384], cv[r, 2 + h // 2, P:S], cv[r, h // 2, P:S])], mqk_here)
        d = dve(lambda h=h, sc=sc: nc.vector.scalar_tensor_tensor(
            st_[:, h, :], sc, 64 ** -0.5, dm[:, h, :], ALU.mult, ALU.mult), p, dd_here)
        o = psum[:, h, 0:2 * (P + 1)]
        outs.append(pe.many([mm(o[:, 0:P + 1], st_[:, h, 0:P], v1[:, 0, h, :]),
                             mm(o[:, P + 1:], st_[:, h, P:S], v1[:, 0, h, :], True, False),
                             mm(o[:, P + 1:], st_[:, h, S:384], v1[:, 1, h, :], False, True)], d, vs, t_ones))
    o4 = psum[:, 0:4, 0:2 * (P + 1)].rearrange("p h (t n) -> p t h n", t=ST)
    den, nd = tiny(ST, 4), tiny(ST, 4)
    d = dve(lambda: nc.vector.tensor_scalar(nd, o4[:, :, :, P], -1.0, None, ALU.mult), outs[-1])
    d = dve(lambda: nc.vector.tensor_tensor(den, o4[:, :, :, P], nd, ALU.max), d)
    d = dve(lambda: nc.vector.tensor_tensor(den, den, gcol[:, R_ENM, :, :], ALU.max), d)
    d = dve(lambda: nc.vector.reciprocal(den, den), d)
    ymh = ym[:, :, 0:NC].rearrange("p t (h n) -> p t h n", n=P)
    for t in range(ST):
        h_here = dve(lambda t=t: nc.vector.tensor_tensor(
            ymh[:, t], o4[:, t, :, 0:P], den[:, t, :].unsqueeze(2).broadcast_to([P, 4, P]), ALU.mult), d)
    for b in range(8):
        bank_free[b] = [h_here]
    n = head_norm(ymh, 4, h_here, view(scr, 0, ST, 4, P))
    ym_here = dve(lambda: nc.vector.tensor_tensor(ym[:, :, 0:NC], ym[:, :, 0:NC], o_gate, ALU.mult), n, og)

    gq, gk, gv = cv[:, 4:8, :], cv[:, 8:12, :], cv[:, 12:16, :]
    qk8 = cv[:, 4:12, :]
    sq8 = view(scr, 3072, 8, S)
    e = act(lambda: nc.scalar.activation(sq8, qk8, ACT.Square), cv_here)
    for b in range(8):
        pe.wait(bank_free[b])
    for i in range(4):
        p = pe(mm(psum[:, i, :], c_("ones"), sq8[:, 2 * i:2 * i + 2, :].rearrange("p a s -> p (a s)")), e)
    ss = psum[:, 0:4, :].rearrange("p b (j s) -> p (b j) s", j=2)
    d = dve(lambda: nc.vector.tensor_scalar(sq8, ss, EPS, None, ALU.add), p)
    e = act(lambda: nc.scalar.activation(sq8, sq8, ACT.Sqrt), d)
    d = dve(lambda: nc.vector.reciprocal(sq8, sq8), e)
    d = dve(lambda: nc.vector.tensor_tensor(gk, gk, sq8[:, 4:8, :], ALU.mult), d)
    qk_n = dve(lambda: nc.vector.scalar_tensor_tensor(gq, gq, P ** -0.5, sq8[:, 0:4, :], ALU.mult, ALU.mult), d)

    dg = view(scr, 0, 8, P)
    at_ = view(scr, 1024, 8, P)
    attn = view(scr, 2048, 8, P)
    cm = [view(scr, 3072 + i * 1024, 8, P) for i in range(2)]
    xx = view(scr, 5120, 8, P)
    xt = view(scr, 6144, 8, P)
    yy = view(scr, 7168, 8, P)
    v_t = view(scr, 8192, 8, P)
    kd = view(scr, 9216, 4, P)
    v_new = view(scr, 9728, ST, 4, P)
    state = view(scr, 10752, 4, P)
    rhs = view(scr, 11264, ST, 4, P)
    o_raw = view(scr, 12288, ST, 4, P)

    def blk(j):
        return slice((j % 2) * P, (j % 2 + 1) * P)

    gu = view(scr, 1024, 4, ST, P)
    g_u = dve(lambda: nc.vector.tensor_tensor(
        gu, c_("upper").unsqueeze(1).unsqueeze(1).broadcast_to([P, 4, ST, P]),
        gcol[:, R_G, :, :].rearrange("p t h -> p h t").unsqueeze(3).broadcast_to([P, 4, ST, P]), ALU.mult),
        gcol_here, ym_here)
    gu_f = view(scr, 1024, 2, NC)
    p = pe.many([mm(psum[:, 4 + i, :], c_("after"), gu_f[:, i, :]) for i in range(2)], g_u)
    p2 = pe.many([row_bcast(R_B, h, psum[:, 6 + h // 2, (h % 2) * S:(h % 2 + 1) * S]) for h in range(4)], g_rows)
    e = act(lambda: nc.scalar.activation(dg, psum[:, 4:6, :].rearrange("p b (j n) -> p (b j) n", n=P), ACT.Exp),
            p, ym_here)
    dg_here = dve(lambda: nc.vector.tensor_tensor(
        dg, dg, c_("upper").unsqueeze(1).broadcast_to([P, 8, P]), ALU.mult), e)
    eg = tiny(4)
    p = pe(mm(psum[:, 4, 0:4], c_("upper"), gcol[:, R_G, 1, :]), e)
    eg_here = act(lambda: nc.scalar.activation(eg, psum[:, 4, 0:4], ACT.Exp), p)
    db = dve(lambda: nc.vector.tensor_tensor(
        at_, dg, psum[:, 6:8, :].rearrange("p b (j n) -> p (b j) n", n=P), ALU.mult), dg_here, p2)
    p = pe.many([mm(psum[:, j // 4, (j % 4) * P:(j % 4 + 1) * P], gk[:, j // 2, blk(j)], gk[:, j // 2, blk(j)])
                 for j in range(8)], qk_n)
    a_here = dve(lambda: nc.vector.tensor_tensor(
        at_, at_, psum[:, 0:2, :].rearrange("p b (j n) -> p (b j) n", n=P), ALU.mult), p, db)
    p = pe.many([mm(psum[:, 2 + j // 4, (j % 4) * P:(j % 4 + 1) * P], gk[:, j // 2, blk(j)], gq[:, j // 2, blk(j)])
                 for j in range(8)], qk_n)
    attn_here = dve(lambda: nc.vector.tensor_tensor(
        attn, dg, psum[:, 2:4, :].rearrange("p b (j n) -> p (b j) n", n=P), ALU.mult), p, dg_here)
    p = pe.many([tr(psum[:, 4 + j // 4, (j % 4) * P:(j % 4 + 1) * P], gv[:, j // 2, blk(j)]) for j in range(8)],
                db, cv_here, eg_here)
    vt_here = act(lambda: nc.scalar.activation(v_t, psum[:, 4:6, :].rearrange("p b (j n) -> p (b j) n", n=P),
                                               ACT.Copy), p, a_here)
    p = pe.many([tr(psum[:, 6, h * P:(h + 1) * P], gk[:, h, 0:P]) for h in range(4)], db)
    for h in range(4):
        kd_here = dve(lambda h=h: nc.vector.tensor_scalar(kd[:, h, :], psum[:, 6, h * P:(h + 1) * P],
                                                          dg[:, 2 * h, P - 1:P], None, ALU.mult), p)

    def level_mask(i):
        at, _ = CONST["levels"]
        return const[:, at + i * P:at + (i + 1) * P].unsqueeze(1).broadcast_to([P, 8, P])

    def b8(b):
        return psum[:, b:b + 2, :].rearrange("p b (j n) -> p (b j) n", n=P)

    cm_free = [[], []]
    id8 = ident.unsqueeze(1).broadcast_to([P, 8, P])
    m = pool(lambda: nc.gpsimd.tensor_tensor(cm[0], at_, level_mask(0), ALU.mult), a_here, qk_n)
    p = pe.many([tr(psum[:, j // 4, (j % 4) * P:(j % 4 + 1) * P], cm[0][:, j, :]) for j in range(8)], m)
    cm_free[0] = [p]
    x_ = dve(lambda: nc.vector.scalar_tensor_tensor(xx.rearrange("p j n -> p (j n)").rearrange(
        "p (j n) -> p j n", n=P), b8(0), -1.0, id8, ALU.mult, ALU.add), p)
    xt_ = dve(lambda: nc.vector.scalar_tensor_tensor(xt, cm[0], -1.0, id8, ALU.mult, ALU.add), m)
    cm_free[0].append(xt_)
    for i in range(1, len(LEVELS)):
        c = cm[i % 2]
        m = pool(lambda c=c, i=i: nc.gpsimd.tensor_tensor(c, at_, level_mask(i), ALU.mult), a_here, cm_free[i % 2])
        p = pe.many([mm(psum[:, j // 4, (j % 4) * P:(j % 4 + 1) * P], c[:, j, :], xx[:, j, :]) for j in range(8)],
                    m, x_)
        cm_free[i % 2] = [p]
        y_ = act(lambda: nc.scalar.activation(yy, b8(0), ACT.Copy), p)
        if i < len(LEVELS) - 1:
            p = pe.many([mm(psum[:, 2 + j // 4, (j % 4) * P:(j % 4 + 1) * P], xt[:, j, :], yy[:, j, :])
                         for j in range(8)], y_, xt_)
            x_ = dve(lambda: nc.vector.tensor_tensor(xx, xx, b8(2), ALU.subtract), p)
        p = pe.many([mm(psum[:, 4 + j // 4, (j % 4) * P:(j % 4 + 1) * P], yy[:, j, :], xt[:, j, :])
                     for j in range(8)], y_, xt_, vt_here)
        xt_ = dve(lambda: nc.vector.tensor_tensor(xt, xt, b8(4), ALU.subtract), p)

    r0 = [dve(lambda h=h: nc.vector.tensor_scalar(rhs[:, 0, h, :], v_t[:, 2 * h, :], gc(R_B, 0, h), None, ALU.mult),
              vt_here) for h in range(4)][-1]
    p = pe.many([mm(psum[:, 0, h * P:(h + 1) * P], xt[:, 2 * h, :], rhs[:, 0, h, :]) for h in range(4)], r0, xt_)
    n0 = act(lambda: nc.scalar.activation(v_new[:, 0], psum[:, 0, :].rearrange("p (h n) -> p h n", n=P), ACT.Copy), p)
    p = pe.many([mm(psum[:, 1, h * P:(h + 1) * P], kd[:, h, :], v_new[:, 0, h, :]) for h in range(4)], n0, kd_here)
    s0 = act(lambda: nc.scalar.activation(state, psum[:, 1, :].rearrange("p (h n) -> p h n", n=P), ACT.Copy), p)
    po = pe.many([mm(psum[:, 2, h * P:(h + 1) * P], attn[:, 2 * h, :], v_new[:, 0, h, :]) for h in range(4)],
                 attn_here)
    o0 = act(lambda: nc.scalar.activation(o_raw[:, 0], psum[:, 2, :].rearrange("p (h n) -> p h n", n=P), ACT.Copy), po)
    p = pe.many([mm(psum[:, 3, h * P:(h + 1) * P], gk[:, h, P:S], state[:, h, :]) for h in range(4)], s0,
                attn_here)
    for h in range(4):
        d = dve(lambda h=h: nc.vector.tensor_scalar(rhs[:, 1, h, :], psum[:, 3, h * P:(h + 1) * P], eg[:, h:h + 1],
                                                    None, ALU.mult), p)
        d = dve(lambda h=h: nc.vector.tensor_tensor(rhs[:, 1, h, :], v_t[:, 2 * h + 1, :], rhs[:, 1, h, :],
                                                    ALU.subtract), d)
        d = dve(lambda h=h: nc.vector.tensor_scalar(rhs[:, 1, h, :], rhs[:, 1, h, :], gc(R_B, 1, h), None, ALU.mult),
                d)
    p = pe.many([mm(psum[:, 6, h * P:(h + 1) * P], xt[:, 2 * h + 1, :], rhs[:, 1, h, :]) for h in range(4)], d,
                kd_here)
    n1 = act(lambda: nc.scalar.activation(v_new[:, 1], psum[:, 6, :].rearrange("p (h n) -> p h n", n=P), ACT.Copy), p)
    pq = pe.many([mm(psum[:, 7, h * P:(h + 1) * P], gq[:, h, P:S], state[:, h, :]) for h in range(4)], s0, db)
    for h in range(4):
        o1 = dve(lambda h=h: nc.vector.tensor_scalar(o_raw[:, 1, h, :], psum[:, 7, h * P:(h + 1) * P],
                                                     eg[:, h:h + 1], None, ALU.mult), pq)
    p = pe.many([mm(psum[:, 4, h * P:(h + 1) * P], attn[:, 2 * h + 1, :], v_new[:, 1, h, :]) for h in range(4)], n1)
    o1 = dve(lambda: nc.vector.tensor_tensor(o_raw[:, 1], o_raw[:, 1], psum[:, 4, :].rearrange(
        "p (h n) -> p h n", n=P), ALU.add), p, o1)
    for b in range(8):
        bank_free[b] = [o1, o0]
    n = head_norm(o_raw, 4, [o0, o1], view(scr, 0, ST, 4, P))
    ym_here = dve(lambda: nc.vector.tensor_tensor(
        ym[:, :, NC:2 * NC], o_raw.rearrange("p t h n -> p t (h n)"), g_gate, ALU.mult), n, gg)
    y_here = to_features(ym, ym_here, lambda k, src, t: [scaled(u2_t[:, k, :], src, col("m_norm", k), k, t)])
    x_here = mix_out(w_out, u2_t, y_here, 0)
    x_here = ffn(0, x_here)

    w_in, w_out = a["c_w_in_2"][0, :, :], a["c_w_out_2"][0, :, :]
    u_here = norm_features(x_here, [(u_t, "n10")], None)
    lbm, lbe, lbs, lb, one_lb = tiny(8), tiny(2, 8), tiny(8), tiny(8), tiny(8)
    lg = cols[:, ROW["lb"]:ROW["lb"] + 16].rearrange("p (l k) -> p l k", l=2)
    d = dve(lambda: nc.vector.tensor_tensor(lbm, lg[:, 0, :], lg[:, 1, :], ALU.max), cols_here)
    d = dve(lambda: nc.vector.tensor_tensor(lbe, lg, lbm.unsqueeze(1).broadcast_to([P, 2, 8]), ALU.subtract), d)
    e = act(lambda: nc.scalar.activation(lbe, lbe, ACT.Exp), d)
    d = dve(lambda: nc.vector.tensor_tensor(lbs, lbe[:, 0, :], lbe[:, 1, :], ALU.add), e)
    d = dve(lambda: nc.vector.reciprocal(lbs, lbs), d)
    d = dve(lambda: nc.vector.tensor_tensor(lbe, lbe, lbs.unsqueeze(1).broadcast_to([P, 2, 8]), ALU.mult), d)
    d = dve(lambda: nc.vector.tensor_tensor(lb, lbe[:, 0, :], lbe[:, 1, :], ALU.add), d)
    d = dve(lambda: nc.vector.tensor_tensor(lb, lb, lbe[:, 0, :], ALU.subtract), d)
    d = dve(lambda: nc.vector.tensor_scalar(lb, lb, 0.0, None, ALU.max), d)
    lb_here = dve(lambda: nc.vector.tensor_scalar(one_lb, lb, -1.0, 1.0, ALU.mult, ALU.add), d)

    cq = feat[:, 0:8, :]
    ck = feat[:, 8:16, :]
    fe = view(scr, 0, 8, S)
    l1 = view(scr, 2048, 8, S)
    gs = view(scr, 4096, 8, S)
    ci, cg = view(big, 0, ST, D), view(big, 2048, ST, D)
    fgot, qgot = [], []
    for c in range(2):
        slot, toks = chunk_features(w_in, D + c * NC, u_t, u_here)
        fgot += take_features(fe[:, 4 * c:4 * c + 4, :], slot, toks)
    for c in range(2):
        slot, toks = chunk_features(w_in, c * NC, u_t, u_here)
        qgot += take_features(cq[:, 4 * c:4 * c + 4, :], slot, toks)
    d = dve(lambda: nc.vector.tensor_scalar(fe, fe, -40.0, None, ALU.max), last_of(fgot))
    e = act(lambda: nc.scalar.activation(gs, fe, ACT.Exp, scale=-1.0), d)
    e = act(lambda: nc.scalar.activation(l1, gs, ACT.Ln, bias=1.0), e)
    d = dve(lambda: nc.vector.tensor_tensor(ck, fe, l1, ALU.add), e)
    for h in range(8):
        e2 = act(lambda h=h: nc.scalar.activation(fe[:, h, :], gs[:, h, :], ACT.Ln, bias=1.0, scale=lb[:, h:h + 1]),
                 d, lb_here)
    e3 = act(lambda: nc.scalar.activation(ck, ck, ACT.Exp, scale=-1.0), d)
    for h in range(8):
        k_here = dve(lambda h=h: nc.vector.tensor_scalar(ck[:, h, :], ck[:, h, :], one_lb[:, h:h + 1], None,
                                                         ALU.mult), e3, lb_here)
    d = dve(lambda: nc.vector.tensor_tensor(fe, fe, l1, ALU.subtract), e2)
    for h in range(8):
        for t in range(ST):
            ts = slice(t * P, (t + 1) * P)
            gs_here = dve(lambda h=h, ts=ts: nc.vector.tensor_tensor_scan(
                gs[:, h, ts], c_("ones"), fe[:, h, ts], 0.0, ALU.mult, ALU.add), d)
    q_here = act(lambda: nc.scalar.activation(cq, cq, ACT.Silu), last_of(qgot))
    q_here = dve(lambda: nc.vector.tensor_scalar(cq, cq, P ** -0.5, None, ALU.mult), q_here)
    vgot, ggot = [], []
    for c in range(2):
        slot, toks = chunk_tokens(w_in, 2 * D + c * NC, u_t, u_here)
        vgot += take_tokens(ci[:, :, c * NC:(c + 1) * NC], slot, toks)
    for c in range(2):
        slot, toks = chunk_tokens(w_in, 3 * D + c * NC, u_t, u_here)
        ggot += take_tokens(cg[:, :, c * NC:(c + 1) * NC], slot, toks)
    gg = silu_of(cg, cg, last_of(ggot))

    att = view(big, 4096, 16, P)
    att1 = view(big, 6144, 8, P)
    dec = [view(scr, i * 2048, 8 * S) for i in range(2)]
    prod = [view(scr, 6144 + i * 2048, 8 * S) for i in range(2)]
    gs_f, q_f, k_f = (v.rearrange("p h s -> p (h s)") for v in (gs, cq, ck))
    for b in range(8):
        pe.wait(bank_free[b])
    z0 = pool(lambda: nc.gpsimd.memset(att, 0.0), u_here)
    prod_free = [[], []]
    quad_free = [[], []]

    def masked(j0, mask, p, quad, *tokens):
        src = psum[:, quad:quad + 2, :].rearrange("p b (j n) -> p (b j) n", n=P)
        return dve(lambda: nc.vector.copy_predicated(
            att[:, j0:j0 + 8, :], mask.bitcast(I32).unsqueeze(1).broadcast_to([P, 8, P]), src), p, *tokens)

    step = 0
    for j0 in (0, 8):
        qd = 2 * (step % 4)
        p = pe.many([mm(psum[:, qd + j // 4, (j % 4) * P:(j % 4 + 1) * P], ck[:, (j0 + j) // 2, blk(j)],
                        cq[:, (j0 + j) // 2, blk(j)]) for j in range(8)], k_here, q_here, bank_free[qd])
        bank_free[qd] = [masked(j0, ident, p, qd, z0)]
        step += 1
    for i, n in enumerate(LEVELS):
        z = i % 2
        blocks = 8 * S // (2 * n)
        g4 = gs_f.rearrange("p (b m) -> p b m", m=2 * n)
        d4 = dec[z].rearrange("p (b m) -> p b m", m=2 * n)
        p4 = prod[z].rearrange("p (b m) -> p b m", m=2 * n)
        q4 = q_f.rearrange("p (b m) -> p b m", m=2 * n)
        k4 = k_f.rearrange("p (b m) -> p b m", m=2 * n)
        d = dve(lambda g4=g4, d4=d4, n=n, blocks=blocks: nc.vector.tensor_tensor(
            d4, g4, g4[:, :, n - 1:n].broadcast_to([P, blocks, 2 * n]), ALU.subtract), gs_here, prod_free[z])
        e1 = act(lambda d4=d4, n=n: nc.scalar.activation(d4[:, :, n:], d4[:, :, n:], ACT.Exp), d)
        e2 = act(lambda d4=d4, n=n: nc.scalar.activation(d4[:, :, 0:n], d4[:, :, 0:n], ACT.Exp, scale=-1.0), d)
        m1 = pool(lambda p4=p4, d4=d4, q4=q4, n=n: nc.gpsimd.tensor_tensor(p4[:, :, n:], d4[:, :, n:], q4[:, :, n:],
                                                                            ALU.mult), e1, q_here, prod_free[z])
        m2 = dve(lambda p4=p4, d4=d4, k4=k4, n=n: nc.vector.tensor_tensor(p4[:, :, 0:n], d4[:, :, 0:n],
                                                                           k4[:, :, 0:n], ALU.mult), e2, k_here)
        pr = view(prod[z], 0, 16, P)
        for j0 in (0, 8):
            qd = 2 * (step % 4)
            p = pe.many([mm(psum[:, qd + j // 4, (j % 4) * P:(j % 4 + 1) * P], pr[:, j0 + j, :], pr[:, j0 + j, :])
                         for j in range(8)], m1, m2, bank_free[qd])
            at, _ = CONST["levels"]
            bank_free[qd] = [masked(j0, const[:, at + i * P:at + (i + 1) * P], p, qd)]
            step += 1
        prod_free[z] = [p, m1, m2]
    dk, dq = view(dec[1], 0, 8, P), view(dec[1], 1024, 8, P)
    d = dve(lambda: nc.vector.tensor_tensor(dk, gs[:, :, P - 1:P].broadcast_to([P, 8, P]), gs[:, :, 0:P],
                                            ALU.subtract), prod_free[1])
    e1 = act(lambda: nc.scalar.activation(dk, dk, ACT.Exp), d)
    e2 = act(lambda: nc.scalar.activation(dq, gs[:, :, P:S], ACT.Exp), prod_free[1])
    d = dve(lambda: nc.vector.tensor_tensor(dk, dk, ck[:, :, 0:P], ALU.mult), e1)
    d = dve(lambda: nc.vector.tensor_tensor(dq, dq, cq[:, :, P:S], ALU.mult), e2)
    qd = 2 * (step % 4)
    p = pe.many([mm(psum[:, qd + h // 4, (h % 4) * P:(h % 4 + 1) * P], dk[:, h, :], dq[:, h, :]) for h in range(8)],
                d, bank_free[qd])
    a1_here = act(lambda: nc.scalar.activation(att1, psum[:, qd:qd + 2, :].rearrange("p b (j n) -> p (b j) n", n=P),
                                               ACT.Copy), p)
    att_here = [bank_free[q][0] for q in (0, 2, 4, 6)]
    co = ym if False else view(scr, 6144, ST, 8, P)
    for t in range(ST):
        bks = [(qd + 2 + 2 * t) % 8, (qd + 2 + 2 * t) % 8 + 1]
        ops = []
        for h in range(8):
            o = psum[:, bks[h // 4], (h % 4) * P:(h % 4 + 1) * P]
            vh = slice(h * P, (h + 1) * P)
            if t == 0:
                ops.append(mm(o, att[:, 2 * h, :], ci[:, 0, vh]))
            else:
                ops.append(mm(o, att1[:, h, :], ci[:, 0, vh], True, False))
                ops.append(mm(o, att[:, 2 * h + 1, :], ci[:, 1, vh], False, True))
        p = pe.many(ops, last_of(att_here), a1_here, last_of(vgot))
        src = psum[:, bks[0]:bks[0] + 2, :].rearrange("p b (j n) -> p (b j) n", n=P)
        if t == 0:
            c0_ = act(lambda src=src: nc.scalar.activation(co[:, 0], src, ACT.Copy), p)
        else:
            c1_ = dve(lambda src=src: nc.vector.tensor_copy(co[:, 1], src), p)
    for b in range(8):
        bank_free[b] = [a1_here, c0_, c1_]
    n = head_norm(co, 8, [c0_, c1_], view(scr, 0, ST, 8, P))
    y_here = dve(lambda: nc.vector.tensor_tensor(normed[:, :, :], co.rearrange("p t h n -> p t (h n)"), cg, ALU.mult),
                 n, gg)
    y_here = to_features(normed, y_here, lambda k, src, t: [scaled(u2_t[:, k, :], src, col("c_norm", k), k, t)])
    x_here = mix_out(w_out, u2_t, y_here, 2)
    x_here = ffn(1, x_here)

    out_done = g.counter("out_written")
    w = sp(lambda: nc.sync.dma_start(out.rearrange("b (t p) n -> p (b t) n", p=P), x_res[:, :, :]), x_here,
           inc=out_done, by=16)
    sp.wait(w)


_INS = ["x", "a_norm", "a_w_in", "a_w_out", "a_q_norm", "a_k_norm", "a_lq1", "a_lk1", "a_lq2", "a_lk2", "a_subln",
        "kv_norm", "w_kv", "b_norm", "b_w_in", "b_w_out", "norm_gains_2", "ab_w_in_2", "ab_conv_m_2",
        "ab_m_gate_bias_2", "ab_m_norm_2", "ab_conv_g_2", "ab_g_a_log_2", "ab_g_dt_bias_2", "ab_g_norm_2",
        "ab_w_out_2", "c_w_in_2", "c_lb_logits_2", "c_norm_2", "c_w_out_2", "ffn_w_up_2", "ffn_conv_w_2",
        "ffn_conv_b_2", "ffn_w_down_2"]


def kernel(**inputs):
    import concourse.bacc as bacc
    from concourse.bass_utils import run_bass_kernel_spmd

    nc = bacc.Bacc("TRN2", target_bir_lowering=False, num_devices=1)
    arrays, aps = {}, {}
    for name in _INS:
        arr = np.ascontiguousarray(inputs[name])
        arrays[f"in_{name}"] = arr
        aps[name] = nc.dram_tensor(f"in_{name}", arr.shape, mybir.dt.from_np(arr.dtype), kind="ExternalInput").ap()
    tab = constant_table()
    arrays["in_table"] = tab
    table = nc.dram_tensor("in_table", tab.shape, F32, kind="ExternalInput").ap()
    out = nc.dram_tensor("out_x", (1, S, D), F32, kind="ExternalOutput").ap()
    build(nc, aps, out, table)
    r = run_bass_kernel_spmd(nc, [arrays], core_ids=[0])
    return r.results[0]["out_x"]
```

```python
import math
import numpy as np
import concourse.bass as bass
from concourse import mybir

F32 = mybir.dt.float32
F32R = mybir.dt.float32r
I32 = mybir.dt.int32
ALU = mybir.AluOpType
ACT = mybir.ActivationFunctionType
AX = mybir.AxisListType

P = 128
D = 1024
S = 256
ST = S // P
KT = D // P
NC = 512
EPS = 1e-6
DA_HEADS, DA_DIM = 8, 64
SB_HEADS, SB_DIM = 16, 64
M_HEADS, G_HEADS, C_HEADS = 4, 4, 8
D_FF = 2816
FT = D_FF // P
LAMBDA_INIT = 0.8 - 0.6 * math.exp(-0.3 * 0)
ROPE_THETA, ROT = 500000.0, 16
LEVELS = [1, 2, 4, 8, 16, 32, 64]
NEG = -1.0e30
PK = 2
PIECE = PK * NC
RAW, SPLIT, AHEAD = 6, 3, 2
SCR = 13312

AB_MQK, AB_MV, AB_MO, AB_MG, AB_GQKV, AB_GG, AB_GAB = 0, 512, 1024, 1536, 1544, 3080, 3592

ROW = {}


def _rows():
    at = 0
    for name, n in [("a_norm", 8), ("kv_norm", 8), ("b_norm", 8), ("subln", 1), ("n00", 8), ("n02", 8),
                    ("n10", 8), ("n12", 8), ("m_norm", 4), ("g_norm", 4), ("c_norm", 8), ("lb", 16),
                    ("conv_m", 16)]:
        ROW[name] = at
        at += n
    assert at <= P
    ROW["conv_g"] = P
    for l in range(2):
        for i, name in enumerate(("tap0", "tap1", "tap2", "bias")):
            ROW[f"{name}_{l}"] = (2 + 2 * l + i // 2) * P + (i % 2) * 2 * FT


_rows()
ROW_COUNTS = [105, 48, 88, 88, 88, 88]

CONST = {}


def _const():
    at = 0
    for name, n in [("ident", P), ("upper", P), ("after", P), ("sb_neg", P), ("neg_ones", P), ("ones", P),
                    ("causal_neg", P), ("sb_mask", 3 * P), ("sb_bias", 3 * P), ("levels", P * len(LEVELS)),
                    ("cos", ST * ROT // 2), ("sin", ST * ROT // 2), ("select", 4 * P)]:
        CONST[name] = (at, n)
        at += n
    return at


N_CONST = _const()


def constant_table():
    t = np.zeros((P, N_CONST), np.float32)
    r, c = np.arange(P)[:, None], np.arange(P)[None, :]

    def put(name, value):
        at, n = CONST[name]
        t[:, at:at + n] = value

    put("ident", r == c)
    put("upper", r <= c)
    put("after", r > c)
    put("sb_neg", -(r >= c).astype(np.float32))
    put("neg_ones", -1.0)
    put("ones", 1.0)
    put("causal_neg", np.where(c <= r, 0.0, NEG))
    strict = (r < c).astype(np.float32)
    full = np.ones((P, P), np.float32)
    put("sb_mask", np.concatenate([strict, full, strict], 1))
    put("sb_bias", np.where(np.concatenate([strict, full, strict], 1) > 0, 0.0, NEG))
    put("levels", np.concatenate([(r // (2 * n) == c // (2 * n)) & (r // n % 2 == 0) & (c // n % 2 == 1)
                                  for n in LEVELS], 1))
    half = ROT // 2
    inv = np.power(np.float32(ROPE_THETA), -np.arange(half, dtype=np.float32) / np.float32(half))
    ang = np.arange(S, dtype=np.float32)[:, None] * inv.astype(np.float32)[None, :]
    for name, f in (("cos", np.cos), ("sin", np.sin)):
        put(name, f(ang).astype(np.float32).reshape(ST, P, half).transpose(1, 0, 2).reshape(P, -1))
    sel = np.zeros((P, 4, P), np.float32)
    for h in range(4):
        sel[h, h] = 1.0
    put("select", sel.reshape(P, -1))
    return t


class Count:

    def __init__(self, nc, name, all_counts):
        self.sem, self.name, self.a, self.b = nc.alloc_semaphore(name), name, 0, 0
        all_counts.append(self)

    def now(self):
        return (self, self.a, self.b)


def before(token):
    return (token[0], token[1] - token[2], token[2])


class Queue:

    def __init__(self, prog, eng, name):
        self.prog, self.eng, self.count, self.seen = prog, eng, Count(prog.nc, name, prog.counts), {}

    def wait(self, *tokens):
        for t in tokens:
            if t is None:
                continue
            if isinstance(t, list):
                self.wait(*t)
                continue
            c, a, b = t
            if b == 0 and a <= 0:
                continue
            if any(bb == b and aa >= a for aa, bb in self.seen.get(c, ())):
                continue
            self.seen.setdefault(c, []).append((a, b))
            if self.prog.dry:
                continue
            assert a >= 1, (c.name, a, b)
            self.eng.wait_ge(c.sem, a + self.prog.i * b if b else a)

    def __call__(self, make, *tokens, inc=None, by=1):
        self.wait(*tokens)
        c = inc or self.count
        if not self.prog.dry:
            make().then_inc(c.sem, by)
        c.a += by
        return c.now()

    def silent(self, make):
        if not self.prog.dry:
            make()

    def many(self, makes, *tokens, inc=None):
        self.wait(*tokens)
        c = inc or self.count
        if not self.prog.dry:
            for m in makes[:-1]:
                m()
            makes[-1]().then_inc(c.sem, 1)
        c.a += 1
        return c.now()


class Program:
    def __init__(self, nc):
        self.nc, self.counts, self.dry, self.i = nc, [], False, 0
        self.pe = Queue(self, nc.tensor, "pe_done")
        self.act = Queue(self, nc.scalar, "act_done")
        self.dve = Queue(self, nc.vector, "dve_done")
        self.pool = Queue(self, nc.gpsimd, "pool_done")
        self.sp = Queue(self, nc.sync, "sp_dma")
        self.queues = [self.pe, self.act, self.dve, self.pool, self.sp]

    def counter(self, name):
        return Count(self.nc, name, self.counts)

    def loop(self, n, body, state):
        start = [(c, c.a) for c in self.counts]
        seen = [{k: list(v) for k, v in q.seen.items()} for q in self.queues]
        self.dry = True
        end = body(0, state)
        self.dry = False
        step = {c: c.a - a for c, a in start}
        for c, a in start:
            c.a, c.b = a, step[c]
        for q, s in zip(self.queues, seen):
            q.seen = {k: list(v) for k, v in s.items()}
        state = {k: (t[0], t[1] - step[t[0]], step[t[0]]) for k, t in end.items()}
        with self.nc.Fori(0, n) as i:
            self.i = i
            body(i, state)
        self.i = 0
        for c, a in start:
            assert c.a == a + step[c]
            c.a, c.b = a + n * step[c], 0
        for q, s in zip(self.queues, seen):
            q.seen = s
        return {k: (t[0], t[0].a - (step[t[0]] - (t[1] - dict(start)[t[0]])), 0) for k, t in end.items()}


def build(nc, a, out, table):
    g = Program(nc)
    pe, act, dve, pool, sp = g.pe, g.act, g.dve, g.pool, g.sp

    def sb(name, *shape, dt=F32):
        return nc.alloc_sbuf_tensor(name, [P, *shape], dt)

    raw = [sb(f"raw{i}", PIECE) for i in range(RAW)]
    w_hi = [sb(f"w_hi{i}", PIECE, dt=F32R) for i in range(SPLIT)]
    w_lo = [sb(f"w_lo{i}", PIECE, dt=F32R) for i in range(SPLIT)]
    x_res = sb("x_res", ST, D)
    normed = sb("normed", ST, D)
    big = sb("big", 4 * ST * D)
    feat = sb("feat", 16, S)
    scr_at = nc.sbuf_base
    scr = sb("scr", SCR)

    def over_scr(name, at, *shape):
        return nc.alloc_sbuf_tensor_at(name, [P, *shape], F32R, offset=scr_at + 4 * at)

    u_t = (sb("u_hi", KT, S, dt=F32R), over_scr("u_lo", SCR - 2048, KT, S))
    u2_t = (sb("u2_hi", KT, S, dt=F32R), over_scr("u2_lo", SCR - 4096, KT, S))
    y_t = (u2_t[0], u_t[1])
    hid = [(over_scr(f"hid_hi{i}", 2048 + i * 2 * S, S), over_scr(f"hid_lo{i}", 2048 + (2 * i + 1) * S, S))
           for i in range(2)]
    const = sb("const", N_CONST)
    cols = sb("cols", 6 * P)
    post_gain = feat[:, 0:4, :].rearrange("p a b -> p (a b)")
    qk_gain = sb("qk_gain", 2, DA_DIM)
    lam_in = sb("lam_in", 4, DA_DIM)
    small = sb("small", 640)
    psum = nc.alloc_psum_tensor("psum", [P, 8, NC], F32)

    def c_(name, lo=0, hi=None):
        at, n = CONST[name]
        return const[:, at + lo:at + (n if hi is None else hi)]

    def col(name, j=0, tile=None):
        k = ROW[name]
        return cols[:, bass.ds(k + j, 1)] if not isinstance(j, int) else cols[:, k + j:k + j + 1]

    def view(buf, at, *dims):
        n = 1
        for d in dims:
            n *= d
        v = buf[:, at:at + n]
        if len(dims) == 1:
            return v
        names = "abcd"[:len(dims)]
        return v.rearrange(f"p ({' '.join(names)}) -> p {' '.join(names)}",
                           **{m: d for m, d in zip(names[1:], dims[1:])})

    small_at = [0]

    def tiny(*dims):
        n = int(np.prod(dims))
        v = view(small, small_at[0], *dims)
        small_at[0] += n
        assert small_at[0] <= 640
        return v

    ident = c_("ident")

    def mm(o, lhs, rhs, start=True, stop=True, loose=False):
        kw = {"skip_group_check": True} if loose else {}
        return lambda: nc.tensor.matmul(o, lhs, rhs, start=start, stop=stop, **kw)

    arrived = [g.counter(f"arrived{i}") for i in range(RAW)]
    hi_split = [g.counter(f"hi_split{i}") for i in range(RAW)]
    lo_split = [g.counter(f"lo_split{i}") for i in range(RAW)]
    used = [g.counter(f"used{i}") for i in range(SPLIT)]
    plan = []
    turn = {"prepared": 0, "taken": 0}
    bank_free = {b: [] for b in range(8)}

    def chunk_pieces(w, c0):
        w3 = w.rearrange("(k p) n -> p k n", p=P)
        return [(lambda r, k=k: [(view(r, 0, PK, NC), w3[:, k:k + PK, c0:c0 + NC])], PIECE)
                for k in range(0, KT, PK)]

    def prepare(cut=None):
        if cut is None:
            if not plan:
                return
            cut = plan.pop(0)
        cut, width = cut
        r, s = turn["prepared"] % RAW, turn["prepared"] % SPLIT
        turn["prepared"] += 1
        for dst, src in cut(raw[r]):
            here = sp(lambda: nc.sync.dma_start(dst, src), hi_split[r].now(), lo_split[r].now(),
                      inc=arrived[r], by=16)
        h = act(lambda: nc.scalar.activation(w_hi[s][:, 0:width], raw[r][:, 0:width], ACT.Copy),
                here, used[s].now(), inc=hi_split[r])
        dve(lambda: nc.vector.tensor_tensor(w_lo[s][:, 0:width], raw[r][:, 0:width],
                                            w_hi[s][:, 0:width].bitcast(F32), ALU.subtract), h, inc=lo_split[r])

    def take(following=None):
        r, s = turn["taken"] % RAW, turn["taken"] % SPLIT
        turn["taken"] += 1
        here = [hi_split[r].now(), lo_split[r].now()]
        prepare(following)
        return s, here

    def mm3(o, lhs, rhs, start, stop):
        (lh, ll), (rh, rl) = lhs, rhs
        return [mm(o, lh, rh, start, False, True), mm(o, lh, rl, False, False, True),
                mm(o, ll, rh, False, stop, True)]

    def tr(o, src, n=P):
        return lambda: nc.tensor.transpose(o, src, ident[0:n, 0:n])

    in_x, in_const, in_rows, in_gain, in_first = (g.counter(n) for n in
                                                  ("in_x", "in_const", "in_rows", "in_gain", "in_first"))

    def fetch(dst, src, inc):
        return act(lambda: nc.scalar.dma_start(dst, src), inc=inc, by=16)

    x_here = fetch(x_res[:, :, :], a["x"].rearrange("b (t p) n -> p (b t) n", p=P), in_x)
    const_here = fetch(const[:, :], table, in_const)
    rows = [view(scr, i * P, P) for i in range(6)]

    def as_rows(src):
        return src.rearrange("(r c) -> r c", c=P)

    def put_rows(name, src, n):
        k = ROW[name]
        fetch(rows[k // P][k % P:k % P + n, :], as_rows(src), in_rows)

    put_rows("a_norm", a["a_norm"][0, :], 8)
    put_rows("kv_norm", a["kv_norm"], 8)
    put_rows("b_norm", a["b_norm"][0, :], 8)
    put_rows("subln", a["a_subln"][0, :], 1)
    for l in range(2):
        put_rows(f"n{l}0", a["norm_gains_2"][l, 0, :], 8)
        put_rows(f"n{l}2", a["norm_gains_2"][l, 2, :], 8)
    put_rows("m_norm", a["ab_m_norm_2"][0, :], 4)
    put_rows("g_norm", a["ab_g_norm_2"][0, :], 4)
    put_rows("c_norm", a["c_norm_2"][0, :], 8)
    put_rows("lb", a["c_lb_logits_2"].rearrange("l c -> (l c)"), 16)
    put_rows("conv_m", a["ab_conv_m_2"][0, :, :].rearrange("t c -> (t c)"), 16)
    put_rows("conv_g", a["ab_conv_g_2"][0, :, :].rearrange("t c -> (t c)"), 48)
    for l in range(2):
        for tap in range(3):
            put_rows(f"tap{tap}_{l}", a["ffn_conv_w_2"][l, tap, :], 2 * FT)
        put_rows(f"bias_{l}", a["ffn_conv_b_2"][l, :], 2 * FT)
    rows_here = in_rows.now()

    def across(src):
        return src.rearrange("(a n) -> a n", a=1).broadcast_to([P, src.shape[0]])

    for i, n in enumerate(("a_q_norm", "a_k_norm")):
        fetch(qk_gain[:, i, :], across(a[n][0, :]), in_gain)
    for i, n in enumerate(("a_lq1", "a_lk1", "a_lq2", "a_lk2")):
        fetch(lam_in[:, i, :], across(a[n][0, :]), in_gain)
    gate_col = tiny(4)
    for i, src in enumerate((a["ab_m_gate_bias_2"][0, 0, :], a["ab_m_gate_bias_2"][0, 1, :],
                             a["ab_g_dt_bias_2"][0, :], a["ab_g_a_log_2"][0, :])):
        fetch(gate_col[0:4, i:i + 1], src.rearrange("(n a) -> n a", a=1), in_gain)
    gains_here = in_gain.now()

    def pipelined(n, stages, between=lambda step: None):
        for step in range(n + len(stages) - 1):
            for s in reversed(range(len(stages))):
                if 0 <= step - s < n:
                    stages[s](step - s)
            between(step)

    def chunk_steps(kind, src_t, ready, finish, pair):
        banks = [2 * pair, 2 * pair + 1]
        for i in range(KT // PK):
            s, here = take()
            hi, lo = (view(w[s], 0, PK, NC) for w in (w_hi, w_lo))
            toks = []
            for b in range(2):
                ops = []
                for kk in range(PK):
                    k = i * PK + kk
                    if kind == "tokens":
                        ops += mm3(psum[:, banks[b], :], [u[:, k, b * P:(b + 1) * P] for u in src_t],
                                   (hi[:, kk, :], lo[:, kk, :]), k == 0, k == KT - 1)
                    else:
                        for f in (2 * b, 2 * b + 1):
                            fs = slice(f * P, (f + 1) * P)
                            ops += mm3(psum[:, banks[b], (f % 2) * S:(f % 2 + 1) * S],
                                       (hi[:, kk, fs], lo[:, kk, fs]), [u[:, k, :] for u in src_t],
                                       k == 0 and f % 2 == 0, k == KT - 1)
                toks.append(pe.many(ops, here, ready, bank_free[banks[b]] if i == 0 else None,
                                    inc=used[s] if b == 1 else None))
            if i < KT // PK - 1:
                yield
        for b, t in zip(banks, finish(banks, toks)):
            bank_free[b] = t
        yield

    def chunk(kind, src_t, ready, finish, pair):
        for _ in chunk_steps(kind, src_t, ready, finish, pair):
            pass

    waiting = []

    def fill(n=1):
        while n and waiting:
            if next(waiting[0], "over") == "over":
                waiting.pop(0)
            else:
                n -= 1

    def rstd_of(sums, n, ready, dst):
        t = dve(lambda: nc.vector.tensor_scalar(dst, sums, 1.0 / n, EPS, ALU.mult, ALU.add), ready)
        t = act(lambda: nc.scalar.activation(dst, dst, ACT.Sqrt), t)
        return dve(lambda: nc.vector.reciprocal(dst, dst), t)

    def to_features(src, ready, dsts, *more, banks=(4, 5, 6, 7)):
        done = []
        for kk in range(KT // 2):
            b = banks[kk % len(banks)]
            t = pe.many([tr(psum[:, b, (j * ST + s) * P:(j * ST + s + 1) * P],
                            src[:, s, (2 * kk + j) * P:(2 * kk + j + 1) * P]) for j in range(2) for s in range(ST)],
                        ready, bank_free[b])
            parts = [(hi[:, 2 * kk + j, :], lo[:, 2 * kk + j, :], psum[:, b, j * S:(j + 1) * S],
                      column(2 * kk + j) if column else None) for (hi, lo), column in dsts for j in range(2)]
            for hi, lo, x, column in parts:
                e = act(lambda: nc.scalar.activation(hi, x, ACT.Copy, scale=1.0 if column is None else column),
                        t, *more)
            for hi, lo, x, column in parts:
                if column is None:
                    d = dve(lambda: nc.vector.tensor_tensor(lo, x, hi.bitcast(F32), ALU.subtract), e)
                else:
                    d = dve(lambda: nc.vector.scalar_tensor_tensor(lo, x, column, hi.bitcast(F32), ALU.mult,
                                                                   ALU.subtract), e)
            bank_free[b] = [d]
            done += [e, d]
        return last_of(done)

    def last_of(tokens):
        best = {}
        for c, v, b in tokens:
            if c not in best or best[c][1] < v:
                best[c] = (c, v, b)
        return list(best.values())

    def norm_features(ready, dsts, free):
        sums, rstd = tiny(ST), tiny(ST)
        sq = [act(lambda: nc.scalar.activation(normed[:, 0, :], x_res[:, 0, :], ACT.Square,
                                               accum_out=sums[:, 0:1]), ready, free),
              act(lambda: nc.scalar.activation(normed[:, 1, :], x_res[:, 1, :], ACT.Square,
                                               accum_out=sums[:, 1:2]))]
        r = rstd_of(sums, D, sq, rstd)
        n = [act(lambda: nc.scalar.activation(normed[:, 0, :], x_res[:, 0, :], ACT.Copy, scale=rstd[:, 0:1]), r),
             dve(lambda: nc.vector.tensor_scalar(normed[:, 1, :], x_res[:, 1, :], rstd[:, 1:2], None, ALU.mult), r)]

        return to_features(normed, n, [(dst, lambda k, gain=gain: col(gain, k)) for dst, gain in dsts], cols_here)

    def ffn_pieces(l, j):
        w_up = a["ffn_w_up_2"][l, :, :].rearrange("(k p) n -> p k n", p=P)

        def cut(first):
            return slice(first + j * P, first + (j + 1) * P) if isinstance(j, int) else bass.ds(j * P + first, P)

        kh = KT // 2
        up = [(lambda r, k=k: [(view(r, i * kh * P, kh, P), w_up[:, k:k + kh, cut(i * D_FF)]) for i in range(2)],
               2 * kh * P) for k in (0, kh)]
        down = (lambda r: [(r[:, 0:D], a["ffn_w_down_2"][l, cut(0), :])], D)
        return up + [down]

    def several(w, first, n):
        return [p for c in range(n) for p in chunk_pieces(w, first + c * NC)]

    def ffn_plan(l):
        t = [ffn_pieces(l, j) for j in range(FT)]
        return ([*t[0][:2], *t[1][:2], t[0][2], *t[2][:2]] +
                [t[FT - 3][2], *t[FT - 1][:2], t[FT - 2][2], t[FT - 1][2]])

    wa, wkv, wb = a["a_w_in"][0, :, :], a["w_kv"], a["b_w_in"][0, :, :]
    wab, wc = a["ab_w_in_2"][0, :, :], a["c_w_in_2"][0, :, :]
    plan += several(wa, 0, 8) + several(a["a_w_out"][0, :, :], 0, 2)
    plan += several(wkv, 0, 2) + several(wb, 0, 2) + several(wkv, D, 2) + several(wb, D, 2)
    plan += several(a["b_w_out"][0, :, :], 0, 2)
    plan += several(wab, AB_GQKV, 3) + several(wab, AB_MQK, 3) + several(wab, AB_GG, 1)
    plan += several(a["ab_w_out_2"][0, :, :], 0, 2) + ffn_plan(0)
    plan += several(wc, D, 2) + several(wc, 0, 2) + several(wc, 2 * D, 4)
    plan += several(a["c_w_out_2"][0, :, :], 0, 2) + ffn_plan(1)

    cols_toks = []
    for i, n in enumerate(ROW_COUNTS):
        t = pe(tr(psum[:, 4 + i % 4, 0:n], rows[i][0:n, :], n), const_here, rows_here, bank_free[4 + i % 4])
        v = dve(lambda i=i, n=n: nc.vector.tensor_copy(cols[:, i * P:i * P + n], psum[:, 4 + i % 4, 0:n]), t)
        bank_free[4 + i % 4] = [v]
        cols_toks.append(v)
    cols_here = cols_toks[-1]

    lam_p, lam_s, lam_e, neg_lam, sub_gain = tiny(2, DA_DIM), tiny(2), tiny(2), tiny(1), tiny(1)
    t = dve(lambda: nc.vector.tensor_tensor(lam_p, lam_in[:, 0:4:2, :], lam_in[:, 1:4:2, :], ALU.mult), gains_here)
    t = dve(lambda: nc.vector.tensor_reduce(lam_s, lam_p, AX.X, ALU.add), t)
    t = act(lambda: nc.scalar.activation(lam_e, lam_s, ACT.Exp), t)
    t = dve(lambda: nc.vector.tensor_tensor(neg_lam, lam_e[:, 1:2], lam_e[:, 0:1], ALU.subtract), t)
    t = dve(lambda: nc.vector.tensor_scalar(neg_lam, neg_lam, LAMBDA_INIT, None, ALU.subtract), t)
    lam_here = dve(lambda: nc.vector.tensor_scalar(sub_gain, col("subln"), 1.0 - LAMBDA_INIT, None, ALU.mult),
                   cols_here)

    u_here = norm_features(x_here, [(u_t, "a_norm")], None)
    proj = view(big, 0, ST, 4 * D)

    def empty_tokens(dst):
        def finish(banks, toks):
            e0 = act(lambda: nc.scalar.activation(dst[:, 0], psum[:, banks[0], :], ACT.Copy), toks[0])
            e1 = dve(lambda: nc.vector.tensor_copy(dst[:, 1], psum[:, banks[1], :]), toks[1])
            done.extend([e0, e1])
            return [e0], [e1]
        done = []
        return finish, done

    for _ in range(AHEAD):
        prepare()
    got = []
    for c in range(8):
        finish, done = empty_tokens(proj[:, :, c * NC:(c + 1) * NC])
        got.append(done)
        steps = chunk_steps("tokens", u_t, u_here, finish, 0 if c > 4 else c % 2)
        if c < 4:
            for _ in steps:
                pass
        else:
            waiting.append(steps)
    got_qk = [t for d in got[0:4] for t in d]

    groups = 2 * D // DA_DIM
    qk_sq = [view(scr, 6 * P + t * 2 * D, groups, DA_DIM) for t in range(ST)]
    qk_sum, qk_rstd = tiny(ST, groups), tiny(ST, groups)
    rope = view(scr, 6 * P + 4 * D, 4, groups, ROT // 2)
    qt, kt = feat[:, 0:8, :], feat[:, 8:16, :]
    qk_written = []
    for t in range(ST):
        qk = proj[:, t, 0:2 * D].rearrange("p (g d) -> p g d", d=DA_DIM)
        s = act(lambda t=t, qk=qk: nc.scalar.activation(qk_sq[t], qk, ACT.Square), got_qk)
        s = dve(lambda t=t: nc.vector.tensor_reduce(qk_sum[:, t, :], qk_sq[t], AX.X, ALU.add), s)
        r = rstd_of(qk_sum[:, t, :], DA_DIM, s, qk_rstd[:, t, :])
        n = dve(lambda t=t, qk=qk: nc.vector.tensor_tensor(
            qk, qk, qk_rstd[:, t, :].unsqueeze(2).broadcast_to([P, groups, DA_DIM]), ALU.mult), r)
        fill(2)
        for m in range(2):
            part = qk[:, m * 16:(m + 1) * 16, :]
            n2 = pool(lambda part=part, m=m: nc.gpsimd.tensor_tensor(
                part, part, qk_gain[:, m:m + 1, :].broadcast_to([P, 16, DA_DIM]), ALU.mult), n, gains_here)
        t1, t2 = qk[:, :, 0:8], qk[:, :, 8:16]
        cs = c_("cos", t * 8, t * 8 + 8).unsqueeze(1).broadcast_to([P, groups, 8])
        sn = c_("sin", t * 8, t * 8 + 8).unsqueeze(1).broadcast_to([P, groups, 8])
        for i, (x, w) in enumerate(((t1, cs), (t2, sn), (t1, sn), (t2, cs))):
            m = dve(lambda i=i, x=x, w=w: nc.vector.tensor_tensor(rope[:, i], x, w, ALU.mult), n2, const_here)
        r1 = dve(lambda: nc.vector.tensor_tensor(t1, rope[:, 0], rope[:, 1], ALU.subtract), m)
        r2 = dve(lambda: nc.vector.tensor_tensor(t2, rope[:, 2], rope[:, 3], ALU.add), m)
        fill(2)
        for q in range(4):
            b = 4 + q
            tt = pe.many([tr(psum[:, b, j * P:(j + 1) * P], proj[:, t, (4 * q + j) * P:(4 * q + j + 1) * P])
                          for j in range(4)], r2, n2, bank_free[b])
            dst = feat[:, 4 * q:4 * q + 4, t * P:(t + 1) * P]
            src = psum[:, b, :].rearrange("p (j t) -> p j t", j=4)
            if q % 2:
                w = act(lambda dst=dst, src=src: nc.scalar.activation(dst, src, ACT.Copy), tt)
            else:
                w = dve(lambda dst=dst, src=src: nc.vector.tensor_copy(dst, src), tt)
            bank_free[b] = [w]
            qk_written.append(w)
    qk_written = last_of(qk_written)

    o_tok = view(big, 0, ST, 4 * D)[:, :, 0:D]
    v_tok = proj[:, :, 2 * D:3 * D]
    v_here = got[4] + got[5]
    probs = [view(scr, 6 * P + i * 768, 2, 384) for i in range(2)]
    mixed = [view(scr, 6 * P + 1536 + i * 384, 384) for i in range(2)]
    mixed_t = [view(scr, 6 * P + 2304 + i * 384, 384) for i in range(2)]
    peak, denom, inv = [[tiny(2, 2) for _ in range(2)] for _ in range(3)]
    scale = DA_DIM ** -0.5
    bt, bo = psum[:, 2, :], psum[:, 3, :]
    sets = [psum[:, 4:6, :], psum[:, 6:8, :]]
    tile_cols = [slice(0, P), slice(P, 3 * P)]
    st = {}
    for b in range(2, 8):
        pe.wait(bank_free[b])

    def a_scores(h):
        for c in range(2):
            r = slice(64 * c, 64 * c + 64)
            sc = sets[h % 2]
            st["score", h] = pe.many([mm(sc[:, c, 0:P], qt[r, h, 0:P], kt[r, h, 0:P]),
                                      mm(sc[:, c, P:3 * P], qt[r, h, P:S], kt[r, h, 0:S])],
                                     qk_written, st.get(("prob", h - 2)))

    def a_softmax(h):
        z, sc = h % 2, sets[h % 2]
        diag = sc.rearrange("p c (j n) -> p c j n", n=P)[:, :, 0:3:2, :]
        m = dve(lambda: nc.vector.tensor_tensor(
            diag, diag, c_("causal_neg").unsqueeze(1).unsqueeze(1).broadcast_to([P, 2, 2, P]), ALU.add),
            st["score", h])
        for t in range(ST):
            m_ = dve(lambda t=t: nc.vector.tensor_reduce(peak[z][:, t, :], sc[:, :, tile_cols[t]], AX.X, ALU.max), m)
        m = dve(lambda: nc.vector.tensor_scalar(peak[z], peak[z], -scale, None, ALU.mult), m_)
        for t in range(ST):
            for c in range(2):
                st["prob", h] = act(lambda t=t, c=c: nc.scalar.activation(
                    probs[z][:, c, tile_cols[t]], sc[:, c, tile_cols[t]], ACT.Exp, bias=peak[z][:, t, c:c + 1],
                    scale=scale, accum_out=denom[z][:, t, c:c + 1]), m, st.get(("mix", h - 2)))

    def a_mix(h):
        z = h % 2
        i_ = dve(lambda: nc.vector.reciprocal(inv[z], denom[z]), st["prob", h])
        i_ = dve(lambda: nc.vector.tensor_scalar(inv[z][:, :, 1], inv[z][:, :, 1], neg_lam, None, ALU.mult),
                 i_, lam_here)
        x1 = [dve(lambda t=t: nc.vector.tensor_scalar(
            mixed[z][:, tile_cols[t]], probs[z][:, 0, tile_cols[t]], inv[z][:, t, 0:1], None, ALU.mult),
            i_, st.get(("turned", h - 2))) for t in range(ST)]
        for t in range(ST):
            st["mix", h] = dve(lambda t=t: nc.vector.scalar_tensor_tensor(
                mixed[z][:, tile_cols[t]], probs[z][:, 1, tile_cols[t]], inv[z][:, t, 1:2], mixed[z][:, tile_cols[t]],
                ALU.mult, ALU.add), x1[t])
        st["turned", h] = pe.many([tr(bt[:, j * P:(j + 1) * P], mixed[z][:, j * P:(j + 1) * P]) for j in range(3)],
                                  st["mix", h], st.get(("turn_out", h - 1)))
        st["turn_out", h] = act(lambda: nc.scalar.activation(mixed_t[z], bt[:, 0:3 * P], ACT.Copy), st["turned", h],
                                st.get(("value", h - 2)))

    def a_values(h):
        z, vh = h % 2, slice(h * P, (h + 1) * P)
        st["value", h] = pe.many([mm(bo[:, 0:P], mixed_t[z][:, 0:P], v_tok[:, 0, vh]),
                                  mm(bo[:, P:S], mixed_t[z][:, P:2 * P], v_tok[:, 0, vh], True, False),
                                  mm(bo[:, P:S], mixed_t[z][:, 2 * P:3 * P], v_tok[:, 1, vh], False, True)],
                                 st["turn_out", h], v_here, st.get(("out", h - 1)))
        st["out", h] = dve(lambda: nc.vector.tensor_copy(o_tok[:, :, vh], bo[:, 0:S].rearrange(
            "p (t n) -> p t n", t=ST)), st["value", h])

    pipelined(DA_HEADS, [a_scores, a_softmax, a_mix, a_values], lambda step: fill(1))
    fill(99)
    o_here = st["out", DA_HEADS - 1]
    for b in range(2, 8):
        bank_free[b] = [o_here]

    def silu_of(dst, src, *ready):
        return act(lambda: nc.scalar.activation(dst, src, ACT.Silu), *ready)

    def head_norm(o, heads, ready, sq):
        sums, rstd = tiny(ST, heads), tiny(ST, heads)
        s = pool(lambda: nc.gpsimd.tensor_tensor(sq, o, o, ALU.mult), ready)
        s = dve(lambda: nc.vector.tensor_reduce(sums, sq, AX.X, ALU.add), s)
        r = rstd_of(sums, P, s, rstd)
        return dve(lambda: nc.vector.tensor_tensor(
            o, o, rstd.unsqueeze(3).broadcast_to([P, ST, heads, P]), ALU.mult), r)

    gate = proj[:, :, 3 * D:4 * D]
    g_here = silu_of(gate, gate, got[6] + got[7])
    sq = view(scr, 6 * P + 4 * D, ST, 8, P)
    n = head_norm(o_tok.rearrange("p t (h n) -> p t h n", n=P), 8, o_here, sq)
    y = normed
    y_here = dve(lambda: nc.vector.tensor_tensor(y[:, :, :], o_tok, gate, ALU.mult), n, g_here)
    y_here = to_features(y, y_here, [(y_t, lambda k: sub_gain)], lam_here)

    def add_projection(src_t, ready):
        done = []
        for c in range(2):
            def finish(banks, toks, c=c):
                for t in range(ST):
                    dst = x_res[:, t, c * NC:(c + 1) * NC]
                    done.append(dve(lambda dst=dst, t=t: nc.vector.tensor_tensor(dst, psum[:, banks[t], :], dst,
                                                                                 ALU.add), toks[t]))
                return [done[-2]], [done[-1]]
            chunk("tokens", src_t, ready, finish, c)
        return done[-1]

    x_here = add_projection(y_t, y_here)

    u_here = norm_features(x_here, [(u_t, "kv_norm"), (u2_t, "b_norm")], None)

    def empty_features(dst, scale=1.0):
        def finish(banks, toks):
            src = [psum[:, b, :].rearrange("p (f t) -> p f t", f=2) for b in banks]
            e0 = act(lambda: nc.scalar.activation(dst[:, 0:2, :], src[0], ACT.Copy, scale=scale), toks[0])
            e1 = dve(lambda: nc.vector.tensor_scalar(dst[:, 2:4, :], src[1], scale, None, ALU.mult), toks[1])
            done.extend([e0, e1])
            return [e0], [e1]
        done = []
        return finish, done

    act.silent(lambda: nc.scalar.preload_act_table_set("natural_log_exp_and_others"))
    v_tok, gate = view(big, 0, ST, D), view(big, ST * D, ST, D)
    o_tok = view(big, 2 * ST * D, ST, D)
    qk_here, v_here, g_here = [], [], []
    for c in range(4):
        to = (kt if c < 2 else qt)[:, 4 * (c % 2):4 * (c % 2) + 4, :]
        finish, done = empty_features(to, 1.0 if c < 2 else SB_DIM ** -0.5)
        chunk("features", u_t if c < 2 else u2_t, u_here, finish, c % 2)
        qk_here += done
    for c in range(4):
        to = (v_tok if c < 2 else gate)[:, :, (c % 2) * NC:(c % 2 + 1) * NC]
        finish, done = empty_tokens(to)
        waiting.append(chunk_steps("tokens", u_t if c < 2 else u2_t, u_here, finish, 0))
        (v_here if c < 2 else g_here).append(done)

    soft = [view(scr, i * 768, 2, 384) for i in range(2)]
    work = [view(scr, 1536 + i * 768, 2, 384) for i in range(2)]
    stick = [view(scr, 3072 + i * 768, 2, 384) for i in range(2)]
    sb_z = [psum[:, 4 + 2 * i:6 + 2 * i, 0:384] for i in range(2)]
    st = {}
    for b in range(2, 8):
        pe.wait(bank_free[b])

    def pair_bcast(name):
        return c_(name).unsqueeze(1).broadcast_to([P, 2, 384])

    def b_scores(hp):
        for c in range(2):
            r = slice(64 * c, 64 * c + 64)
            zz = sb_z[hp % 2]
            st["score", hp] = pe.many([mm(zz[:, c, 0:S], kt[r, hp, 0:P], qt[r, hp, :], True, False),
                                       mm(zz[:, c, S:384], kt[r, hp, P:S], qt[r, hp, P:S], False, True)],
                                      qk_here, st.get(("log", hp - 2)))

    def b_softplus(hp):
        i, zz = hp % 2, sb_z[hp % 2]
        e = act(lambda: nc.scalar.activation(work[i], zz, ACT.Abs), st["score", hp], st.get(("soft", hp - 2)))
        e = act(lambda: nc.scalar.activation(work[i], work[i], ACT.Exp, scale=-1.0), e)
        e = act(lambda: nc.scalar.activation(work[i], work[i], ACT.Ln, bias=1.0), e)
        d = dve(lambda: nc.vector.scalar_tensor_tensor(soft[i], zz, 0.0, work[i], ALU.max, ALU.add), e,
                st.get(("sum", hp - 2)))
        st["soft", hp] = dve(lambda: nc.vector.tensor_tensor(soft[i], soft[i], pair_bcast("sb_mask"), ALU.mult), d)

    def b_sticks(hp):
        i, zz = hp % 2, sb_z[hp % 2]
        for c in range(2):
            st["sum", hp] = pe.many([mm(zz[:, c, :], c_("sb_neg"), soft[i][:, c, :], False, False, True),
                                     mm(zz[:, c, P:S], c_("neg_ones"), soft[i][:, c, S:384], False, True, True)],
                                    st["soft", hp])
        st["log", hp] = dve(lambda: nc.vector.scalar_tensor_tensor(
            stick[i], zz, 0.0, pair_bcast("sb_bias"), ALU.min, ALU.add), st["sum", hp], st.get(("value", hp - 2)))
        st["stick", hp] = act(lambda: nc.scalar.activation(stick[i], stick[i], ACT.Exp), st["log", hp])

    def b_values(hp):
        i, bank = hp % 2, 2 + hp % 2
        for c in range(2):
            vh = slice((2 * hp + c) * 64, (2 * hp + c) * 64 + 64)
            o0, o1 = (psum[:, bank, t * P + c * 64:t * P + c * 64 + 64] for t in range(ST))
            st["value", hp] = pe.many([mm(o0, stick[i][:, c, 0:P], v_tok[:, 0, vh]),
                                       mm(o1, stick[i][:, c, P:S], v_tok[:, 0, vh], True, False),
                                       mm(o1, stick[i][:, c, S:384], v_tok[:, 1, vh], False, True)],
                                      st["stick", hp], v_here[0], v_here[1], st.get(("out", hp - 2)))
        st["out", hp] = dve(lambda: nc.vector.tensor_copy(o_tok[:, :, hp * P:(hp + 1) * P], psum[:, bank, 0:S].rearrange(
            "p (t n) -> p t n", t=ST)), st["value", hp])

    pipelined(SB_HEADS // 2, [b_scores, b_softplus, b_sticks, b_values],
              lambda step: fill(4 if step < 2 else 1))
    fill(99)
    g_here = silu_of(gate, gate, g_here)
    y_here = [dve(lambda t=t: nc.vector.tensor_tensor(normed[:, t, :], o_tok[:, t, :], gate[:, t, :], ALU.mult),
                  st["out", SB_HEADS // 2 - 1], g_here) for t in range(ST)]
    for b in range(2, 8):
        bank_free[b] = [st["out", SB_HEADS // 2 - 1]]
    y_here = to_features(normed, y_here, [(y_t, None)])
    x_here = add_projection(y_t, y_here)

    mix = view(scr, 0, ST, D)

    gain_in = g.counter("gain_in")

    def fetch_gain(layer, which, ready):
        return pool(lambda: nc.gpsimd.dma_start(post_gain, across(a["norm_gains_2"][layer, which, :])), ready,
                    inc=gain_in, by=16)

    def mix_out(src_t, ready, layer):
        gain = fetch_gain(layer, 1, ready)
        got = []
        for c in range(2):
            finish, done = empty_tokens(mix[:, :, c * NC:(c + 1) * NC])
            chunk("tokens", src_t, ready, finish, c)
            got += done
        return add_normed(mix, last_of(got), gain, normed)

    def add_normed(src, ready, gain, sq):
        sums, rstd = tiny(ST), tiny(ST)
        for t in range(ST):
            s = act(lambda t=t: nc.scalar.activation(sq[:, t, :], src[:, t, :], ACT.Square,
                                                     accum_out=sums[:, t:t + 1]), ready)
        r = rstd_of(sums, D, s, rstd)
        for t in range(ST):
            d = dve(lambda t=t: nc.vector.scalar_tensor_tensor(
                sq[:, t, :], src[:, t, :], rstd[:, t:t + 1], post_gain, ALU.mult, ALU.mult), r, gain)
            d = dve(lambda t=t: nc.vector.tensor_tensor(x_res[:, t, :], x_res[:, t, :], sq[:, t, :], ALU.add), d)
        return d

    conv_done = [g.counter(f"conv{i}") for i in range(2)]
    hid_hi = [g.counter(f"hid_hi{i}") for i in range(2)]
    hid_lo = [g.counter(f"hid_lo{i}") for i in range(2)]
    down_used = [g.counter(f"down_used{i}") for i in range(2)]

    def ffn(l, x_here):
        u_here = norm_features(x_here, [(u_t, f"n{l}2")], None)
        gain = fetch_gain(l, 3, x_here)
        conv = [view(scr, i * 512, 2, S) for i in range(2)]
        silu = [view(scr, 1024 + i * S, S) for i in range(2)]
        prod = [view(scr, 1536 + i * S, S) for i in range(2)]
        for b in range(8):
            pe.wait(bank_free[b])

        def up(j, s, following):
            for part in range(2):
                w, here = take(following[part])
                hi, lo = (view(v[w], 0, 2, KT // 2, P) for v in (w_hi, w_lo))
                ops = []
                for i in range(2):
                    for kk in range(KT // 2):
                        k = part * KT // 2 + kk
                        ops += mm3(psum[:, s, i * S:(i + 1) * S], (hi[:, i, kk, :], lo[:, i, kk, :]),
                                   [u[:, k, :] for u in u_t], (i, k) == (0, 0), k == KT - 1)
                p = pe.many(ops, here, u_here, conv_done[s].now(), inc=used[w])
            for i in range(2):
                e = act(lambda i=i: nc.scalar.activation(
                    conv[s][:, i, :], psum[:, s, i * S:(i + 1) * S], ACT.Identity,
                    scale=col(f"tap2_{l}", j + i * FT), bias=col(f"bias_{l}", j + i * FT)),
                    p, hid_lo[s].now())
            d = [e, e]
            for tap in (1, 0):
                back = 2 - tap
                for i in range(2):
                    d[i] = dve(lambda i=i, back=back, tap=tap: nc.vector.scalar_tensor_tensor(
                        conv[s][:, i, back:], psum[:, s, i * S:(i + 1) * S - back], col(f"tap{tap}_{l}", j + i * FT),
                        conv[s][:, i, back:], ALU.mult, ALU.add), d[i],
                        inc=conv_done[s] if (tap, i) == (0, 1) else None)
            return d

        def gated(s, d):
            e = act(lambda: nc.scalar.activation(silu[s], conv[s][:, 0, :], ACT.Silu), d[0], hid_lo[s].now())
            m = dve(lambda: nc.vector.tensor_tensor(prod[s], silu[s], conv[s][:, 1, :], ALU.mult), e, d[1],
                    hid_hi[s].now())
            e = act(lambda: nc.scalar.activation(hid[s][0][:, :], prod[s], ACT.Copy), m, down_used[s].now(),
                    inc=hid_hi[s])
            dve(lambda: nc.vector.tensor_tensor(hid[s][1][:, :], prod[s], hid[s][0][:, :].bitcast(F32),
                                                ALU.subtract), e, down_used[s].now(), inc=hid_lo[s])

        def down(s, following=None, first=False, last=False):
            w, here = take(following)
            ops = [m for t in range(ST) for n in range(2)
                   for m in mm3(psum[:, 4 + 2 * t + n, :], [h[:, t * P:(t + 1) * P] for h in hid[s]],
                                [v[w][:, n * NC:(n + 1) * NC] for v in (w_hi, w_lo)], first, last)]
            pe.many(ops[:-1], here, hid_hi[s].now(), hid_lo[s].now(), inc=down_used[s])
            return pe.many(ops[-1:], inc=used[w])

        none = (None, None)
        gated(0, up(0, 0, none))
        d = up(1, 1, none)
        down(0, first=True)
        gated(1, d)

        def steps(i, st):
            for s in range(2):
                j = i * 2 + (2 + s)
                d = up(j, s, (ffn_pieces(l, j - 1)[2], ffn_pieces(l, j + 1)[0]))
                down(1 - s, ffn_pieces(l, j + 1)[1])
                gated(s, d)
            return {}

        g.loop(FT // 2 - 2, steps, {})
        for s in range(2):
            d = up(FT - 2 + s, s, none)
            down(1 - s)
            gated(s, d)
        done = down(1, last=True)
        for s in range(2):
            bank_free[s] = [conv_done[s].now()]
        out_ps = psum[:, 4:8, :].rearrange("p (t b) n -> p t (b n)", t=ST)
        x_here = add_normed(out_ps, done, gain, normed)
        for b in range(4, 8):
            bank_free[b] = [x_here]
        return x_here

    u_here = norm_features(x_here, [(u_t, "n00")], None)
    gate_w = view(feat[:, :, :].rearrange("p k s -> p (k s)"), 0, KT, 16)
    gw_here = g.counter("gate_weights")
    w3 = wab.rearrange("(k p) n -> p k n", p=P)
    pool(lambda: nc.gpsimd.dma_start(gate_w[:, :, 0:8], w3[:, :, AB_MG:AB_MG + 8]), x_here, inc=gw_here, by=16)
    gw = pool(lambda: nc.gpsimd.dma_start(gate_w[:, :, 8:16], w3[:, :, AB_GAB:AB_GAB + 8]), inc=gw_here, by=16)
    cv = feat
    v1 = view(big, 0, ST, M_HEADS, P + 1)
    o_gate = view(big, 1032, ST, NC)
    g_gate = view(big, 2056, ST, NC)
    ym = view(big, 3080, ST, D)
    g_tok = view(big, 5128, ST, 16)
    row = view(big, 5160, 11, S)
    t_ones = pool(lambda: nc.gpsimd.memset(v1[:, :, :, P:P + 1], 1.0), x_here)

    for t in range(ST):
        p = gates_taken = pe.many([mm(psum[:, 4, t * 16:(t + 1) * 16], u[:, k, t * P:(t + 1) * P].bitcast(F32),
                                      gate_w[:, k, :], (k, m) == (0, 0), (k, m) == (KT - 1, 1))
                                   for k in range(KT) for m, u in enumerate(u_t)], u_here, gw, bank_free[4])
    e = dve(lambda: nc.vector.tensor_copy(g_tok, psum[:, 4, 0:32].rearrange("p (t n) -> p t n", t=ST)), p)
    p = pe.many([tr(psum[0:4, 5 + kd // 2, (kd % 2) * S + t * P:(kd % 2) * S + (t + 1) * P],
                    g_tok[:, t, kd * 4:kd * 4 + 4]) for kd in range(4) for t in range(ST)],
                e, bank_free[5], bank_free[6])
    bank_free[4] = [e]
    gi, gf, ga, gb = (psum[0:4, 5 + kd // 2, (kd % 2) * S:(kd % 2 + 1) * S] for kd in range(4))
    R_A, R_ENM, R_G, R_B, R_C, R_T, R_U, R_V, R_I, R_X, R_Y = range(11)
    R_W = R_T

    def rw(k):
        return row[0:4, k, :]

    b15 = tiny(4)
    t0 = dve(lambda: nc.vector.tensor_scalar(b15[0:4, 0:2], gate_col[0:4, 0:2], 1.0 / 15.0, None, ALU.mult),
             gains_here)
    e1 = act(lambda: nc.scalar.activation(rw(R_I), gi, ACT.Tanh, scale=1.0 / 15.0, bias=b15[0:4, 0:1]), p, t0)
    e2 = act(lambda: nc.scalar.activation(rw(R_T), gf, ACT.Tanh, scale=1.0 / 15.0, bias=b15[0:4, 1:2]), p, t0)
    e = act(lambda: nc.scalar.activation(rw(R_T), rw(R_T), ACT.Exp, scale=-15.0), e2)
    e = act(lambda: nc.scalar.activation(rw(R_T), rw(R_T), ACT.Ln, bias=1.0), e)
    d = dve(lambda: nc.vector.tensor_tensor_scan(rw(R_U), c_("ones")[0:4, 0:1].broadcast_to([4, S]), rw(R_T), 0.0,
                                                 ALU.mult, ALU.add), e)
    d = dve(lambda: nc.vector.scalar_tensor_tensor(rw(R_A), rw(R_I), 15.0, rw(R_U), ALU.mult, ALU.add), d, e1)
    d = dve(lambda: nc.vector.tensor_tensor_scan(rw(R_C), c_("ones")[0:4, 0:1].broadcast_to([4, S]), rw(R_A), 0.0,
                                                 ALU.mult, ALU.max), d)
    d = dve(lambda: nc.vector.tensor_tensor(rw(R_ENM), rw(R_U), rw(R_C), ALU.subtract), d)
    m_rows = act(lambda: nc.scalar.activation(rw(R_ENM), rw(R_ENM), ACT.Exp), d)
    ea = tiny(1)
    e0 = act(lambda: nc.scalar.activation(ea[0:4, :], gate_col[0:4, 3:4], ACT.Exp), gains_here)
    d = ga_read = dve(lambda: nc.vector.tensor_scalar(rw(R_V), ga, gate_col[0:4, 2:3], None, ALU.add), p,
                      gains_here)
    e = act(lambda: nc.scalar.activation(rw(R_W), rw(R_V), ACT.Abs), d)
    e = act(lambda: nc.scalar.activation(rw(R_W), rw(R_W), ACT.Exp, scale=-1.0), e)
    d = dve(lambda: nc.vector.tensor_scalar(rw(R_X), rw(R_W), 2.0, None, ALU.add), e)
    d = dve(lambda: nc.vector.reciprocal(rw(R_X), rw(R_X)), d)
    d = dve(lambda: nc.vector.tensor_tensor(rw(R_W), rw(R_W), rw(R_X), ALU.mult), d)
    sq_here = d = dve(lambda: nc.vector.tensor_tensor(rw(R_X), rw(R_W), rw(R_W), ALU.mult), d)
    d = dve(lambda: nc.vector.tensor_scalar(rw(R_Y), rw(R_X), 1.0 / 17, None, ALU.mult), d)
    for k in (15, 13, 11, 9, 7, 5, 3):
        d = dve(lambda k=k: nc.vector.scalar_tensor_tensor(rw(R_Y), rw(R_Y), 1.0 / k, rw(R_X), ALU.add, ALU.mult), d)
    d = dve(lambda: nc.vector.scalar_tensor_tensor(rw(R_Y), rw(R_Y), 1.0, rw(R_W), ALU.add, ALU.mult), d)
    d = dve(lambda: nc.vector.tensor_scalar(rw(R_Y), rw(R_Y), 2.0, None, ALU.mult), d)
    d = dve(lambda: nc.vector.scalar_tensor_tensor(rw(R_V), rw(R_V), 0.0, rw(R_Y), ALU.max, ALU.add), d)
    g_row = dve(lambda: nc.vector.tensor_scalar(rw(R_G), rw(R_V), ea[0:4, :], -1.0, ALU.mult, ALU.mult), d, e0)
    e = act(lambda: nc.scalar.activation(rw(R_B), gb, ACT.Exp, scale=-1.0), p, ga_read)
    d = dve(lambda: nc.vector.tensor_scalar(rw(R_B), rw(R_B), 1.0, None, ALU.add), e)
    g_rows = dve(lambda: nc.vector.reciprocal(rw(R_B), rw(R_B)), d)
    bank_free[5] = bank_free[6] = [g_rows, e]
    gcol = tiny(4, ST, 4)
    p = pe.many([tr(psum[:, 4, (kd * ST + t) * 4:(kd * ST + t) * 4 + 4], row[0:4, kd, t * P:(t + 1) * P], 4)
                 for kd in range(4) for t in range(ST)], m_rows, g_rows, g_row, e, bank_free[4])
    gcol_here = dve(lambda: nc.vector.tensor_copy(gcol, psum[:, 4, 0:32].rearrange(
        "p (k t h) -> p k t h", k=4, t=ST)), p)
    bank_free[4] = [gcol_here]

    def gc(kind, t, h):
        return gcol[:, kind, t, h:h + 1]

    def conv_chunk(tiles, taps, stride, base, pair):
        def finish(banks, toks):
            out_t, last_tap = [], []
            srcs = [psum[:, banks[f // 2], (f % 2) * S:(f % 2 + 1) * S] for f in range(4)]
            for f, src in enumerate(srcs):
                dst = cv[:, tiles + f, :]
                last_tap.append(act(lambda dst=dst, src=src, f=f: nc.scalar.activation(
                    dst, src, ACT.Copy, scale=col(taps, 3 * stride + base + f)), toks[f // 2], gates_taken))
            out_t = [last_tap[f // 2 * 2 + 1] for f in range(4)]
            for tap in (2, 1, 0):
                back = 3 - tap
                for f, src in enumerate(srcs):
                    dst = cv[:, tiles + f, :]
                    out_t[f] = dve(lambda dst=dst, src=src, f=f, back=back, tap=tap: nc.vector.scalar_tensor_tensor(
                        dst[:, back:], src[:, 0:S - back], col(taps, tap * stride + base + f), dst[:, back:],
                        ALU.mult, ALU.add), out_t[f])
            done.append(silu_of(cv[:, tiles:tiles + 4, :], cv[:, tiles:tiles + 4, :], out_t[3]))
            return [out_t[1]], [out_t[3]]
        done = []
        return chunk_steps("features", u_t, u_here, finish, pair), done

    cv_here = []
    for n in range(3):
        steps, done = conv_chunk(4 + 4 * n, "conv_g", 12, 4 * n, n % 2)
        for _ in steps:
            pass
        cv_here += done
    steps, mqk_here = conv_chunk(0, "conv_m", 4, 0, 0)
    waiting.append(steps)

    def v1_finish(banks, toks):
        e = [act(lambda: nc.scalar.activation(v1[:, 0, :, 0:P], psum[:, banks[0], :].rearrange(
            "p (h n) -> p h n", n=P), ACT.Copy), toks[0]),
            dve(lambda: nc.vector.tensor_copy(v1[:, 1, :, 0:P], psum[:, banks[1], :].rearrange(
                "p (h n) -> p h n", n=P)), toks[1])]
        vs.extend(e)
        return [e[0]], [e[1]]

    vs = []
    waiting.append(chunk_steps("tokens", u_t, u_here, v1_finish, 0))
    finish, og = empty_tokens(o_gate)
    waiting.append(chunk_steps("tokens", u_t, u_here, finish, 0))
    finish, gg = empty_tokens(g_gate)
    waiting.append(chunk_steps("tokens", u_t, u_here, finish, 0))
    fill(99)
    og = act(lambda: nc.scalar.activation(o_gate, o_gate, ACT.Sigmoid), og)
    gg = silu_of(g_gate, g_gate, gg)

    def row_bcast(kind, h, dst):
        return mm(dst, c_("select", h * P, (h + 1) * P)[0:4, :], rw(kind))

    dm = view(scr, 0, M_HEADS, 384)
    st_ = view(scr, 1536, M_HEADS, 384)
    for b in range(8):
        pe.wait(bank_free[b])
    p = pe.many([row_bcast(R_C, h, psum[:, h // 2, (h % 2) * S:(h % 2 + 1) * S]) for h in range(4)], m_rows)
    for h in range(M_HEADS):
        cb = psum[:, h // 2, (h % 2) * S:(h % 2 + 1) * S]
        d = dve(lambda h=h, cb=cb: nc.vector.tensor_scalar(dm[:, h, 0:S], cb, gc(R_A, 0, h), 0.0,
                                                           ALU.subtract, ALU.max), p, gcol_here)
        d = dve(lambda h=h, cb=cb: nc.vector.tensor_scalar(dm[:, h, S:384], cb[:, P:S], gc(R_A, 1, h), 0.0,
                                                           ALU.subtract, ALU.max))
    e = act(lambda: nc.scalar.activation(dm, dm, ACT.Exp, scale=-1.0), d)
    dd = dm.rearrange("p h (j n) -> p h j n", n=P)[:, :, 0:3:2, :]
    msk = c_("upper").unsqueeze(1).unsqueeze(1).broadcast_to([P, 4, 2, P])
    dd_here = dve(lambda: nc.vector.tensor_tensor(dd, dd, msk, ALU.mult), e)
    outs = []
    for h in range(M_HEADS):
        r = slice(64 * (h % 2), 64 * (h % 2) + 64)
        sc = psum[:, 4 + h, 0:384]
        p = pe.many([mm(sc[:, 0:S], cv[r, 2 + h // 2, 0:P], cv[r, h // 2, :]),
                     mm(sc[:, S:384], cv[r, 2 + h // 2, P:S], cv[r, h // 2, P:S])], mqk_here)
        d = dve(lambda h=h, sc=sc: nc.vector.scalar_tensor_tensor(
            st_[:, h, :], sc, 64 ** -0.5, dm[:, h, :], ALU.mult, ALU.mult), p, dd_here)
        o = psum[:, h, 0:2 * (P + 1)]
        outs.append(pe.many([mm(o[:, 0:P + 1], st_[:, h, 0:P], v1[:, 0, h, :]),
                             mm(o[:, P + 1:], st_[:, h, P:S], v1[:, 0, h, :], True, False),
                             mm(o[:, P + 1:], st_[:, h, S:384], v1[:, 1, h, :], False, True)], d, vs, t_ones))
    o4 = psum[:, 0:4, 0:2 * (P + 1)].rearrange("p h (t n) -> p t h n", t=ST)
    den, nd = tiny(ST, 4), tiny(ST, 4)
    d = dve(lambda: nc.vector.tensor_scalar(nd, o4[:, :, :, P], -1.0, None, ALU.mult), outs[-1])
    d = dve(lambda: nc.vector.tensor_tensor(den, o4[:, :, :, P], nd, ALU.max), d)
    d = dve(lambda: nc.vector.tensor_tensor(den, den, gcol[:, R_ENM, :, :], ALU.max), d)
    d = dve(lambda: nc.vector.reciprocal(den, den), d)
    ymh = ym[:, :, 0:NC].rearrange("p t (h n) -> p t h n", n=P)
    for t in range(ST):
        h_here = dve(lambda t=t: nc.vector.tensor_tensor(
            ymh[:, t], o4[:, t, :, 0:P], den[:, t, :].unsqueeze(2).broadcast_to([P, 4, P]), ALU.mult), d)
    for b in range(8):
        bank_free[b] = [h_here]
    n = head_norm(ymh, 4, h_here, view(scr, 0, ST, 4, P))
    ym_here = dve(lambda: nc.vector.tensor_tensor(ym[:, :, 0:NC], ym[:, :, 0:NC], o_gate, ALU.mult), n, og)

    gq, gk, gv = cv[:, 4:8, :], cv[:, 8:12, :], cv[:, 12:16, :]
    qk8 = cv[:, 4:12, :]
    sq8 = view(scr, 3072, 8, S)
    e = act(lambda: nc.scalar.activation(sq8, qk8, ACT.Square), cv_here)
    for b in range(8):
        pe.wait(bank_free[b])
    for i in range(4):
        p = pe(mm(psum[:, i, :], c_("ones"), sq8[:, 2 * i:2 * i + 2, :].rearrange("p a s -> p (a s)")), e)
    ss = psum[:, 0:4, :].rearrange("p b (j s) -> p (b j) s", j=2)
    d = dve(lambda: nc.vector.tensor_scalar(sq8, ss, EPS, None, ALU.add), p)
    e = act(lambda: nc.scalar.activation(sq8, sq8, ACT.Sqrt), d)
    d = dve(lambda: nc.vector.reciprocal(sq8, sq8), e)
    d = dve(lambda: nc.vector.tensor_tensor(gk, gk, sq8[:, 4:8, :], ALU.mult), d)
    qk_n = dve(lambda: nc.vector.scalar_tensor_tensor(gq, gq, P ** -0.5, sq8[:, 0:4, :], ALU.mult, ALU.mult), d)

    dg = view(scr, 0, 8, P)
    at_ = view(scr, 1024, 8, P)
    attn = view(scr, 2048, 8, P)
    cm = [view(scr, 3072 + i * 1024, 8, P) for i in range(2)]
    xx = view(scr, 5120, 8, P)
    xt = view(scr, 6144, 8, P)
    yy = view(scr, 7168, 8, P)
    v_t = view(scr, 8192, 8, P)
    kd = view(scr, 9216, 4, P)
    v_new = view(scr, 9728, ST, 4, P)
    state = view(scr, 10752, 4, P)
    rhs = view(scr, 11264, ST, 4, P)
    o_raw = view(scr, 12288, ST, 4, P)

    def blk(j):
        return slice((j % 2) * P, (j % 2 + 1) * P)

    gu = view(scr, 1024, 4, ST, P)
    g_u = dve(lambda: nc.vector.tensor_tensor(
        gu, c_("upper").unsqueeze(1).unsqueeze(1).broadcast_to([P, 4, ST, P]),
        gcol[:, R_G, :, :].rearrange("p t h -> p h t").unsqueeze(3).broadcast_to([P, 4, ST, P]), ALU.mult),
        gcol_here, ym_here)
    gu_f = view(scr, 1024, 2, NC)
    p = pe.many([mm(psum[:, 4 + i, :], c_("after"), gu_f[:, i, :]) for i in range(2)], g_u)
    p2 = pe.many([row_bcast(R_B, h, psum[:, 6 + h // 2, (h % 2) * S:(h % 2 + 1) * S]) for h in range(4)], g_rows)
    e = act(lambda: nc.scalar.activation(dg, psum[:, 4:6, :].rearrange("p b (j n) -> p (b j) n", n=P), ACT.Exp),
            p, ym_here)
    dg_here = dve(lambda: nc.vector.tensor_tensor(
        dg, dg, c_("upper").unsqueeze(1).broadcast_to([P, 8, P]), ALU.mult), e)
    eg = tiny(4)
    p = pe(mm(psum[:, 4, 0:4], c_("upper"), gcol[:, R_G, 1, :]), e)
    eg_here = act(lambda: nc.scalar.activation(eg, psum[:, 4, 0:4], ACT.Exp), p)
    db = dve(lambda: nc.vector.tensor_tensor(
        at_, dg, psum[:, 6:8, :].rearrange("p b (j n) -> p (b j) n", n=P), ALU.mult), dg_here, p2)
    p = pe.many([mm(psum[:, j // 4, (j % 4) * P:(j % 4 + 1) * P], gk[:, j // 2, blk(j)], gk[:, j // 2, blk(j)])
                 for j in range(8)], qk_n)
    a_here = dve(lambda: nc.vector.tensor_tensor(
        at_, at_, psum[:, 0:2, :].rearrange("p b (j n) -> p (b j) n", n=P), ALU.mult), p, db)
    p = pe.many([mm(psum[:, 2 + j // 4, (j % 4) * P:(j % 4 + 1) * P], gk[:, j // 2, blk(j)], gq[:, j // 2, blk(j)])
                 for j in range(8)], qk_n)
    attn_here = dve(lambda: nc.vector.tensor_tensor(
        attn, dg, psum[:, 2:4, :].rearrange("p b (j n) -> p (b j) n", n=P), ALU.mult), p, dg_here)
    p = pe.many([tr(psum[:, 4 + j // 4, (j % 4) * P:(j % 4 + 1) * P], gv[:, j // 2, blk(j)]) for j in range(8)],
                db, cv_here, eg_here)
    vt_here = act(lambda: nc.scalar.activation(v_t, psum[:, 4:6, :].rearrange("p b (j n) -> p (b j) n", n=P),
                                               ACT.Copy), p, a_here)
    p = pe.many([tr(psum[:, 6, h * P:(h + 1) * P], gk[:, h, 0:P]) for h in range(4)], db)
    for h in range(4):
        kd_here = dve(lambda h=h: nc.vector.tensor_scalar(kd[:, h, :], psum[:, 6, h * P:(h + 1) * P],
                                                          dg[:, 2 * h, P - 1:P], None, ALU.mult), p)

    def level_mask(i):
        at, _ = CONST["levels"]
        return const[:, at + i * P:at + (i + 1) * P].unsqueeze(1).broadcast_to([P, 8, P])

    def b8(b):
        return psum[:, b:b + 2, :].rearrange("p b (j n) -> p (b j) n", n=P)

    cm_free = [[], []]
    id8 = ident.unsqueeze(1).broadcast_to([P, 8, P])
    m = pool(lambda: nc.gpsimd.tensor_tensor(cm[0], at_, level_mask(0), ALU.mult), a_here, qk_n)
    p = pe.many([tr(psum[:, j // 4, (j % 4) * P:(j % 4 + 1) * P], cm[0][:, j, :]) for j in range(8)], m)
    cm_free[0] = [p]
    x_ = dve(lambda: nc.vector.scalar_tensor_tensor(xx.rearrange("p j n -> p (j n)").rearrange(
        "p (j n) -> p j n", n=P), b8(0), -1.0, id8, ALU.mult, ALU.add), p)
    xt_ = dve(lambda: nc.vector.scalar_tensor_tensor(xt, cm[0], -1.0, id8, ALU.mult, ALU.add), m)
    cm_free[0].append(xt_)
    for i in range(1, len(LEVELS)):
        c = cm[i % 2]
        m = pool(lambda c=c, i=i: nc.gpsimd.tensor_tensor(c, at_, level_mask(i), ALU.mult), a_here, cm_free[i % 2])
        p = pe.many([mm(psum[:, j // 4, (j % 4) * P:(j % 4 + 1) * P], c[:, j, :], xx[:, j, :]) for j in range(8)],
                    m, x_)
        cm_free[i % 2] = [p]
        y_ = act(lambda: nc.scalar.activation(yy, b8(0), ACT.Copy), p)
        if i < len(LEVELS) - 1:
            p = pe.many([mm(psum[:, 2 + j // 4, (j % 4) * P:(j % 4 + 1) * P], xt[:, j, :], yy[:, j, :])
                         for j in range(8)], y_, xt_)
            x_ = dve(lambda: nc.vector.tensor_tensor(xx, xx, b8(2), ALU.subtract), p)
        p = pe.many([mm(psum[:, 4 + j // 4, (j % 4) * P:(j % 4 + 1) * P], yy[:, j, :], xt[:, j, :])
                     for j in range(8)], y_, xt_, vt_here)
        xt_ = dve(lambda: nc.vector.tensor_tensor(xt, xt, b8(4), ALU.subtract), p)

    r0 = [dve(lambda h=h: nc.vector.tensor_scalar(rhs[:, 0, h, :], v_t[:, 2 * h, :], gc(R_B, 0, h), None, ALU.mult),
              vt_here) for h in range(4)][-1]
    p = pe.many([mm(psum[:, 0, h * P:(h + 1) * P], xt[:, 2 * h, :], rhs[:, 0, h, :]) for h in range(4)], r0, xt_)
    n0 = act(lambda: nc.scalar.activation(v_new[:, 0], psum[:, 0, :].rearrange("p (h n) -> p h n", n=P), ACT.Copy), p)
    p = pe.many([mm(psum[:, 1, h * P:(h + 1) * P], kd[:, h, :], v_new[:, 0, h, :]) for h in range(4)], n0, kd_here)
    s0 = act(lambda: nc.scalar.activation(state, psum[:, 1, :].rearrange("p (h n) -> p h n", n=P), ACT.Copy), p)
    po = pe.many([mm(psum[:, 2, h * P:(h + 1) * P], attn[:, 2 * h, :], v_new[:, 0, h, :]) for h in range(4)],
                 attn_here)
    o0 = act(lambda: nc.scalar.activation(o_raw[:, 0], psum[:, 2, :].rearrange("p (h n) -> p h n", n=P), ACT.Copy), po)
    p = pe.many([mm(psum[:, 3, h * P:(h + 1) * P], gk[:, h, P:S], state[:, h, :]) for h in range(4)], s0,
                attn_here)
    for h in range(4):
        d = dve(lambda h=h: nc.vector.tensor_scalar(rhs[:, 1, h, :], psum[:, 3, h * P:(h + 1) * P], eg[:, h:h + 1],
                                                    None, ALU.mult), p)
        d = dve(lambda h=h: nc.vector.tensor_tensor(rhs[:, 1, h, :], v_t[:, 2 * h + 1, :], rhs[:, 1, h, :],
                                                    ALU.subtract), d)
        d = dve(lambda h=h: nc.vector.tensor_scalar(rhs[:, 1, h, :], rhs[:, 1, h, :], gc(R_B, 1, h), None, ALU.mult),
                d)
    p = pe.many([mm(psum[:, 6, h * P:(h + 1) * P], xt[:, 2 * h + 1, :], rhs[:, 1, h, :]) for h in range(4)], d,
                kd_here)
    n1 = act(lambda: nc.scalar.activation(v_new[:, 1], psum[:, 6, :].rearrange("p (h n) -> p h n", n=P), ACT.Copy), p)
    pq = pe.many([mm(psum[:, 7, h * P:(h + 1) * P], gq[:, h, P:S], state[:, h, :]) for h in range(4)], s0, db)
    for h in range(4):
        o1 = dve(lambda h=h: nc.vector.tensor_scalar(o_raw[:, 1, h, :], psum[:, 7, h * P:(h + 1) * P],
                                                     eg[:, h:h + 1], None, ALU.mult), pq)
    p = pe.many([mm(psum[:, 4, h * P:(h + 1) * P], attn[:, 2 * h + 1, :], v_new[:, 1, h, :]) for h in range(4)], n1)
    o1 = dve(lambda: nc.vector.tensor_tensor(o_raw[:, 1], o_raw[:, 1], psum[:, 4, :].rearrange(
        "p (h n) -> p h n", n=P), ALU.add), p, o1)
    for b in range(8):
        bank_free[b] = [o1, o0]
    n = head_norm(o_raw, 4, [o0, o1], view(scr, 0, ST, 4, P))
    ym_here = dve(lambda: nc.vector.tensor_tensor(
        ym[:, :, NC:2 * NC], o_raw.rearrange("p t h n -> p t (h n)"), g_gate, ALU.mult), n, gg)
    y_here = to_features(ym, ym_here, [(y_t, lambda k: col("m_norm", k))])
    x_here = mix_out(y_t, y_here, 0)
    x_here = ffn(0, x_here)

    u_here = norm_features(x_here, [(u_t, "n10")], None)
    lbm, lbe, lbs, lb, one_lb = tiny(8), tiny(2, 8), tiny(8), tiny(8), tiny(8)
    lg = cols[:, ROW["lb"]:ROW["lb"] + 16].rearrange("p (l k) -> p l k", l=2)
    d = dve(lambda: nc.vector.tensor_tensor(lbm, lg[:, 0, :], lg[:, 1, :], ALU.max), cols_here)
    d = dve(lambda: nc.vector.tensor_tensor(lbe, lg, lbm.unsqueeze(1).broadcast_to([P, 2, 8]), ALU.subtract), d)
    e = act(lambda: nc.scalar.activation(lbe, lbe, ACT.Exp), d)
    d = dve(lambda: nc.vector.tensor_tensor(lbs, lbe[:, 0, :], lbe[:, 1, :], ALU.add), e)
    d = dve(lambda: nc.vector.reciprocal(lbs, lbs), d)
    d = dve(lambda: nc.vector.tensor_tensor(lbe, lbe, lbs.unsqueeze(1).broadcast_to([P, 2, 8]), ALU.mult), d)
    d = dve(lambda: nc.vector.tensor_tensor(lb, lbe[:, 0, :], lbe[:, 1, :], ALU.add), d)
    d = dve(lambda: nc.vector.tensor_tensor(lb, lb, lbe[:, 0, :], ALU.subtract), d)
    d = dve(lambda: nc.vector.tensor_scalar(lb, lb, 0.0, None, ALU.max), d)
    lb_here = dve(lambda: nc.vector.tensor_scalar(one_lb, lb, -1.0, 1.0, ALU.mult, ALU.add), d)

    cq = feat[:, 0:8, :]
    ck = feat[:, 8:16, :]
    fe = view(scr, 0, 8, S)
    l1 = view(scr, 2048, 8, S)
    gs = view(scr, 4096, 8, S)
    ci, cg = view(big, 0, ST, D), view(big, 2048, ST, D)
    fgot, qgot = [], []
    for c in range(4):
        to, got = (fe, fgot) if c < 2 else (cq, qgot)
        finish, done = empty_features(to[:, 4 * (c % 2):4 * (c % 2) + 4, :])
        chunk("features", u_t, u_here, finish, c % 2)
        got += done
    vgot, ggot = [], []
    for c in range(4):
        to = (ci if c < 2 else cg)[:, :, (c % 2) * NC:(c % 2 + 1) * NC]
        finish, done = empty_tokens(to)
        waiting.append(chunk_steps("tokens", u_t, u_here, finish, 0))
        (vgot if c < 2 else ggot).append(done)
    d = dve(lambda: nc.vector.tensor_scalar(fe, fe, -40.0, None, ALU.max), last_of(fgot))
    e = act(lambda: nc.scalar.activation(gs, fe, ACT.Exp, scale=-1.0), d)
    e = act(lambda: nc.scalar.activation(l1, gs, ACT.Ln, bias=1.0), e)
    d = dve(lambda: nc.vector.tensor_tensor(ck, fe, l1, ALU.add), e)
    for h in range(8):
        e2 = act(lambda h=h: nc.scalar.activation(fe[:, h, :], gs[:, h, :], ACT.Ln, bias=1.0, scale=lb[:, h:h + 1]),
                 d, lb_here)
    e3 = act(lambda: nc.scalar.activation(ck, ck, ACT.Exp, scale=-1.0), d)
    for h in range(8):
        k_here = dve(lambda h=h: nc.vector.tensor_scalar(ck[:, h, :], ck[:, h, :], one_lb[:, h:h + 1], None,
                                                         ALU.mult), e3, lb_here)
    d = dve(lambda: nc.vector.tensor_tensor(fe, fe, l1, ALU.subtract), e2)
    for h in range(8):
        for t in range(ST):
            ts = slice(t * P, (t + 1) * P)
            gs_here = dve(lambda h=h, ts=ts: nc.vector.tensor_tensor_scan(
                gs[:, h, ts], c_("ones"), fe[:, h, ts], 0.0, ALU.mult, ALU.add), d)
    q_here = act(lambda: nc.scalar.activation(cq, cq, ACT.Silu), last_of(qgot))
    q_here = dve(lambda: nc.vector.tensor_scalar(cq, cq, P ** -0.5, None, ALU.mult), q_here)
    fill(99)
    gg = silu_of(cg, cg, ggot)

    att = view(big, 4096, 16, P)
    att1 = view(big, 6144, 8, P)
    dec = [view(scr, i * 2048, 8 * S) for i in range(2)]
    prod = [view(scr, 6144 + i * 2048, 8 * S) for i in range(2)]
    gs_f, q_f, k_f = (v.rearrange("p h s -> p (h s)") for v in (gs, cq, ck))
    for b in range(8):
        pe.wait(bank_free[b])
    z0 = pool(lambda: nc.gpsimd.memset(att, 0.0), u_here)
    prod_free = [[], []]
    quad_free = [[], []]

    def masked(j0, mask, p, quad, *tokens):
        src = psum[:, quad:quad + 2, :].rearrange("p b (j n) -> p (b j) n", n=P)
        return dve(lambda: nc.vector.copy_predicated(
            att[:, j0:j0 + 8, :], mask.bitcast(I32).unsqueeze(1).broadcast_to([P, 8, P]), src), p, *tokens)

    step = 0
    for j0 in (0, 8):
        qd = 2 * (step % 4)
        p = pe.many([mm(psum[:, qd + j // 4, (j % 4) * P:(j % 4 + 1) * P], ck[:, (j0 + j) // 2, blk(j)],
                        cq[:, (j0 + j) // 2, blk(j)]) for j in range(8)], k_here, q_here, bank_free[qd])
        bank_free[qd] = [masked(j0, ident, p, qd, z0)]
        step += 1
    for i, n in enumerate(LEVELS):
        z = i % 2
        blocks = 8 * S // (2 * n)
        g4 = gs_f.rearrange("p (b m) -> p b m", m=2 * n)
        d4 = dec[z].rearrange("p (b m) -> p b m", m=2 * n)
        p4 = prod[z].rearrange("p (b m) -> p b m", m=2 * n)
        q4 = q_f.rearrange("p (b m) -> p b m", m=2 * n)
        k4 = k_f.rearrange("p (b m) -> p b m", m=2 * n)
        d = dve(lambda g4=g4, d4=d4, n=n, blocks=blocks: nc.vector.tensor_tensor(
            d4, g4, g4[:, :, n - 1:n].broadcast_to([P, blocks, 2 * n]), ALU.subtract), gs_here, prod_free[z])
        e1 = act(lambda d4=d4, n=n: nc.scalar.activation(d4[:, :, n:], d4[:, :, n:], ACT.Exp), d)
        e2 = act(lambda d4=d4, n=n: nc.scalar.activation(d4[:, :, 0:n], d4[:, :, 0:n], ACT.Exp, scale=-1.0), d)
        m1 = pool(lambda p4=p4, d4=d4, q4=q4, n=n: nc.gpsimd.tensor_tensor(p4[:, :, n:], d4[:, :, n:], q4[:, :, n:],
                                                                            ALU.mult), e1, q_here, prod_free[z])
        m2 = dve(lambda p4=p4, d4=d4, k4=k4, n=n: nc.vector.tensor_tensor(p4[:, :, 0:n], d4[:, :, 0:n],
                                                                           k4[:, :, 0:n], ALU.mult), e2, k_here)
        pr = view(prod[z], 0, 16, P)
        for j0 in (0, 8):
            qd = 2 * (step % 4)
            p = pe.many([mm(psum[:, qd + j // 4, (j % 4) * P:(j % 4 + 1) * P], pr[:, j0 + j, :], pr[:, j0 + j, :])
                         for j in range(8)], m1, m2, bank_free[qd])
            at, _ = CONST["levels"]
            bank_free[qd] = [masked(j0, const[:, at + i * P:at + (i + 1) * P], p, qd)]
            step += 1
        prod_free[z] = [p, m1, m2]
    dk, dq = view(dec[1], 0, 8, P), view(dec[1], 1024, 8, P)
    d = dve(lambda: nc.vector.tensor_tensor(dk, gs[:, :, P - 1:P].broadcast_to([P, 8, P]), gs[:, :, 0:P],
                                            ALU.subtract), prod_free[1])
    e1 = act(lambda: nc.scalar.activation(dk, dk, ACT.Exp), d)
    e2 = act(lambda: nc.scalar.activation(dq, gs[:, :, P:S], ACT.Exp), prod_free[1])
    d = dve(lambda: nc.vector.tensor_tensor(dk, dk, ck[:, :, 0:P], ALU.mult), e1)
    d = dve(lambda: nc.vector.tensor_tensor(dq, dq, cq[:, :, P:S], ALU.mult), e2)
    qd = 2 * (step % 4)
    p = pe.many([mm(psum[:, qd + h // 4, (h % 4) * P:(h % 4 + 1) * P], dk[:, h, :], dq[:, h, :]) for h in range(8)],
                d, bank_free[qd])
    a1_here = act(lambda: nc.scalar.activation(att1, psum[:, qd:qd + 2, :].rearrange("p b (j n) -> p (b j) n", n=P),
                                               ACT.Copy), p)
    att_here = [bank_free[q][0] for q in (0, 2, 4, 6)]
    co = ym if False else view(scr, 6144, ST, 8, P)
    for t in range(ST):
        bks = [(qd + 2 + 2 * t) % 8, (qd + 2 + 2 * t) % 8 + 1]
        ops = []
        for h in range(8):
            o = psum[:, bks[h // 4], (h % 4) * P:(h % 4 + 1) * P]
            vh = slice(h * P, (h + 1) * P)
            if t == 0:
                ops.append(mm(o, att[:, 2 * h, :], ci[:, 0, vh]))
            else:
                ops.append(mm(o, att1[:, h, :], ci[:, 0, vh], True, False))
                ops.append(mm(o, att[:, 2 * h + 1, :], ci[:, 1, vh], False, True))
        p = pe.many(ops, last_of(att_here), a1_here, vgot)
        src = psum[:, bks[0]:bks[0] + 2, :].rearrange("p b (j n) -> p (b j) n", n=P)
        if t == 0:
            c0_ = act(lambda src=src: nc.scalar.activation(co[:, 0], src, ACT.Copy), p)
        else:
            c1_ = dve(lambda src=src: nc.vector.tensor_copy(co[:, 1], src), p)
    for b in range(8):
        bank_free[b] = [a1_here, c0_, c1_]
    n = head_norm(co, 8, [c0_, c1_], view(scr, 0, ST, 8, P))
    y_here = dve(lambda: nc.vector.tensor_tensor(normed[:, :, :], co.rearrange("p t h n -> p t (h n)"), cg, ALU.mult),
                 n, gg)
    y_here = to_features(normed, y_here, [(y_t, lambda k: col("c_norm", k))])
    x_here = mix_out(y_t, y_here, 1)
    x_here = ffn(1, x_here)

    out_done = g.counter("out_written")
    w = sp(lambda: nc.sync.dma_start(out.rearrange("b (t p) n -> p (b t) n", p=P), x_res[:, :, :]), x_here,
           inc=out_done, by=16)
    sp.wait(w)


_INS = ["x", "a_norm", "a_w_in", "a_w_out", "a_q_norm", "a_k_norm", "a_lq1", "a_lk1", "a_lq2", "a_lk2", "a_subln",
        "kv_norm", "w_kv", "b_norm", "b_w_in", "b_w_out", "norm_gains_2", "ab_w_in_2", "ab_conv_m_2",
        "ab_m_gate_bias_2", "ab_m_norm_2", "ab_conv_g_2", "ab_g_a_log_2", "ab_g_dt_bias_2", "ab_g_norm_2",
        "ab_w_out_2", "c_w_in_2", "c_lb_logits_2", "c_norm_2", "c_w_out_2", "ffn_w_up_2", "ffn_conv_w_2",
        "ffn_conv_b_2", "ffn_w_down_2"]


def kernel(**inputs):
    import concourse.bacc as bacc
    from concourse.bass_utils import run_bass_kernel_spmd

    nc = bacc.Bacc("TRN2", target_bir_lowering=False, num_devices=1)
    arrays, aps = {}, {}
    for name in _INS:
        arr = np.ascontiguousarray(inputs[name])
        arrays[f"in_{name}"] = arr
        aps[name] = nc.dram_tensor(f"in_{name}", arr.shape, mybir.dt.from_np(arr.dtype), kind="ExternalInput").ap()
    tab = constant_table()
    arrays["in_table"] = tab
    table = nc.dram_tensor("in_table", tab.shape, F32, kind="ExternalInput").ap()
    out = nc.dram_tensor("out_x", (1, S, D), F32, kind="ExternalOutput").ap()
    build(nc, aps, out, table)
    r = run_bass_kernel_spmd(nc, [arrays], core_ids=[0])
    return r.results[0]["out_x"]
```

```python
import math
import numpy as np
import concourse.bass as bass
from concourse import mybir

F32 = mybir.dt.float32
F32R = mybir.dt.float32r
I32 = mybir.dt.int32
ALU = mybir.AluOpType
ACT = mybir.ActivationFunctionType
AX = mybir.AxisListType

P = 128
D = 1024
S = 256
ST = S // P
KT = D // P
NC = 512
EPS = 1e-6
DA_HEADS, DA_DIM = 8, 64
SB_HEADS, SB_DIM = 16, 64
M_HEADS, G_HEADS, C_HEADS = 4, 4, 8
D_FF = 2816
FT = D_FF // P
LAMBDA_INIT = 0.8 - 0.6 * math.exp(-0.3 * 0)
ROPE_THETA, ROT = 500000.0, 16
LEVELS = [1, 2, 4, 8, 16, 32, 64]
NEG = -1.0e30
PK = 2
PIECE = PK * NC
RAW, SPLIT, AHEAD = 6, 3, 2
SCR = 13312

AB_MQK, AB_MV, AB_MO, AB_MG, AB_GQKV, AB_GG, AB_GAB = 0, 512, 1024, 1536, 1544, 3080, 3592

ROW = {}


def _rows():
    at = 0
    for name, n in [("a_norm", 8), ("kv_norm", 8), ("b_norm", 8), ("subln", 1), ("n00", 8), ("n02", 8),
                    ("n10", 8), ("n12", 8), ("m_norm", 4), ("g_norm", 4), ("c_norm", 8), ("lb", 16),
                    ("conv_m", 16)]:
        ROW[name] = at
        at += n
    assert at <= P
    ROW["conv_g"] = P
    for l in range(2):
        for i, name in enumerate(("tap0", "tap1", "tap2", "bias")):
            ROW[f"{name}_{l}"] = (2 + 2 * l + i // 2) * P + (i % 2) * 2 * FT


_rows()
ROW_COUNTS = [105, 48, 88, 88, 88, 88]

CONST = {}


def _const():
    at = 0
    for name, n in [("ident", P), ("upper", P), ("after", P), ("sb_neg", P), ("neg_ones", P), ("ones", P),
                    ("causal_neg", P), ("sb_mask", 3 * P), ("sb_bias", 3 * P), ("levels", P * len(LEVELS)),
                    ("cos", ST * ROT // 2), ("sin", ST * ROT // 2), ("select", 4 * P)]:
        CONST[name] = (at, n)
        at += n
    return at


N_CONST = _const()


def constant_table():
    t = np.zeros((P, N_CONST), np.float32)
    r, c = np.arange(P)[:, None], np.arange(P)[None, :]

    def put(name, value):
        at, n = CONST[name]
        t[:, at:at + n] = value

    put("ident", r == c)
    put("upper", r <= c)
    put("after", r > c)
    put("sb_neg", -(r >= c).astype(np.float32))
    put("neg_ones", -1.0)
    put("ones", 1.0)
    put("causal_neg", np.where(c <= r, 0.0, NEG))
    strict = (r < c).astype(np.float32)
    full = np.ones((P, P), np.float32)
    put("sb_mask", np.concatenate([strict, full, strict], 1))
    put("sb_bias", np.where(np.concatenate([strict, full, strict], 1) > 0, 0.0, NEG))
    put("levels", np.concatenate([(r // (2 * n) == c // (2 * n)) & (r // n % 2 == 0) & (c // n % 2 == 1)
                                  for n in LEVELS], 1))
    half = ROT // 2
    inv = np.power(np.float32(ROPE_THETA), -np.arange(half, dtype=np.float32) / np.float32(half))
    ang = np.arange(S, dtype=np.float32)[:, None] * inv.astype(np.float32)[None, :]
    for name, f in (("cos", np.cos), ("sin", np.sin)):
        put(name, f(ang).astype(np.float32).reshape(ST, P, half).transpose(1, 0, 2).reshape(P, -1))
    sel = np.zeros((P, 4, P), np.float32)
    for h in range(4):
        sel[h, h] = 1.0
    put("select", sel.reshape(P, -1))
    return t


class Count:

    def __init__(self, nc, name, all_counts):
        self.sem, self.name, self.a, self.b = nc.alloc_semaphore(name), name, 0, 0
        all_counts.append(self)

    def now(self):
        return (self, self.a, self.b)


def before(token):
    return (token[0], token[1] - token[2], token[2])


class Queue:

    def __init__(self, prog, eng, name):
        self.prog, self.eng, self.count, self.seen = prog, eng, Count(prog.nc, name, prog.counts), {}

    def wait(self, *tokens):
        for t in tokens:
            if t is None:
                continue
            if isinstance(t, list):
                self.wait(*t)
                continue
            c, a, b = t
            if b == 0 and a <= 0:
                continue
            if any(bb == b and aa >= a for aa, bb in self.seen.get(c, ())):
                continue
            self.seen.setdefault(c, []).append((a, b))
            if self.prog.dry:
                continue
            assert a >= 1, (c.name, a, b)
            self.eng.wait_ge(c.sem, a + self.prog.i * b if b else a)

    def __call__(self, make, *tokens, inc=None, by=1):
        self.wait(*tokens)
        c = inc or self.count
        if not self.prog.dry:
            make().then_inc(c.sem, by)
        c.a += by
        return c.now()

    def silent(self, make):
        if not self.prog.dry:
            make()

    def many(self, makes, *tokens, inc=None):
        self.wait(*tokens)
        c = inc or self.count
        if not self.prog.dry:
            for m in makes[:-1]:
                m()
            makes[-1]().then_inc(c.sem, 1)
        c.a += 1
        return c.now()


class Program:
    def __init__(self, nc):
        self.nc, self.counts, self.dry, self.i = nc, [], False, 0
        self.pe = Queue(self, nc.tensor, "pe_done")
        self.act = Queue(self, nc.scalar, "act_done")
        self.dve = Queue(self, nc.vector, "dve_done")
        self.pool = Queue(self, nc.gpsimd, "pool_done")
        self.sp = Queue(self, nc.sync, "sp_dma")
        self.queues = [self.pe, self.act, self.dve, self.pool, self.sp]

    def counter(self, name):
        return Count(self.nc, name, self.counts)

    def loop(self, n, body, state):
        start = [(c, c.a) for c in self.counts]
        seen = [{k: list(v) for k, v in q.seen.items()} for q in self.queues]
        self.dry = True
        end = body(0, state)
        self.dry = False
        step = {c: c.a - a for c, a in start}
        for c, a in start:
            c.a, c.b = a, step[c]
        for q, s in zip(self.queues, seen):
            q.seen = {k: list(v) for k, v in s.items()}
        state = {k: (t[0], t[1] - step[t[0]], step[t[0]]) for k, t in end.items()}
        with self.nc.Fori(0, n) as i:
            self.i = i
            body(i, state)
        self.i = 0
        for c, a in start:
            assert c.a == a + step[c]
            c.a, c.b = a + n * step[c], 0
        for q, s in zip(self.queues, seen):
            q.seen = s
        return {k: (t[0], t[0].a - (step[t[0]] - (t[1] - dict(start)[t[0]])), 0) for k, t in end.items()}


def build(nc, a, out, table):
    g = Program(nc)
    pe, act, dve, pool, sp = g.pe, g.act, g.dve, g.pool, g.sp

    def sb(name, *shape, dt=F32):
        return nc.alloc_sbuf_tensor(name, [P, *shape], dt)

    raw = [sb(f"raw{i}", PIECE) for i in range(RAW)]
    w_hi = [sb(f"w_hi{i}", PIECE, dt=F32R) for i in range(SPLIT)]
    w_lo = [sb(f"w_lo{i}", PIECE, dt=F32R) for i in range(SPLIT)]
    x_res = sb("x_res", ST, D)
    normed = sb("normed", ST, D)
    big = sb("big", 4 * ST * D)
    feat = sb("feat", 16, S)
    scr_at = nc.sbuf_base
    scr = sb("scr", SCR)

    def over_scr(name, at, *shape):
        return nc.alloc_sbuf_tensor_at(name, [P, *shape], F32R, offset=scr_at + 4 * at)

    u_t = (sb("u_hi", KT, S, dt=F32R), over_scr("u_lo", SCR - 2048, KT, S))
    u2_t = (sb("u2_hi", KT, S, dt=F32R), over_scr("u2_lo", SCR - 4096, KT, S))
    y_t = (u2_t[0], u_t[1])
    hid = [(over_scr(f"hid_hi{i}", 2048 + i * 2 * S, S), over_scr(f"hid_lo{i}", 2048 + (2 * i + 1) * S, S))
           for i in range(2)]
    const = sb("const", N_CONST)
    cols = sb("cols", 6 * P)
    post_gain = feat[:, 0:4, :].rearrange("p a b -> p (a b)")
    qk_gain = sb("qk_gain", 2, DA_DIM)
    lam_in = sb("lam_in", 4, DA_DIM)
    small = sb("small", 640)
    gate_w = sb("gate_w", KT, 16)
    psum = nc.alloc_psum_tensor("psum", [P, 8, NC], F32)

    def c_(name, lo=0, hi=None):
        at, n = CONST[name]
        return const[:, at + lo:at + (n if hi is None else hi)]

    def col(name, j=0, tile=None):
        k = ROW[name]
        return cols[:, bass.ds(k + j, 1)] if not isinstance(j, int) else cols[:, k + j:k + j + 1]

    def view(buf, at, *dims):
        n = 1
        for d in dims:
            n *= d
        v = buf[:, at:at + n]
        if len(dims) == 1:
            return v
        names = "abcd"[:len(dims)]
        return v.rearrange(f"p ({' '.join(names)}) -> p {' '.join(names)}",
                           **{m: d for m, d in zip(names[1:], dims[1:])})

    small_at = [0]

    def tiny(*dims):
        n = int(np.prod(dims))
        v = view(small, small_at[0], *dims)
        small_at[0] += n
        assert small_at[0] <= 640
        return v

    ident = c_("ident")

    def mm(o, lhs, rhs, start=True, stop=True, loose=False):
        kw = {"skip_group_check": True} if loose else {}
        return lambda: nc.tensor.matmul(o, lhs, rhs, start=start, stop=stop, **kw)

    arrived = [g.counter(f"arrived{i}") for i in range(RAW)]
    hi_split = [g.counter(f"hi_split{i}") for i in range(RAW)]
    lo_split = [g.counter(f"lo_split{i}") for i in range(RAW)]
    used = [g.counter(f"used{i}") for i in range(SPLIT)]
    plan = []
    turn = {"prepared": 0, "taken": 0}
    bank_free = {b: [] for b in range(8)}

    def chunk_pieces(w, c0):
        w3 = w.rearrange("(k p) n -> p k n", p=P)
        return [(lambda r, k=k: [(view(r, 0, PK, NC), w3[:, k:k + PK, c0:c0 + NC])], PIECE)
                for k in range(0, KT, PK)]

    def prepare(cut=None):
        if cut is None:
            if not plan:
                return
            cut = plan.pop(0)
        cut, width = cut
        r, s = turn["prepared"] % RAW, turn["prepared"] % SPLIT
        turn["prepared"] += 1
        for dst, src in cut(raw[r]):
            here = sp(lambda: nc.sync.dma_start(dst, src), hi_split[r].now(), lo_split[r].now(),
                      inc=arrived[r], by=16)
        h = act(lambda: nc.scalar.activation(w_hi[s][:, 0:width], raw[r][:, 0:width], ACT.Copy),
                here, used[s].now(), inc=hi_split[r])
        dve(lambda: nc.vector.tensor_tensor(w_lo[s][:, 0:width], raw[r][:, 0:width],
                                            w_hi[s][:, 0:width].bitcast(F32), ALU.subtract), h, inc=lo_split[r])

    def take(following=None):
        r, s = turn["taken"] % RAW, turn["taken"] % SPLIT
        turn["taken"] += 1
        here = [hi_split[r].now(), lo_split[r].now()]
        prepare(following)
        return s, here

    def mm3(o, lhs, rhs, start, stop):
        (lh, ll), (rh, rl) = lhs, rhs
        return [mm(o, lh, rh, start, False, True), mm(o, lh, rl, False, False, True),
                mm(o, ll, rh, False, stop, True)]

    def tr(o, src, n=P):
        return lambda: nc.tensor.transpose(o, src, ident[0:n, 0:n])

    in_const, in_rows, in_gain, in_first = (g.counter(n) for n in ("in_const", "in_rows", "in_gain", "in_first"))
    in_x = [g.counter(f"in_x{t}") for t in range(ST)]

    def fetch(dst, src, inc):
        return act(lambda: nc.scalar.dma_start(dst, src), inc=inc, by=16)

    rows = [view(scr, i * P, P) for i in range(6)]

    def as_rows(src):
        return src.rearrange("(r c) -> r c", c=P)

    x_here = [fetch(x_res[:, t, :], a["x"][0, t * P:(t + 1) * P, :], in_x[t]) for t in range(ST)]
    ident_here = fetch(const[:, 0:P], table[:, 0:P], in_first)
    first_here = fetch(rows[0][0:8, :], as_rows(a["a_norm"][0, :]), in_first)
    sp.wait(x_here)

    def pipelined(n, stages, between=lambda step: None):
        for step in range(n + len(stages) - 1):
            for s in reversed(range(len(stages))):
                if 0 <= step - s < n:
                    stages[s](step - s)
            between(step)

    def chunk_steps(kind, src_t, ready, finish, pair):
        banks = [2 * pair, 2 * pair + 1]
        for i in range(KT // PK):
            s, here = take()
            hi, lo = (view(w[s], 0, PK, NC) for w in (w_hi, w_lo))
            toks = []
            for b in range(2):
                ops = []
                for kk in range(PK):
                    k = i * PK + kk
                    if kind == "tokens":
                        ops += mm3(psum[:, banks[b], :], [u[:, k, b * P:(b + 1) * P] for u in src_t],
                                   (hi[:, kk, :], lo[:, kk, :]), k == 0, k == KT - 1)
                    else:
                        for f in (2 * b, 2 * b + 1):
                            fs = slice(f * P, (f + 1) * P)
                            ops += mm3(psum[:, banks[b], (f % 2) * S:(f % 2 + 1) * S],
                                       (hi[:, kk, fs], lo[:, kk, fs]), [u[:, k, :] for u in src_t],
                                       k == 0 and f % 2 == 0, k == KT - 1)
                toks.append(pe.many(ops, here, ready[i], bank_free[banks[b]] if i == 0 else None,
                                    inc=used[s] if b == 1 else None))
            if i < KT // PK - 1:
                yield
        for b, t in zip(banks, finish(banks, toks)):
            bank_free[b] = t
        yield

    def chunk(kind, src_t, ready, finish, pair):
        for _ in chunk_steps(kind, src_t, ready, finish, pair):
            pass

    waiting = []

    def fill(n=1):
        while n and waiting:
            if next(waiting[0], "over") == "over":
                waiting.pop(0)
            else:
                n -= 1

    def rstd_of(sums, n, ready, dst):
        t = dve(lambda: nc.vector.tensor_scalar(dst, sums, 1.0 / n, EPS, ALU.mult, ALU.add), ready)
        t = act(lambda: nc.scalar.activation(dst, dst, ACT.Sqrt), t)
        return dve(lambda: nc.vector.reciprocal(dst, dst), t)

    def to_features(src, ready, dsts, *more, banks=(4, 5, 6, 7)):
        done = []
        for kk in range(KT // 2):
            b = banks[kk % len(banks)]
            t = pe.many([tr(psum[:, b, (j * ST + s) * P:(j * ST + s + 1) * P],
                            src[:, s, (2 * kk + j) * P:(2 * kk + j + 1) * P]) for j in range(2) for s in range(ST)],
                        ready[kk] if len(ready) == KT // 2 else ready, bank_free[b])
            parts = [(hi[:, 2 * kk + j, :], lo[:, 2 * kk + j, :], psum[:, b, j * S:(j + 1) * S],
                      column(2 * kk + j) if column else None) for (hi, lo), column in dsts for j in range(2)]
            for hi, lo, x, column in parts:
                e = act(lambda: nc.scalar.activation(hi, x, ACT.Copy, scale=1.0 if column is None else column),
                        t, *more)
            for hi, lo, x, column in parts:
                if column is None:
                    d = dve(lambda: nc.vector.tensor_tensor(lo, x, hi.bitcast(F32), ALU.subtract), e)
                else:
                    d = dve(lambda: nc.vector.scalar_tensor_tensor(lo, x, column, hi.bitcast(F32), ALU.mult,
                                                                   ALU.subtract), e)
            bank_free[b] = [d]
            done.append([e, d])
        return done

    def last_of(tokens):
        best = {}
        for c, v, b in tokens:
            if c not in best or best[c][1] < v:
                best[c] = (c, v, b)
        return list(best.values())

    def norm_features(ready, dsts, gains=None):
        rstd = rstd_rows(x_res, ready, normed)
        n = []
        for c in range(2):
            cs = slice(c * NC, (c + 1) * NC)
            n.append([dve(lambda: nc.vector.tensor_scalar(normed[:, 0, cs], x_res[:, 0, cs], rstd[0][0], None,
                                                          ALU.mult), rstd[0][1]),
                      act(lambda: nc.scalar.activation(normed[:, 1, cs], x_res[:, 1, cs], ACT.Copy,
                                                       scale=rstd[1][0]), rstd[1][1])])
        return to_features(normed, [n[0], n[0], n[1], n[1]],
                           [(dst, lambda k, gain=gain: col(gain, k)) for dst, gain in dsts], gains)

    def rstd_rows(src, ready, junk):
        act.silent(lambda: nc.scalar.preload_act_table_set("sqrt_and_others"))
        found = []
        for t in range(ST):
            sums, rstd = tiny(1), tiny(1)
            s = act(lambda: nc.scalar.activation(junk[:, t, :], src[:, t, :], ACT.Square, accum_out=sums), ready[t])
            found.append((rstd, rstd_of(sums, D, s, rstd)))
        return found

    def ffn_pieces(l, j):
        w_up = a["ffn_w_up_2"][l, :, :].rearrange("(k p) n -> p k n", p=P)

        def cut(first):
            return slice(first + j * P, first + (j + 1) * P) if isinstance(j, int) else bass.ds(j * P + first, P)

        kh = KT // 2
        up = [(lambda r, k=k: [(view(r, i * kh * P, kh, P), w_up[:, k:k + kh, cut(i * D_FF)]) for i in range(2)],
               2 * kh * P) for k in (0, kh)]
        down = (lambda r: [(r[:, 0:D], a["ffn_w_down_2"][l, cut(0), :])], D)
        return up + [down]

    def several(w, first, n):
        return [p for c in range(n) for p in chunk_pieces(w, first + c * NC)]

    def ffn_plan(l):
        t = [ffn_pieces(l, j) for j in range(FT)]
        return ([*t[0][:2], *t[1][:2], t[0][2], *t[2][:2]] +
                [t[FT - 3][2], *t[FT - 1][:2], t[FT - 2][2], t[FT - 1][2]])

    wa, wkv, wb = a["a_w_in"][0, :, :], a["w_kv"], a["b_w_in"][0, :, :]
    wab, wc = a["ab_w_in_2"][0, :, :], a["c_w_in_2"][0, :, :]
    plan += several(wa, 0, 8) + several(a["a_w_out"][0, :, :], 0, 2)
    plan += several(wkv, 0, 2) + several(wb, 0, 2) + several(wkv, D, 2) + several(wb, D, 2)
    plan += several(a["b_w_out"][0, :, :], 0, 2)
    plan += several(wab, AB_GQKV, 3) + several(wab, AB_MQK, 3) + several(wab, AB_GG, 1)
    plan += several(a["ab_w_out_2"][0, :, :], 0, 2) + ffn_plan(0)
    plan += several(wc, D, 2) + several(wc, 0, 2) + several(wc, 2 * D, 4)
    plan += several(a["c_w_out_2"][0, :, :], 0, 2) + ffn_plan(1)

    t = pe(tr(psum[:, 0, 0:8], rows[0][0:8, :], 8), first_here)
    first_cols_here = dve(lambda: nc.vector.tensor_copy(cols[:, 0:8], psum[:, 0, 0:8]), t)
    bank_free[0] = [first_cols_here]
    u_here = norm_features(x_here, [(u_t, "a_norm")], first_cols_here)
    for _ in range(AHEAD):
        prepare()

    gw_here = g.counter("gate_weights")
    w3 = wab.rearrange("(k p) n -> p k n", p=P)
    pool(lambda: nc.gpsimd.dma_start(gate_w[:, :, 0:8], w3[:, :, AB_MG:AB_MG + 8]), x_here, inc=gw_here, by=16)
    gw = pool(lambda: nc.gpsimd.dma_start(gate_w[:, :, 8:16], w3[:, :, AB_GAB:AB_GAB + 8]), inc=gw_here, by=16)
    const_here = fetch(const[:, P:], table[:, P:], in_const)
    def put_rows(name, src, n):
        k = ROW[name]
        fetch(rows[k // P][k % P:k % P + n, :], as_rows(src), in_rows)

    put_rows("kv_norm", a["kv_norm"], 8)
    put_rows("b_norm", a["b_norm"][0, :], 8)
    put_rows("subln", a["a_subln"][0, :], 1)
    for l in range(2):
        put_rows(f"n{l}0", a["norm_gains_2"][l, 0, :], 8)
        put_rows(f"n{l}2", a["norm_gains_2"][l, 2, :], 8)
    put_rows("m_norm", a["ab_m_norm_2"][0, :], 4)
    put_rows("g_norm", a["ab_g_norm_2"][0, :], 4)
    put_rows("c_norm", a["c_norm_2"][0, :], 8)
    put_rows("lb", a["c_lb_logits_2"].rearrange("l c -> (l c)"), 16)
    put_rows("conv_m", a["ab_conv_m_2"][0, :, :].rearrange("t c -> (t c)"), 16)
    put_rows("conv_g", a["ab_conv_g_2"][0, :, :].rearrange("t c -> (t c)"), 48)
    for l in range(2):
        for tap in range(3):
            put_rows(f"tap{tap}_{l}", a["ffn_conv_w_2"][l, tap, :], 2 * FT)
        put_rows(f"bias_{l}", a["ffn_conv_b_2"][l, :], 2 * FT)
    rows_here = in_rows.now()

    def across(src):
        return src.rearrange("(a n) -> a n", a=1).broadcast_to([P, src.shape[0]])

    for i, n in enumerate(("a_q_norm", "a_k_norm")):
        fetch(qk_gain[:, i, :], across(a[n][0, :]), in_gain)
    for i, n in enumerate(("a_lq1", "a_lk1", "a_lq2", "a_lk2")):
        fetch(lam_in[:, i, :], across(a[n][0, :]), in_gain)
    gate_col = tiny(4)
    for i, src in enumerate((a["ab_m_gate_bias_2"][0, 0, :], a["ab_m_gate_bias_2"][0, 1, :],
                             a["ab_g_dt_bias_2"][0, :], a["ab_g_a_log_2"][0, :])):
        fetch(gate_col[0:4, i:i + 1], src.rearrange("(n a) -> n a", a=1), in_gain)
    gains_here = in_gain.now()

    proj = view(big, 0, ST, 4 * D)

    def empty_tokens(dst):
        def finish(banks, toks):
            e0 = act(lambda: nc.scalar.activation(dst[:, 0], psum[:, banks[0], :], ACT.Copy), toks[0])
            e1 = dve(lambda: nc.vector.tensor_copy(dst[:, 1], psum[:, banks[1], :]), toks[1])
            done.extend([e0, e1])
            return [e0], [e1]
        done = []
        return finish, done

    got = []
    for c in range(8):
        finish, done = empty_tokens(proj[:, :, c * NC:(c + 1) * NC])
        got.append(done)
        steps = chunk_steps("tokens", u_t, u_here, finish, 0 if c > 4 else c % 2)
        if c < 4:
            for _ in steps:
                pass
        else:
            waiting.append(steps)
    cols_toks = []
    for i, n in enumerate(ROW_COUNTS):
        t = pe(tr(psum[:, 4 + i % 4, 0:n], rows[i][0:n, :], n), const_here, rows_here, bank_free[4 + i % 4])
        v = dve(lambda i=i, n=n: nc.vector.tensor_copy(
            cols[:, i * P + (8 if i == 0 else 0):i * P + n], psum[:, 4 + i % 4, (8 if i == 0 else 0):n]), t)
        bank_free[4 + i % 4] = [v]
        cols_toks.append(v)
    cols_here = cols_toks[-1]

    lam_p, lam_s, lam_e, neg_lam, sub_gain = tiny(2, DA_DIM), tiny(2), tiny(2), tiny(1), tiny(1)
    t = dve(lambda: nc.vector.tensor_tensor(lam_p, lam_in[:, 0:4:2, :], lam_in[:, 1:4:2, :], ALU.mult), gains_here)
    t = dve(lambda: nc.vector.tensor_reduce(lam_s, lam_p, AX.X, ALU.add), t)
    t = act(lambda: nc.scalar.activation(lam_e, lam_s, ACT.Exp), t)
    t = dve(lambda: nc.vector.tensor_tensor(neg_lam, lam_e[:, 1:2], lam_e[:, 0:1], ALU.subtract), t)
    t = dve(lambda: nc.vector.tensor_scalar(neg_lam, neg_lam, LAMBDA_INIT, None, ALU.subtract), t)
    lam_here = dve(lambda: nc.vector.tensor_scalar(sub_gain, col("subln"), 1.0 - LAMBDA_INIT, None, ALU.mult),
                   cols_here)

    got_qk = [t for d in got[0:4] for t in d]

    groups = 2 * D // DA_DIM
    qk_sq = [view(scr, 6 * P + t * 2 * D, groups, DA_DIM) for t in range(ST)]
    qk_sum, qk_rstd = tiny(ST, groups), tiny(ST, groups)
    rope = view(scr, 6 * P + 4 * D, 4, groups, ROT // 2)
    qt, kt = feat[:, 0:8, :], feat[:, 8:16, :]
    qk_written = []
    for t in range(ST):
        qk = proj[:, t, 0:2 * D].rearrange("p (g d) -> p g d", d=DA_DIM)
        s = act(lambda t=t, qk=qk: nc.scalar.activation(qk_sq[t], qk, ACT.Square), got_qk)
        s = dve(lambda t=t: nc.vector.tensor_reduce(qk_sum[:, t, :], qk_sq[t], AX.X, ALU.add), s)
        r = rstd_of(qk_sum[:, t, :], DA_DIM, s, qk_rstd[:, t, :])
        n = dve(lambda t=t, qk=qk: nc.vector.tensor_tensor(
            qk, qk, qk_rstd[:, t, :].unsqueeze(2).broadcast_to([P, groups, DA_DIM]), ALU.mult), r)
        fill(2)
        for m in range(2):
            part = qk[:, m * 16:(m + 1) * 16, :]
            n2 = pool(lambda part=part, m=m: nc.gpsimd.tensor_tensor(
                part, part, qk_gain[:, m:m + 1, :].broadcast_to([P, 16, DA_DIM]), ALU.mult), n, gains_here)
        t1, t2 = qk[:, :, 0:8], qk[:, :, 8:16]
        cs = c_("cos", t * 8, t * 8 + 8).unsqueeze(1).broadcast_to([P, groups, 8])
        sn = c_("sin", t * 8, t * 8 + 8).unsqueeze(1).broadcast_to([P, groups, 8])
        for i, (x, w) in enumerate(((t1, cs), (t2, sn), (t1, sn), (t2, cs))):
            m = dve(lambda i=i, x=x, w=w: nc.vector.tensor_tensor(rope[:, i], x, w, ALU.mult), n2, const_here)
        r1 = dve(lambda: nc.vector.tensor_tensor(t1, rope[:, 0], rope[:, 1], ALU.subtract), m)
        r2 = dve(lambda: nc.vector.tensor_tensor(t2, rope[:, 2], rope[:, 3], ALU.add), m)
        fill(2)
        for q in range(4):
            b = 4 + q
            tt = pe.many([tr(psum[:, b, j * P:(j + 1) * P], proj[:, t, (4 * q + j) * P:(4 * q + j + 1) * P])
                          for j in range(4)], r2, n2, bank_free[b])
            dst = feat[:, 4 * q:4 * q + 4, t * P:(t + 1) * P]
            src = psum[:, b, :].rearrange("p (j t) -> p j t", j=4)
            if q % 2:
                w = act(lambda dst=dst, src=src: nc.scalar.activation(dst, src, ACT.Copy), tt)
            else:
                w = dve(lambda dst=dst, src=src: nc.vector.tensor_copy(dst, src), tt)
            bank_free[b] = [w]
            qk_written.append(w)
    qk_written = last_of(qk_written)

    o_tok = view(big, 0, ST, 4 * D)[:, :, 0:D]
    v_tok = proj[:, :, 2 * D:3 * D]
    v_here = got[4] + got[5]
    probs = [view(scr, 6 * P + i * 768, 2, 384) for i in range(2)]
    mixed = [view(scr, 6 * P + 1536 + i * 384, 384) for i in range(2)]
    mixed_t = [view(scr, 6 * P + 2304 + i * 384, 384) for i in range(2)]
    peak, denom, inv = [[tiny(2, 2) for _ in range(2)] for _ in range(3)]
    scale = DA_DIM ** -0.5
    bt, bo = psum[:, 2, :], psum[:, 3, :]
    sets = [psum[:, 4:6, :], psum[:, 6:8, :]]
    tile_cols = [slice(0, P), slice(P, 3 * P)]
    st = {}
    for b in range(2, 8):
        pe.wait(bank_free[b])

    def a_scores(h):
        for c in range(2):
            r = slice(64 * c, 64 * c + 64)
            sc = sets[h % 2]
            st["score", h] = pe.many([mm(sc[:, c, 0:P], qt[r, h, 0:P], kt[r, h, 0:P]),
                                      mm(sc[:, c, P:3 * P], qt[r, h, P:S], kt[r, h, 0:S])],
                                     qk_written, st.get(("prob", h - 2)))

    def a_softmax(h):
        z, sc = h % 2, sets[h % 2]
        diag = sc.rearrange("p c (j n) -> p c j n", n=P)[:, :, 0:3:2, :]
        m = dve(lambda: nc.vector.tensor_tensor(
            diag, diag, c_("causal_neg").unsqueeze(1).unsqueeze(1).broadcast_to([P, 2, 2, P]), ALU.add),
            st["score", h])
        for t in range(ST):
            m_ = dve(lambda t=t: nc.vector.tensor_reduce(peak[z][:, t, :], sc[:, :, tile_cols[t]], AX.X, ALU.max), m)
        m = dve(lambda: nc.vector.tensor_scalar(peak[z], peak[z], -scale, None, ALU.mult), m_)
        for t in range(ST):
            for c in range(2):
                st["prob", h] = act(lambda t=t, c=c: nc.scalar.activation(
                    probs[z][:, c, tile_cols[t]], sc[:, c, tile_cols[t]], ACT.Exp, bias=peak[z][:, t, c:c + 1],
                    scale=scale, accum_out=denom[z][:, t, c:c + 1]), m, st.get(("mix", h - 2)))

    def a_mix(h):
        z = h % 2
        i_ = dve(lambda: nc.vector.reciprocal(inv[z], denom[z]), st["prob", h])
        i_ = dve(lambda: nc.vector.tensor_scalar(inv[z][:, :, 1], inv[z][:, :, 1], neg_lam, None, ALU.mult),
                 i_, lam_here)
        x1 = [dve(lambda t=t: nc.vector.tensor_scalar(
            mixed[z][:, tile_cols[t]], probs[z][:, 0, tile_cols[t]], inv[z][:, t, 0:1], None, ALU.mult),
            i_, st.get(("turned", h - 2))) for t in range(ST)]
        for t in range(ST):
            st["mix", h] = dve(lambda t=t: nc.vector.scalar_tensor_tensor(
                mixed[z][:, tile_cols[t]], probs[z][:, 1, tile_cols[t]], inv[z][:, t, 1:2], mixed[z][:, tile_cols[t]],
                ALU.mult, ALU.add), x1[t])
        st["turned", h] = pe.many([tr(bt[:, j * P:(j + 1) * P], mixed[z][:, j * P:(j + 1) * P]) for j in range(3)],
                                  st["mix", h], st.get(("turn_out", h - 1)))
        st["turn_out", h] = act(lambda: nc.scalar.activation(mixed_t[z], bt[:, 0:3 * P], ACT.Copy), st["turned", h],
                                st.get(("value", h - 2)))

    def a_values(h):
        z, vh = h % 2, slice(h * P, (h + 1) * P)
        st["value", h] = pe.many([mm(bo[:, 0:P], mixed_t[z][:, 0:P], v_tok[:, 0, vh]),
                                  mm(bo[:, P:S], mixed_t[z][:, P:2 * P], v_tok[:, 0, vh], True, False),
                                  mm(bo[:, P:S], mixed_t[z][:, 2 * P:3 * P], v_tok[:, 1, vh], False, True)],
                                 st["turn_out", h], v_here, st.get(("out", h - 1)))
        st["out", h] = dve(lambda: nc.vector.tensor_copy(o_tok[:, :, vh], bo[:, 0:S].rearrange(
            "p (t n) -> p t n", t=ST)), st["value", h])

    pipelined(DA_HEADS, [a_scores, a_softmax, a_mix, a_values], lambda step: fill(1))
    fill(99)
    o_here = st["out", DA_HEADS - 1]
    for b in range(2, 8):
        bank_free[b] = [o_here]

    def silu_of(dst, src, *ready):
        return act(lambda: nc.scalar.activation(dst, src, ACT.Silu), *ready)

    def head_norm(dst, o, gates, heads, ready, gates_here, sq):
        sums, rstd = tiny(ST, heads), tiny(ST, heads)
        act.silent(lambda: nc.scalar.preload_act_table_set("sqrt_and_others"))
        s = [act(lambda t=t: nc.scalar.activation(sq[:, t], o[:, t], ACT.Square), ready) for t in range(ST)]
        m = [dve(lambda t=t: nc.vector.tensor_tensor(dst[:, t], o[:, t], gates[:, t], ALU.mult), ready, gates_here)
             for t in range(ST)]
        s = [dve(lambda t=t: nc.vector.tensor_reduce(sums[:, t, :], sq[:, t], AX.X, ALU.add), s[t])
             for t in range(ST)]
        r = rstd_of(sums, P, s, rstd)
        return [dve(lambda t=t: nc.vector.tensor_tensor(
            dst[:, t], dst[:, t], rstd[:, t, :].unsqueeze(2).broadcast_to([P, heads, P]), ALU.mult), r, m[t])
            for t in range(ST)]

    gate = proj[:, :, 3 * D:4 * D]
    g_here = silu_of(gate, gate, got[6] + got[7])
    sq = view(scr, 6 * P + 4 * D, ST, 8, P)
    y = normed

    def by_head(v):
        return v.rearrange("p t (h n) -> p t h n", n=P)

    y_here = head_norm(by_head(y[:, :, :]), by_head(o_tok), by_head(gate), 8, o_here, g_here, sq)
    y_here = to_features(y, y_here, [(y_t, lambda k: sub_gain)], lam_here)

    def add_projection(src_t, ready):
        done = []
        for c in range(2):
            def finish(banks, toks, c=c):
                for t in range(ST):
                    dst = x_res[:, t, c * NC:(c + 1) * NC]
                    done.append(dve(lambda dst=dst, t=t: nc.vector.tensor_tensor(dst, psum[:, banks[t], :], dst,
                                                                                 ALU.add), toks[t]))
                return [done[-2]], [done[-1]]
            chunk("tokens", src_t, ready, finish, c)
        return done[-2:]

    x_here = add_projection(y_t, y_here)

    u_here = norm_features(x_here, [(u_t, "kv_norm"), (u2_t, "b_norm")], cols_here)

    def empty_features(dst, scale=1.0):
        def finish(banks, toks):
            src = [psum[:, b, :].rearrange("p (f t) -> p f t", f=2) for b in banks]
            e0 = act(lambda: nc.scalar.activation(dst[:, 0:2, :], src[0], ACT.Copy, scale=scale), toks[0])
            e1 = dve(lambda: nc.vector.tensor_scalar(dst[:, 2:4, :], src[1], scale, None, ALU.mult), toks[1])
            done.extend([e0, e1])
            return [e0], [e1]
        done = []
        return finish, done

    act.silent(lambda: nc.scalar.preload_act_table_set("natural_log_exp_and_others"))
    v_tok, gate = view(big, 0, ST, D), view(big, ST * D, ST, D)
    o_tok = view(big, 2 * ST * D, ST, D)
    qk_here, v_here, g_here = [], [], []
    for c in range(4):
        to = (kt if c < 2 else qt)[:, 4 * (c % 2):4 * (c % 2) + 4, :]
        finish, done = empty_features(to, 1.0 if c < 2 else SB_DIM ** -0.5)
        chunk("features", u_t if c < 2 else u2_t, u_here, finish, c % 2)
        qk_here += done
    for c in range(4):
        to = (v_tok if c < 2 else gate)[:, :, (c % 2) * NC:(c % 2 + 1) * NC]
        finish, done = empty_tokens(to)
        waiting.append(chunk_steps("tokens", u_t if c < 2 else u2_t, u_here, finish, 0))
        (v_here if c < 2 else g_here).append(done)

    soft = [view(scr, i * 768, 2, 384) for i in range(2)]
    work = [view(scr, 1536 + i * 768, 2, 384) for i in range(2)]
    stick = [view(scr, 3072 + i * 768, 2, 384) for i in range(2)]
    sb_z = [psum[:, 4 + 2 * i:6 + 2 * i, 0:384] for i in range(2)]
    st = {}
    for b in range(2, 8):
        pe.wait(bank_free[b])

    def pair_bcast(name):
        return c_(name).unsqueeze(1).broadcast_to([P, 2, 384])

    def b_scores(hp):
        for c in range(2):
            r = slice(64 * c, 64 * c + 64)
            zz = sb_z[hp % 2]
            st["score", hp] = pe.many([mm(zz[:, c, 0:S], kt[r, hp, 0:P], qt[r, hp, :], True, False),
                                       mm(zz[:, c, S:384], kt[r, hp, P:S], qt[r, hp, P:S], False, True)],
                                      qk_here, st.get(("log", hp - 2)))

    def b_softplus(hp):
        i, zz = hp % 2, sb_z[hp % 2]
        e = act(lambda: nc.scalar.activation(work[i], zz, ACT.Abs), st["score", hp], st.get(("soft", hp - 2)))
        e = act(lambda: nc.scalar.activation(work[i], work[i], ACT.Exp, scale=-1.0), e)
        e = act(lambda: nc.scalar.activation(work[i], work[i], ACT.Ln, bias=1.0), e)
        d = dve(lambda: nc.vector.scalar_tensor_tensor(soft[i], zz, 0.0, work[i], ALU.max, ALU.add), e,
                st.get(("sum", hp - 2)))
        st["soft", hp] = dve(lambda: nc.vector.tensor_tensor(soft[i], soft[i], pair_bcast("sb_mask"), ALU.mult), d)

    def b_sticks(hp):
        i, zz = hp % 2, sb_z[hp % 2]
        for c in range(2):
            st["sum", hp] = pe.many([mm(zz[:, c, :], c_("sb_neg"), soft[i][:, c, :], False, False, True),
                                     mm(zz[:, c, P:S], c_("neg_ones"), soft[i][:, c, S:384], False, True, True)],
                                    st["soft", hp])
        st["log", hp] = dve(lambda: nc.vector.scalar_tensor_tensor(
            stick[i], zz, 0.0, pair_bcast("sb_bias"), ALU.min, ALU.add), st["sum", hp], st.get(("value", hp - 2)))
        st["stick", hp] = act(lambda: nc.scalar.activation(stick[i], stick[i], ACT.Exp), st["log", hp])

    def b_values(hp):
        i, bank = hp % 2, 2 + hp % 2
        for c in range(2):
            vh = slice((2 * hp + c) * 64, (2 * hp + c) * 64 + 64)
            o0, o1 = (psum[:, bank, t * P + c * 64:t * P + c * 64 + 64] for t in range(ST))
            st["value", hp] = pe.many([mm(o0, stick[i][:, c, 0:P], v_tok[:, 0, vh]),
                                       mm(o1, stick[i][:, c, P:S], v_tok[:, 0, vh], True, False),
                                       mm(o1, stick[i][:, c, S:384], v_tok[:, 1, vh], False, True)],
                                      st["stick", hp], v_here[0], v_here[1], st.get(("out", hp - 2)))
        st["out", hp] = dve(lambda: nc.vector.tensor_copy(o_tok[:, :, hp * P:(hp + 1) * P], psum[:, bank, 0:S].rearrange(
            "p (t n) -> p t n", t=ST)), st["value", hp])

    pipelined(SB_HEADS // 2, [b_scores, b_softplus, b_sticks, b_values],
              lambda step: fill(4 if step < 2 else 1))
    fill(99)
    g_here = silu_of(gate, gate, g_here)
    y_here = [dve(lambda t=t: nc.vector.tensor_tensor(normed[:, t, :], o_tok[:, t, :], gate[:, t, :], ALU.mult),
                  st["out", SB_HEADS // 2 - 1], g_here) for t in range(ST)]
    for b in range(2, 8):
        bank_free[b] = [st["out", SB_HEADS // 2 - 1]]
    y_here = to_features(normed, y_here, [(y_t, None)])
    x_here = add_projection(y_t, y_here)

    mix = view(scr, 0, ST, D)

    gain_in = g.counter("gain_in")

    def fetch_gain(layer, which, ready):
        return pool(lambda: nc.gpsimd.dma_start(post_gain, across(a["norm_gains_2"][layer, which, :])), ready,
                    inc=gain_in, by=16)

    def mix_out(src_t, ready, layer):
        gain = fetch_gain(layer, 1, ready)
        got = []
        for c in range(2):
            finish, done = empty_tokens(mix[:, :, c * NC:(c + 1) * NC])
            chunk("tokens", src_t, ready, finish, c)
            got += done
        return add_normed(mix, last_of(got), gain, view(scr, 4096, ST, D))

    def add_normed(src, ready, gain, times_gain):
        act.silent(lambda: nc.scalar.preload_act_table_set("sqrt_and_others"))
        sums, rstd = tiny(ST), tiny(ST)
        s, m = [None] * ST, [None] * ST
        for i in range(ST):
            t0, t1 = i, ST - 1 - i
            s[t0] = act(lambda: nc.scalar.activation(normed[:, t0, :], src[:, t0, :], ACT.Square,
                                                     accum_out=sums[:, t0:t0 + 1]), ready, m[t0])
            m[t1] = dve(lambda: nc.vector.tensor_tensor(times_gain[:, t1, :], src[:, t1, :], post_gain, ALU.mult),
                        ready, gain, s[t1])
        r = rstd_of(sums, D, s, rstd)
        return [dve(lambda t=t: nc.vector.scalar_tensor_tensor(
            x_res[:, t, :], times_gain[:, t, :], rstd[:, t:t + 1], x_res[:, t, :], ALU.mult, ALU.add), m, r)
            for t in range(ST)]

    conv_done = [g.counter(f"conv{i}") for i in range(2)]
    hid_hi = [g.counter(f"hid_hi{i}") for i in range(2)]
    hid_lo = [g.counter(f"hid_lo{i}") for i in range(2)]
    down_used = [g.counter(f"down_used{i}") for i in range(2)]

    def ffn(l, x_here):
        u_here = norm_features(x_here, [(u_t, f"n{l}2")], cols_here)
        gain = fetch_gain(l, 3, x_here)
        conv = [view(scr, i * 512, 2, S) for i in range(2)]
        silu = [view(scr, 1024 + i * S, S) for i in range(2)]
        prod = [view(scr, 1536 + i * S, S) for i in range(2)]
        for b in range(8):
            pe.wait(bank_free[b])

        def up(j, s, following):
            for part in range(2):
                w, here = take(following[part])
                hi, lo = (view(v[w], 0, 2, KT // 2, P) for v in (w_hi, w_lo))
                ops = []
                for i in range(2):
                    for kk in range(KT // 2):
                        k = part * KT // 2 + kk
                        ops += mm3(psum[:, s, i * S:(i + 1) * S], (hi[:, i, kk, :], lo[:, i, kk, :]),
                                   [u[:, k, :] for u in u_t], (i, k) == (0, 0), k == KT - 1)
                p = pe.many(ops, here, u_here[2 * part:2 * part + 2], conv_done[s].now(), inc=used[w])
            for i in range(2):
                e = act(lambda i=i: nc.scalar.activation(
                    conv[s][:, i, :], psum[:, s, i * S:(i + 1) * S], ACT.Identity,
                    scale=col(f"tap2_{l}", j + i * FT), bias=col(f"bias_{l}", j + i * FT)),
                    p, hid_lo[s].now())
            d = [e, e]
            for tap in (1, 0):
                back = 2 - tap
                for i in range(2):
                    d[i] = dve(lambda i=i, back=back, tap=tap: nc.vector.scalar_tensor_tensor(
                        conv[s][:, i, back:], psum[:, s, i * S:(i + 1) * S - back], col(f"tap{tap}_{l}", j + i * FT),
                        conv[s][:, i, back:], ALU.mult, ALU.add), d[i],
                        inc=conv_done[s] if (tap, i) == (0, 1) else None)
            return d

        def gated(s, d):
            e = act(lambda: nc.scalar.activation(silu[s], conv[s][:, 0, :], ACT.Silu), d[0], hid_lo[s].now())
            m = dve(lambda: nc.vector.tensor_tensor(prod[s], silu[s], conv[s][:, 1, :], ALU.mult), e, d[1],
                    hid_hi[s].now())
            e = act(lambda: nc.scalar.activation(hid[s][0][:, :], prod[s], ACT.Copy), m, down_used[s].now(),
                    inc=hid_hi[s])
            dve(lambda: nc.vector.tensor_tensor(hid[s][1][:, :], prod[s], hid[s][0][:, :].bitcast(F32),
                                                ALU.subtract), e, down_used[s].now(), inc=hid_lo[s])

        def down(s, following=None, first=False, last=False):
            w, here = take(following)
            ops = [m for t in range(ST) for n in range(2)
                   for m in mm3(psum[:, 4 + 2 * t + n, :], [h[:, t * P:(t + 1) * P] for h in hid[s]],
                                [v[w][:, n * NC:(n + 1) * NC] for v in (w_hi, w_lo)], first, last)]
            pe.many(ops[:-1], here, hid_hi[s].now(), hid_lo[s].now(), inc=down_used[s])
            return pe.many(ops[-1:], inc=used[w])

        none = (None, None)
        gated(0, up(0, 0, none))
        d = up(1, 1, none)
        down(0, first=True)
        gated(1, d)

        def steps(i, st):
            for s in range(2):
                j = i * 2 + (2 + s)
                d = up(j, s, (ffn_pieces(l, j - 1)[2], ffn_pieces(l, j + 1)[0]))
                down(1 - s, ffn_pieces(l, j + 1)[1])
                gated(s, d)
            return {}

        g.loop(FT // 2 - 2, steps, {})
        for s in range(2):
            d = up(FT - 2 + s, s, none)
            down(1 - s)
            gated(s, d)
        done = down(1, last=True)
        for s in range(2):
            bank_free[s] = [conv_done[s].now()]
        out_ps = psum[:, 4:8, :].rearrange("p (t b) n -> p t (b n)", t=ST)
        x_here = add_normed(out_ps, done, gain, view(scr, 0, ST, D))
        for b in range(4, 8):
            bank_free[b] = x_here
        return x_here

    u_here = norm_features(x_here, [(u_t, "n00")], cols_here)
    cv = feat
    v1 = view(big, 0, ST, M_HEADS, P + 1)
    o_gate = view(big, 1032, ST, NC)
    g_gate = view(big, 2056, ST, NC)
    ym = view(big, 3080, ST, D)
    g_tok = view(big, 5128, ST, 16)
    row = view(big, 5160, 11, S)
    t_ones = pool(lambda: nc.gpsimd.memset(v1[:, :, :, P:P + 1], 1.0), x_here)

    for t in range(ST):
        p = gates_taken = pe.many([mm(psum[:, 4, t * 16:(t + 1) * 16], u[:, k, t * P:(t + 1) * P].bitcast(F32),
                                      gate_w[:, k, :], (k, m) == (0, 0), (k, m) == (KT - 1, 1))
                                   for k in range(KT) for m, u in enumerate(u_t)], u_here, gw, bank_free[4])
    e = dve(lambda: nc.vector.tensor_copy(g_tok, psum[:, 4, 0:32].rearrange("p (t n) -> p t n", t=ST)), p)
    p = pe.many([tr(psum[0:4, 5 + kd // 2, (kd % 2) * S + t * P:(kd % 2) * S + (t + 1) * P],
                    g_tok[:, t, kd * 4:kd * 4 + 4]) for kd in range(4) for t in range(ST)],
                e, bank_free[5], bank_free[6])
    bank_free[4] = [e]
    gi, gf, ga, gb = (psum[0:4, 5 + kd // 2, (kd % 2) * S:(kd % 2 + 1) * S] for kd in range(4))
    R_A, R_ENM, R_G, R_B, R_C, R_T, R_U, R_V, R_I, R_X, R_Y = range(11)
    R_W = R_T

    def rw(k):
        return row[0:4, k, :]

    def gc(kind, t, h):
        return gcol[:, kind, t, h:h + 1]

    def gate_rows(p):
        b15 = tiny(4)
        t0 = dve(lambda: nc.vector.tensor_scalar(b15[0:4, 0:2], gate_col[0:4, 0:2], 1.0 / 15.0, None, ALU.mult),
                 gains_here)
        e1 = act(lambda: nc.scalar.activation(rw(R_I), gi, ACT.Tanh, scale=1.0 / 15.0, bias=b15[0:4, 0:1]), p, t0)
        yield
        e2 = act(lambda: nc.scalar.activation(rw(R_T), gf, ACT.Tanh, scale=1.0 / 15.0, bias=b15[0:4, 1:2]), p, t0)
        e = act(lambda: nc.scalar.activation(rw(R_T), rw(R_T), ACT.Exp, scale=-15.0), e2)
        e = act(lambda: nc.scalar.activation(rw(R_T), rw(R_T), ACT.Ln, bias=1.0), e)
        yield
        d = dve(lambda: nc.vector.tensor_tensor_scan(rw(R_U), c_("ones")[0:4, 0:1].broadcast_to([4, S]), rw(R_T), 0.0,
                                                     ALU.mult, ALU.add), e)
        d = dve(lambda: nc.vector.scalar_tensor_tensor(rw(R_A), rw(R_I), 15.0, rw(R_U), ALU.mult, ALU.add), d, e1)
        d = dve(lambda: nc.vector.tensor_tensor_scan(rw(R_C), c_("ones")[0:4, 0:1].broadcast_to([4, S]), rw(R_A), 0.0,
                                                     ALU.mult, ALU.max), d)
        yield
        d = dve(lambda: nc.vector.tensor_tensor(rw(R_ENM), rw(R_U), rw(R_C), ALU.subtract), d)
        m_rows = act(lambda: nc.scalar.activation(rw(R_ENM), rw(R_ENM), ACT.Exp), d)
        ea = tiny(1)
        yield
        e0 = act(lambda: nc.scalar.activation(ea[0:4, :], gate_col[0:4, 3:4], ACT.Exp), gains_here)
        d = ga_read = dve(lambda: nc.vector.tensor_scalar(rw(R_V), ga, gate_col[0:4, 2:3], None, ALU.add), p,
                          gains_here)
        e = act(lambda: nc.scalar.activation(rw(R_W), rw(R_V), ACT.Abs), d)
        yield
        e = act(lambda: nc.scalar.activation(rw(R_W), rw(R_W), ACT.Exp, scale=-1.0), e)
        d = dve(lambda: nc.vector.tensor_scalar(rw(R_X), rw(R_W), 2.0, None, ALU.add), e)
        d = dve(lambda: nc.vector.reciprocal(rw(R_X), rw(R_X)), d)
        yield
        d = dve(lambda: nc.vector.tensor_tensor(rw(R_W), rw(R_W), rw(R_X), ALU.mult), d)
        sq_here = d = dve(lambda: nc.vector.tensor_tensor(rw(R_X), rw(R_W), rw(R_W), ALU.mult), d)
        d = dve(lambda: nc.vector.tensor_scalar(rw(R_Y), rw(R_X), 1.0 / 17, None, ALU.mult), d)
        yield
        for k in (15, 13, 11, 9, 7, 5, 3):
            d = dve(lambda k=k: nc.vector.scalar_tensor_tensor(rw(R_Y), rw(R_Y), 1.0 / k, rw(R_X), ALU.add, ALU.mult), d)
        d = dve(lambda: nc.vector.scalar_tensor_tensor(rw(R_Y), rw(R_Y), 1.0, rw(R_W), ALU.add, ALU.mult), d)
        d = dve(lambda: nc.vector.tensor_scalar(rw(R_Y), rw(R_Y), 2.0, None, ALU.mult), d)
        yield
        d = dve(lambda: nc.vector.scalar_tensor_tensor(rw(R_V), rw(R_V), 0.0, rw(R_Y), ALU.max, ALU.add), d)
        g_row = dve(lambda: nc.vector.tensor_scalar(rw(R_G), rw(R_V), ea[0:4, :], -1.0, ALU.mult, ALU.mult), d, e0)
        e = act(lambda: nc.scalar.activation(rw(R_B), gb, ACT.Exp, scale=-1.0), p, ga_read)
        yield
        d = dve(lambda: nc.vector.tensor_scalar(rw(R_B), rw(R_B), 1.0, None, ALU.add), e)
        g_rows = dve(lambda: nc.vector.reciprocal(rw(R_B), rw(R_B)), d)
        bank_free[5] = bank_free[6] = [g_rows, e]
        yield
        p = pe.many([tr(psum[:, 4, (kd * ST + t) * 4:(kd * ST + t) * 4 + 4], row[0:4, kd, t * P:(t + 1) * P], 4)
                     for kd in range(4) for t in range(ST)], m_rows, g_rows, g_row, e, bank_free[4])
        gcol_here = dve(lambda: nc.vector.tensor_copy(gcol, psum[:, 4, 0:32].rearrange(
            "p (k t h) -> p k t h", k=4, t=ST)), p)
        bank_free[4] = [gcol_here]
        found.update(m_rows=m_rows, g_rows=g_rows, gcol_here=gcol_here)
        yield

    found = {}
    gcol = tiny(4, ST, 4)
    gate_steps = gate_rows(p)

    def conv_chunk(tiles, taps, stride, base, pair):
        def finish(banks, toks):
            out_t, last_tap = [], []
            srcs = [psum[:, banks[f // 2], (f % 2) * S:(f % 2 + 1) * S] for f in range(4)]
            for f, src in enumerate(srcs):
                dst = cv[:, tiles + f, :]
                last_tap.append(act(lambda dst=dst, src=src, f=f: nc.scalar.activation(
                    dst, src, ACT.Copy, scale=col(taps, 3 * stride + base + f)), toks[f // 2], gates_taken))
            out_t = [last_tap[f // 2 * 2 + 1] for f in range(4)]
            for tap in (2, 1, 0):
                back = 3 - tap
                for f, src in enumerate(srcs):
                    dst = cv[:, tiles + f, :]
                    out_t[f] = dve(lambda dst=dst, src=src, f=f, back=back, tap=tap: nc.vector.scalar_tensor_tensor(
                        dst[:, back:], src[:, 0:S - back], col(taps, tap * stride + base + f), dst[:, back:],
                        ALU.mult, ALU.add), out_t[f])
            done.append(silu_of(cv[:, tiles:tiles + 4, :], cv[:, tiles:tiles + 4, :], out_t[3]))
            return [out_t[1]], [out_t[3]]
        done = []
        return chunk_steps("features", u_t, u_here, finish, pair), done

    cv_here = []
    for n in range(3):
        steps, done = conv_chunk(4 + 4 * n, "conv_g", 12, 4 * n, n % 2)
        for _ in steps:
            next(gate_steps, None)
        cv_here += done
    for _ in gate_steps:
        pass
    m_rows, g_rows, gcol_here = found["m_rows"], found["g_rows"], found["gcol_here"]
    steps, mqk_here = conv_chunk(0, "conv_m", 4, 0, 0)
    waiting.append(steps)

    def v1_finish(banks, toks):
        e = [act(lambda: nc.scalar.activation(v1[:, 0, :, 0:P], psum[:, banks[0], :].rearrange(
            "p (h n) -> p h n", n=P), ACT.Copy), toks[0]),
            dve(lambda: nc.vector.tensor_copy(v1[:, 1, :, 0:P], psum[:, banks[1], :].rearrange(
                "p (h n) -> p h n", n=P)), toks[1])]
        vs.extend(e)
        return [e[0]], [e[1]]

    vs = []
    waiting.append(chunk_steps("tokens", u_t, u_here, v1_finish, 0))
    finish, og = empty_tokens(o_gate)
    waiting.append(chunk_steps("tokens", u_t, u_here, finish, 0))
    finish, gg = empty_tokens(g_gate)
    waiting.append(chunk_steps("tokens", u_t, u_here, finish, 0))

    def row_bcast(kind, h, dst):
        return mm(dst, c_("select", h * P, (h + 1) * P)[0:4, :], rw(kind))

    gq, gk, gv = cv[:, 4:8, :], cv[:, 8:12, :], cv[:, 12:16, :]
    qk8 = cv[:, 4:12, :]
    sq8 = view(scr, 3072, 8, S)
    e = act(lambda: nc.scalar.activation(sq8, qk8, ACT.Square), cv_here)
    for b in range(2, 8):
        pe.wait(bank_free[b])
    for i in range(4):
        p = pe(mm(psum[:, 2 + i, :], c_("ones"), sq8[:, 2 * i:2 * i + 2, :].rearrange("p a s -> p (a s)")), e)
    ss = psum[:, 2:6, :].rearrange("p b (j s) -> p (b j) s", j=2)
    d = dve(lambda: nc.vector.tensor_scalar(sq8, ss, EPS, None, ALU.add), p)
    e = act(lambda: nc.scalar.activation(sq8, sq8, ACT.Sqrt), d)
    d = dve(lambda: nc.vector.reciprocal(sq8, sq8), e)
    d = dve(lambda: nc.vector.tensor_tensor(gk, gk, sq8[:, 4:8, :], ALU.mult), d)
    fill(1)
    qk_n = dve(lambda: nc.vector.scalar_tensor_tensor(gq, gq, P ** -0.5, sq8[:, 0:4, :], ALU.mult, ALU.mult), d)

    dg = view(scr, 0, 8, P)
    at_ = view(scr, 1024, 8, P)
    attn = view(scr, 2048, 8, P)
    cm = [view(scr, 3072 + i * 1024, 8, P) for i in range(2)]
    xx = view(scr, 5120, 8, P)
    xt = view(scr, 6144, 8, P)
    yy = view(scr, 7168, 8, P)
    v_t = view(scr, 8192, 8, P)
    kd = view(scr, 9216, 4, P)
    v_new = view(scr, 9728, ST, 4, P)
    state = view(scr, 10752, 4, P)
    rhs = view(scr, 11264, ST, 4, P)
    o_raw = view(scr, 12288, ST, 4, P)

    def blk(j):
        return slice((j % 2) * P, (j % 2 + 1) * P)

    gu = view(scr, 1024, 4, ST, P)
    g_u = dve(lambda: nc.vector.tensor_tensor(
        gu, c_("upper").unsqueeze(1).unsqueeze(1).broadcast_to([P, 4, ST, P]),
        gcol[:, R_G, :, :].rearrange("p t h -> p h t").unsqueeze(3).broadcast_to([P, 4, ST, P]), ALU.mult),
        gcol_here)
    gu_f = view(scr, 1024, 2, NC)
    p = pe.many([mm(psum[:, 6 + i, :], c_("after"), gu_f[:, i, :]) for i in range(2)], g_u)
    e = act(lambda: nc.scalar.activation(dg, psum[:, 6:8, :].rearrange("p b (j n) -> p (b j) n", n=P), ACT.Exp), p)
    fill(1)
    dg_here = dve(lambda: nc.vector.tensor_tensor(
        dg, dg, c_("upper").unsqueeze(1).broadcast_to([P, 8, P]), ALU.mult), e)
    eg = tiny(4)
    p = pe(mm(psum[:, 6, 0:4], c_("upper"), gcol[:, R_G, 1, :]), e)
    eg_here = act(lambda: nc.scalar.activation(eg, psum[:, 6, 0:4], ACT.Exp), p)
    p2 = pe.many([row_bcast(R_B, h, psum[:, 6 + h // 2, (h % 2) * S:(h % 2 + 1) * S]) for h in range(4)],
                 g_rows, eg_here)
    db = dve(lambda: nc.vector.tensor_tensor(
        at_, dg, psum[:, 6:8, :].rearrange("p b (j n) -> p (b j) n", n=P), ALU.mult), dg_here, p2)
    p = pe.many([mm(psum[:, 2 + j // 4, (j % 4) * P:(j % 4 + 1) * P], gk[:, j // 2, blk(j)], gk[:, j // 2, blk(j)])
                 for j in range(8)], qk_n)
    a_here = dve(lambda: nc.vector.tensor_tensor(
        at_, at_, psum[:, 2:4, :].rearrange("p b (j n) -> p (b j) n", n=P), ALU.mult), p, db)
    p = pe.many([mm(psum[:, 4 + j // 4, (j % 4) * P:(j % 4 + 1) * P], gk[:, j // 2, blk(j)], gq[:, j // 2, blk(j)])
                 for j in range(8)], qk_n)
    attn_here = dve(lambda: nc.vector.tensor_tensor(
        attn, dg, psum[:, 4:6, :].rearrange("p b (j n) -> p (b j) n", n=P), ALU.mult), p, dg_here)
    fill(1)
    p = pe.many([tr(psum[:, 2 + j // 4, (j % 4) * P:(j % 4 + 1) * P], gv[:, j // 2, blk(j)]) for j in range(8)],
                a_here, cv_here)
    vt_here = act(lambda: nc.scalar.activation(v_t, psum[:, 2:4, :].rearrange("p b (j n) -> p (b j) n", n=P),
                                               ACT.Copy), p, a_here)
    p = pe.many([tr(psum[:, 4, h * P:(h + 1) * P], gk[:, h, 0:P]) for h in range(4)], attn_here)
    for h in range(4):
        kd_here = dve(lambda h=h: nc.vector.tensor_scalar(kd[:, h, :], psum[:, 4, h * P:(h + 1) * P],
                                                          dg[:, 2 * h, P - 1:P], None, ALU.mult), p)

    def level_mask(i):
        at, _ = CONST["levels"]
        return const[:, at + i * P:at + (i + 1) * P].unsqueeze(1).broadcast_to([P, 8, P])

    def quad(buf, q):
        return buf[:, 4 * q:4 * q + 4, :]

    def b4(b):
        return psum[:, b, :].rearrange("p (j n) -> p j n", n=P)

    cm_free = [[], []]
    id4 = ident.unsqueeze(1).broadcast_to([P, 4, P])
    m = pool(lambda: nc.gpsimd.tensor_tensor(cm[0], at_, level_mask(0), ALU.mult), a_here, qk_n)
    x_, xt_ = [None, None], [None, None]
    for q in range(2):
        p = pe.many([tr(psum[:, 6 + q, j * P:(j + 1) * P], cm[0][:, 4 * q + j, :]) for j in range(4)], m, db)
        x_[q] = dve(lambda q=q: nc.vector.scalar_tensor_tensor(quad(xx, q), b4(6 + q), -1.0, id4, ALU.mult, ALU.add), p)
        xt_[q] = dve(lambda q=q: nc.vector.scalar_tensor_tensor(quad(xt, q), quad(cm[0], q), -1.0, id4, ALU.mult,
                                                                ALU.add), m)
    cm_free[0] = [p, xt_[1]]
    fill(1)
    for i in range(1, len(LEVELS)):
        c = cm[i % 2]
        m = pool(lambda c=c, i=i: nc.gpsimd.tensor_tensor(c, at_, level_mask(i), ALU.mult), a_here, cm_free[i % 2])
        y_ = [None, None]
        for q in range(2):
            p = pe.many([mm(psum[:, 6 + q, j * P:(j + 1) * P], c[:, 4 * q + j, :], xx[:, 4 * q + j, :])
                         for j in range(4)], m, x_[q])
            y_[q] = act(lambda q=q: nc.scalar.activation(quad(yy, q), b4(6 + q), ACT.Copy), p, xt_[q])
        cm_free[i % 2] = [p]
        fill(1)
        for q in range(2):
            if i < len(LEVELS) - 1:
                p = pe.many([mm(psum[:, 2 + q, j * P:(j + 1) * P], xt[:, 4 * q + j, :], yy[:, 4 * q + j, :])
                             for j in range(4)], y_[q], xt_[q], vt_here)
                x_[q] = dve(lambda q=q: nc.vector.tensor_tensor(quad(xx, q), quad(xx, q), b4(2 + q), ALU.subtract), p)
            p = pe.many([mm(psum[:, 4 + q, j * P:(j + 1) * P], yy[:, 4 * q + j, :], xt[:, 4 * q + j, :])
                         for j in range(4)], y_[q], xt_[q], kd_here)
            xt_[q] = dve(lambda q=q: nc.vector.tensor_tensor(quad(xt, q), quad(xt, q), b4(4 + q), ALU.subtract), p)
        fill(1)

    fill(99)
    og = act(lambda: nc.scalar.activation(o_gate, o_gate, ACT.Sigmoid), og)
    gg = silu_of(g_gate, g_gate, gg)

    dm = view(scr, 3072, M_HEADS, 384)
    st_ = view(scr, 0, M_HEADS, 384)
    for b in range(8):
        pe.wait(bank_free[b])
    p = pe.many([row_bcast(R_C, h, psum[:, h // 2, (h % 2) * S:(h % 2 + 1) * S]) for h in range(4)], m_rows)
    for h in range(M_HEADS):
        cb = psum[:, h // 2, (h % 2) * S:(h % 2 + 1) * S]
        d = dve(lambda h=h, cb=cb: nc.vector.tensor_scalar(dm[:, h, 0:S], cb, gc(R_A, 0, h), 0.0,
                                                           ALU.subtract, ALU.max), p, gcol_here, xt_)
        d = dve(lambda h=h, cb=cb: nc.vector.tensor_scalar(dm[:, h, S:384], cb[:, P:S], gc(R_A, 1, h), 0.0,
                                                           ALU.subtract, ALU.max))
    e = act(lambda: nc.scalar.activation(dm, dm, ACT.Exp, scale=-1.0), d)
    dd = dm.rearrange("p h (j n) -> p h j n", n=P)[:, :, 0:3:2, :]
    msk = c_("upper").unsqueeze(1).unsqueeze(1).broadcast_to([P, 4, 2, P])
    dd_here = dve(lambda: nc.vector.tensor_tensor(dd, dd, msk, ALU.mult), e)
    outs = []
    for h in range(M_HEADS):
        r = slice(64 * (h % 2), 64 * (h % 2) + 64)
        sc = psum[:, 4 + h, 0:384]
        p = pe.many([mm(sc[:, 0:S], cv[r, 2 + h // 2, 0:P], cv[r, h // 2, :]),
                     mm(sc[:, S:384], cv[r, 2 + h // 2, P:S], cv[r, h // 2, P:S])], mqk_here)
        d = dve(lambda h=h, sc=sc: nc.vector.scalar_tensor_tensor(
            st_[:, h, :], sc, 64 ** -0.5, dm[:, h, :], ALU.mult, ALU.mult), p, dd_here)
        o = psum[:, h, 0:2 * (P + 1)]
        outs.append(pe.many([mm(o[:, 0:P + 1], st_[:, h, 0:P], v1[:, 0, h, :]),
                             mm(o[:, P + 1:], st_[:, h, P:S], v1[:, 0, h, :], True, False),
                             mm(o[:, P + 1:], st_[:, h, S:384], v1[:, 1, h, :], False, True)], d, vs, t_ones))
    o4 = psum[:, 0:4, 0:2 * (P + 1)].rearrange("p h (t n) -> p t h n", t=ST)
    den, nd = tiny(ST, 4), tiny(ST, 4)
    d = dve(lambda: nc.vector.tensor_scalar(nd, o4[:, :, :, P], -1.0, None, ALU.mult), outs[-1])
    d = dve(lambda: nc.vector.tensor_tensor(den, o4[:, :, :, P], nd, ALU.max), d)
    d = dve(lambda: nc.vector.tensor_tensor(den, den, gcol[:, R_ENM, :, :], ALU.max), d)
    d = dve(lambda: nc.vector.reciprocal(den, den), d)
    hm = view(scr, 1024, ST, 4, P)
    for t in range(ST):
        h_here = dve(lambda t=t: nc.vector.tensor_tensor(
            hm[:, t], o4[:, t, :, 0:P], den[:, t, :].unsqueeze(2).broadcast_to([P, 4, P]), ALU.mult), d)
    for b in range(8):
        bank_free[b] = [h_here]
    ym_m = head_norm(by_head(ym[:, :, 0:NC]), hm, by_head(o_gate), 4, h_here, og, view(scr, 0, ST, 4, P))

    r0 = [dve(lambda h=h: nc.vector.tensor_scalar(rhs[:, 0, h, :], v_t[:, 2 * h, :], gc(R_B, 0, h), None, ALU.mult),
              vt_here) for h in range(4)][-1]
    p = pe.many([mm(psum[:, 0, h * P:(h + 1) * P], xt[:, 2 * h, :], rhs[:, 0, h, :]) for h in range(4)], r0, xt_)
    n0 = act(lambda: nc.scalar.activation(v_new[:, 0], psum[:, 0, :].rearrange("p (h n) -> p h n", n=P), ACT.Copy), p)
    p = pe.many([mm(psum[:, 1, h * P:(h + 1) * P], kd[:, h, :], v_new[:, 0, h, :]) for h in range(4)], n0, kd_here)
    s0 = act(lambda: nc.scalar.activation(state, psum[:, 1, :].rearrange("p (h n) -> p h n", n=P), ACT.Copy), p)
    po = pe.many([mm(psum[:, 2, h * P:(h + 1) * P], attn[:, 2 * h, :], v_new[:, 0, h, :]) for h in range(4)],
                 attn_here)
    o0 = act(lambda: nc.scalar.activation(o_raw[:, 0], psum[:, 2, :].rearrange("p (h n) -> p h n", n=P), ACT.Copy), po)
    p = pe.many([mm(psum[:, 3, h * P:(h + 1) * P], gk[:, h, P:S], state[:, h, :]) for h in range(4)], s0,
                attn_here)
    for h in range(4):
        d = dve(lambda h=h: nc.vector.tensor_scalar(rhs[:, 1, h, :], psum[:, 3, h * P:(h + 1) * P], eg[:, h:h + 1],
                                                    None, ALU.mult), p)
        d = dve(lambda h=h: nc.vector.tensor_tensor(rhs[:, 1, h, :], v_t[:, 2 * h + 1, :], rhs[:, 1, h, :],
                                                    ALU.subtract), d)
        d = dve(lambda h=h: nc.vector.tensor_scalar(rhs[:, 1, h, :], rhs[:, 1, h, :], gc(R_B, 1, h), None, ALU.mult),
                d)
    p = pe.many([mm(psum[:, 6, h * P:(h + 1) * P], xt[:, 2 * h + 1, :], rhs[:, 1, h, :]) for h in range(4)], d,
                kd_here)
    n1 = act(lambda: nc.scalar.activation(v_new[:, 1], psum[:, 6, :].rearrange("p (h n) -> p h n", n=P), ACT.Copy), p)
    pq = pe.many([mm(psum[:, 7, h * P:(h + 1) * P], gq[:, h, P:S], state[:, h, :]) for h in range(4)], s0, db)
    for h in range(4):
        o1 = dve(lambda h=h: nc.vector.tensor_scalar(o_raw[:, 1, h, :], psum[:, 7, h * P:(h + 1) * P],
                                                     eg[:, h:h + 1], None, ALU.mult), pq)
    p = pe.many([mm(psum[:, 4, h * P:(h + 1) * P], attn[:, 2 * h + 1, :], v_new[:, 1, h, :]) for h in range(4)], n1)
    o1 = dve(lambda: nc.vector.tensor_tensor(o_raw[:, 1], o_raw[:, 1], psum[:, 4, :].rearrange(
        "p (h n) -> p h n", n=P), ALU.add), p, o1)
    for b in range(8):
        bank_free[b] = [o1, o0]
    ym_g = head_norm(by_head(ym[:, :, NC:2 * NC]), o_raw, by_head(g_gate), 4, [o0, o1], gg,
                     view(scr, 0, ST, 4, P))
    y_here = to_features(ym, [ym_m, ym_m, ym_g, ym_g], [(y_t, lambda k: col("m_norm", k))])
    x_here = mix_out(y_t, y_here, 0)
    x_here = ffn(0, x_here)

    u_here = norm_features(x_here, [(u_t, "n10")], cols_here)
    lbm, lbe, lbs, lb, one_lb = tiny(8), tiny(2, 8), tiny(8), tiny(8), tiny(8)
    lg = cols[:, ROW["lb"]:ROW["lb"] + 16].rearrange("p (l k) -> p l k", l=2)
    d = dve(lambda: nc.vector.tensor_tensor(lbm, lg[:, 0, :], lg[:, 1, :], ALU.max), cols_here)
    d = dve(lambda: nc.vector.tensor_tensor(lbe, lg, lbm.unsqueeze(1).broadcast_to([P, 2, 8]), ALU.subtract), d)
    e = act(lambda: nc.scalar.activation(lbe, lbe, ACT.Exp), d)
    d = dve(lambda: nc.vector.tensor_tensor(lbs, lbe[:, 0, :], lbe[:, 1, :], ALU.add), e)
    d = dve(lambda: nc.vector.reciprocal(lbs, lbs), d)
    d = dve(lambda: nc.vector.tensor_tensor(lbe, lbe, lbs.unsqueeze(1).broadcast_to([P, 2, 8]), ALU.mult), d)
    d = dve(lambda: nc.vector.tensor_tensor(lb, lbe[:, 0, :], lbe[:, 1, :], ALU.add), d)
    d = dve(lambda: nc.vector.tensor_tensor(lb, lb, lbe[:, 0, :], ALU.subtract), d)
    d = dve(lambda: nc.vector.tensor_scalar(lb, lb, 0.0, None, ALU.max), d)
    lb_here = dve(lambda: nc.vector.tensor_scalar(one_lb, lb, -1.0, 1.0, ALU.mult, ALU.add), d)

    cq = feat[:, 0:8, :]
    ck = feat[:, 8:16, :]
    fe = view(scr, 0, 8, S)
    l1 = view(scr, 2048, 8, S)
    gs = view(scr, 4096, 8, S)
    ci, cg = view(big, 0, ST, D), view(big, 2048, ST, D)
    fgot, qgot, vgot, ggot = [], [], [], []
    for c in range(2):
        finish, done = empty_features(fe[:, 4 * c:4 * c + 4, :])
        chunk("features", u_t, u_here, finish, c % 2)
        fgot += done
    for c in range(6):
        if c < 2:
            finish, done = empty_features(cq[:, 4 * c:4 * c + 4, :])
        else:
            finish, done = empty_tokens((ci if c < 4 else cg)[:, :, (c % 2) * NC:(c % 2 + 1) * NC])
        waiting.append(chunk_steps("features" if c < 2 else "tokens", u_t, u_here, finish, 0))
        (qgot, vgot, ggot)[c // 2].append(done)
    act.silent(lambda: nc.scalar.preload_act_table_set("natural_log_exp_and_others"))
    d = dve(lambda: nc.vector.tensor_scalar(fe, fe, -40.0, None, ALU.max), last_of(fgot))
    e = act(lambda: nc.scalar.activation(gs, fe, ACT.Exp, scale=-1.0), d)
    fill(1)
    e = act(lambda: nc.scalar.activation(l1, gs, ACT.Ln, bias=1.0), e)
    fill(1)
    d = dve(lambda: nc.vector.tensor_tensor(ck, fe, l1, ALU.add), e)
    for h in range(8):
        e2 = act(lambda h=h: nc.scalar.activation(fe[:, h, :], gs[:, h, :], ACT.Ln, bias=1.0, scale=lb[:, h:h + 1]),
                 d, lb_here)
        if h % 4 == 3:
            fill(1)
    e3 = act(lambda: nc.scalar.activation(ck, ck, ACT.Exp, scale=-1.0), d)
    d = dve(lambda: nc.vector.tensor_tensor(fe, fe, l1, ALU.subtract), e2)
    fill(1)
    for h in range(8):
        for t in range(ST):
            ts = slice(t * P, (t + 1) * P)
            gs_here = dve(lambda h=h, ts=ts: nc.vector.tensor_tensor_scan(
                gs[:, h, ts], c_("ones"), fe[:, h, ts], 0.0, ALU.mult, ALU.add), d)
        if h % 4 == 3:
            fill(1)
    k_here = dve(lambda: nc.vector.tensor_tensor(ck, ck, one_lb.unsqueeze(2).broadcast_to([P, 8, S]), ALU.mult),
                 e3, lb_here)
    fill(1)
    q_here = act(lambda: nc.scalar.activation(cq, cq, ACT.Silu), qgot)
    q_here = dve(lambda: nc.vector.tensor_scalar(cq, cq, P ** -0.5, None, ALU.mult), q_here)
    act.silent(lambda: nc.scalar.preload_act_table_set("natural_log_exp_and_others"))

    att = view(big, 4096, 16, P)
    att1 = view(big, 6144, 8, P)
    dec = [view(scr, i * 2048, 8 * S) for i in range(2)]
    prod = [view(scr, 6144 + i * 2048, 8 * S) for i in range(2)]
    gs_f, q_f, k_f = (v.rearrange("p h s -> p (h s)") for v in (gs, cq, ck))
    for b in range(2, 8):
        pe.wait(bank_free[b])
    z0 = pool(lambda: nc.gpsimd.memset(att, 0.0), u_here)
    quads = [2, 4, 6]
    quad_free = {q: bank_free[q] + bank_free[q + 1] for q in quads}
    st = {}
    turns = [0]

    def meet(left, right, *tokens):
        found = []
        for j0 in (0, 8):
            q = quads[turns[0] % 3]
            turns[0] += 1
            p = pe.many([mm(psum[:, q + j // 4, (j % 4) * P:(j % 4 + 1) * P], left(j0 + j), right(j0 + j))
                         for j in range(8)], quad_free[q], *tokens)
            found.append((j0, q, p))
        return found

    def keep(found, mask, *tokens):
        for j0, q, p in found:
            src = psum[:, q:q + 2, :].rearrange("p b (j n) -> p (b j) n", n=P)
            quad_free[q] = [dve(lambda: nc.vector.copy_predicated(
                att[:, j0:j0 + 8, :], mask.bitcast(I32).unsqueeze(1).broadcast_to([P, 8, P]), src), p, *tokens)]

    def lev(buf, n):
        return buf.rearrange("p (b m) -> p b m", m=2 * n)

    def c_decay(i):
        n, z = LEVELS[i], i % 2
        g4, d4 = lev(gs_f, n), lev(dec[z], n)
        d = dve(lambda: nc.vector.tensor_tensor(
            d4, g4, g4[:, :, n - 1:n].broadcast_to([P, 8 * S // (2 * n), 2 * n]), ALU.subtract),
            gs_here, e3, st.get(("prod", i - 2)))
        st["right", i] = act(lambda: nc.scalar.activation(d4[:, :, n:], d4[:, :, n:], ACT.Exp), d)
        st["left", i] = act(lambda: nc.scalar.activation(d4[:, :, 0:n], d4[:, :, 0:n], ACT.Exp, scale=-1.0), d)

    def c_meet(i):
        n, z = LEVELS[i], i % 2
        d4, p4, q4, k4 = lev(dec[z], n), lev(prod[z], n), lev(q_f, n), lev(k_f, n)
        m1 = pool(lambda: nc.gpsimd.tensor_tensor(p4[:, :, n:], d4[:, :, n:], q4[:, :, n:], ALU.mult),
                  st["right", i], q_here, st.get(("met", i - 2)))
        m2 = dve(lambda: nc.vector.tensor_tensor(p4[:, :, 0:n], d4[:, :, 0:n], k4[:, :, 0:n], ALU.mult),
                 st["left", i], k_here, st.get(("met", i - 2)))
        st["prod", i] = [m1, m2]
        pr = view(prod[z], 0, 16, P)
        st["found", i] = meet(lambda j: pr[:, j, :], lambda j: pr[:, j, :], m1, m2)
        st["met", i] = st["found", i][-1][2]

    def c_keep(i):
        at, _ = CONST["levels"]
        keep(st["found", i], const[:, at + i * P:at + (i + 1) * P])

    keep(meet(lambda j: ck[:, j // 2, blk(j)], lambda j: cq[:, j // 2, blk(j)], k_here, q_here), ident, z0)
    pipelined(len(LEVELS), [c_decay, c_meet, c_keep], lambda step: fill(2))
    fill(99)
    gg = silu_of(cg, cg, ggot)
    act.silent(lambda: nc.scalar.preload_act_table_set("natural_log_exp_and_others"))
    last = len(LEVELS) - 1
    prod_free = st["prod", last] + [st["met", last], st["met", last - 1], st["prod", last - 1]]
    att_here = [t for q in quads for t in quad_free[q]]
    dk, dq = view(dec[1], 0, 8, P), view(dec[1], 1024, 8, P)
    d = dve(lambda: nc.vector.tensor_tensor(dk, gs[:, :, P - 1:P].broadcast_to([P, 8, P]), gs[:, :, 0:P],
                                            ALU.subtract), prod_free)
    e1 = act(lambda: nc.scalar.activation(dk, dk, ACT.Exp), d)
    e2 = act(lambda: nc.scalar.activation(dq, gs[:, :, P:S], ACT.Exp), prod_free)
    d = dve(lambda: nc.vector.tensor_tensor(dk, dk, ck[:, :, 0:P], ALU.mult), e1)
    d = dve(lambda: nc.vector.tensor_tensor(dq, dq, cq[:, :, P:S], ALU.mult), e2)
    p = pe.many([mm(psum[:, h // 4, (h % 4) * P:(h % 4 + 1) * P], dk[:, h, :], dq[:, h, :]) for h in range(8)],
                d, bank_free[0], bank_free[1])
    a1_here = act(lambda: nc.scalar.activation(att1, psum[:, 0:2, :].rearrange("p b (j n) -> p (b j) n", n=P),
                                               ACT.Copy), p)
    co = view(scr, 6144, ST, 8, P)
    for t in range(ST):
        bks = [2 + 2 * t, 3 + 2 * t]
        ops = []
        for h in range(8):
            o = psum[:, bks[h // 4], (h % 4) * P:(h % 4 + 1) * P]
            vh = slice(h * P, (h + 1) * P)
            if t == 0:
                ops.append(mm(o, att[:, 2 * h, :], ci[:, 0, vh]))
            else:
                ops.append(mm(o, att1[:, h, :], ci[:, 0, vh], True, False))
                ops.append(mm(o, att[:, 2 * h + 1, :], ci[:, 1, vh], False, True))
        p = pe.many(ops, last_of(att_here), a1_here, vgot)
        src = psum[:, bks[0]:bks[0] + 2, :].rearrange("p b (j n) -> p (b j) n", n=P)
        if t == 0:
            c0_ = act(lambda src=src: nc.scalar.activation(co[:, 0], src, ACT.Copy), p)
        else:
            c1_ = dve(lambda src=src: nc.vector.tensor_copy(co[:, 1], src), p)
    for b in range(8):
        bank_free[b] = [a1_here, c0_, c1_]
    y_here = head_norm(by_head(normed[:, :, :]), co, by_head(cg), 8, [c0_, c1_], gg, view(scr, 0, ST, 8, P))
    y_here = to_features(normed, y_here, [(y_t, lambda k: col("c_norm", k))])
    x_here = mix_out(y_t, y_here, 1)
    x_here = ffn(1, x_here)

    out_done = g.counter("out_written")
    w = sp(lambda: nc.sync.dma_start(out.rearrange("b (t p) n -> p (b t) n", p=P), x_res[:, :, :]), x_here,
           inc=out_done, by=16)
    sp.wait(w)


_INS = ["x", "a_norm", "a_w_in", "a_w_out", "a_q_norm", "a_k_norm", "a_lq1", "a_lk1", "a_lq2", "a_lk2", "a_subln",
        "kv_norm", "w_kv", "b_norm", "b_w_in", "b_w_out", "norm_gains_2", "ab_w_in_2", "ab_conv_m_2",
        "ab_m_gate_bias_2", "ab_m_norm_2", "ab_conv_g_2", "ab_g_a_log_2", "ab_g_dt_bias_2", "ab_g_norm_2",
        "ab_w_out_2", "c_w_in_2", "c_lb_logits_2", "c_norm_2", "c_w_out_2", "ffn_w_up_2", "ffn_conv_w_2",
        "ffn_conv_b_2", "ffn_w_down_2"]


def kernel(**inputs):
    import concourse.bacc as bacc
    from concourse.bass_utils import run_bass_kernel_spmd

    nc = bacc.Bacc("TRN2", target_bir_lowering=False, num_devices=1)
    arrays, aps = {}, {}
    for name in _INS:
        arr = np.ascontiguousarray(inputs[name])
        arrays[f"in_{name}"] = arr
        aps[name] = nc.dram_tensor(f"in_{name}", arr.shape, mybir.dt.from_np(arr.dtype), kind="ExternalInput").ap()
    tab = constant_table()
    arrays["in_table"] = tab
    table = nc.dram_tensor("in_table", tab.shape, F32, kind="ExternalInput").ap()
    out = nc.dram_tensor("out_x", (1, S, D), F32, kind="ExternalOutput").ap()
    build(nc, aps, out, table)
    r = run_bass_kernel_spmd(nc, [arrays], core_ids=[0])
    return r.results[0]["out_x"]
```
